# Optimizing a Trainium2 kernel written in Bass

```python
import jax, jax.numpy as jnp
from jax import lax
import numpy as np

D_MODEL = 1024
BATCH = 1
SEQ = 2048
DEPTH = 1
DEC_BATCH = 8
DEC_SEQ = 4
PAST_LEN = 16384
PAGE_SIZE = 128

MIX_WIDTH = D_MODEL
GLA_WIDTH = MIX_WIDTH // 2
GMLP_WIDTH = MIX_WIDTH - GLA_WIDTH
GLA_HEADS = 4
GLA_DV = GLA_WIDTH // GLA_HEADS
GLA_KEY = GLA_WIDTH // 2
GLA_DK = GLA_KEY // GLA_HEADS
GLA_GATE_RANK = 16
GLA_TAU = 16.0
GLA_CHUNK = 64
GMLP_HEADS = 4
GMLP_DC = GMLP_WIDTH // GMLP_HEADS
GMLP_CHUNK = 128
D_FF = 2816
CONV_W = 3
PLE_DIM = 256
EPS = 1e-6
IN_SIZES = (GLA_KEY, GLA_KEY, GLA_WIDTH, GLA_WIDTH, GLA_GATE_RANK, GMLP_WIDTH, GMLP_WIDTH)
IN_COLS = sum(IN_SIZES)
SPLIT_POINTS = tuple(int(s) for s in np.cumsum(IN_SIZES)[:-1])

kernel_name = 'hymba_gla_sgu_convffn_step'

def _rmsnorm(x, g):
    xf = x.astype(jnp.float32)
    y = xf * lax.rsqrt(jnp.mean(xf * xf, axis=-1, keepdims=True) + EPS)
    return (y * g.astype(jnp.float32)).astype(x.dtype)

def _gla_chunk(S, q, k, v, g):
    b = jnp.cumsum(g, axis=2)
    b_last = b[:, :, -1, :]
    o_inter = jnp.einsum('nhld,nhde->nhle', q * jnp.exp(b), S)
    c = q.shape[2]
    causal = jnp.tril(jnp.ones((c, c), dtype=bool))
    diff = b[:, :, :, None, :] - b[:, :, None, :, :]
    decay = jnp.exp(jnp.where(causal[:, :, None], diff, -jnp.inf))
    scores = jnp.einsum('nhid,nhjd,nhijd->nhij', q, k, decay)
    o_intra = jnp.einsum('nhij,nhje->nhie', scores, v)
    k_dec = k * jnp.exp(b_last[:, :, None, :] - b)
    S_new = jnp.exp(b_last)[..., None] * S + jnp.einsum('nhld,nhle->nhde', k_dec, v)
    return S_new, o_inter + o_intra

def _to_chunks(t, c):
    n, h, l, d = t.shape
    return jnp.moveaxis(t.reshape(n, h, l // c, c, d), 2, 0)

def _gla(q, k, v, g, S0):
    q, k, v, g = (jnp.transpose(t, (0, 2, 1, 3)) for t in (q, k, v, g))
    n, h, l, dv = v.shape
    c = min(GLA_CHUNK, l)
    xs = (_to_chunks(q, c), _to_chunks(k, c), _to_chunks(v, c), _to_chunks(g, c))
    S, o = lax.scan(lambda s, inp: _gla_chunk(s, *inp), S0, xs)
    o = jnp.moveaxis(o, 0, 2).reshape(n, h, l, dv)
    return jnp.transpose(o, (0, 2, 1, 3)), S

def _sgu(u, v, g_ln, b_ln, w_s, b_s):
    n, l, _ = v.shape
    vh = v.reshape(n, l, GMLP_HEADS, GMLP_DC).astype(jnp.float32)
    mu = jnp.mean(vh, axis=-1, keepdims=True)
    var = jnp.mean(jnp.square(vh - mu), axis=-1, keepdims=True)
    vn = ((vh - mu) * lax.rsqrt(var + EPS)).reshape(n, l, GMLP_WIDTH)
    vn = (vn * g_ln.astype(jnp.float32) + b_ln.astype(jnp.float32)).astype(v.dtype)
    c = min(GMLP_CHUNK, l)
    w = w_s[:, :c, :c] * jnp.tril(jnp.ones((c, c), dtype=w_s.dtype))
    vc = vn.reshape(n, l // c, c, GMLP_HEADS, GMLP_DC)
    mixed = jnp.einsum('hts,bnshd->bnthd', w, vc) + jnp.transpose(b_s[:, :c])[:, :, None]
    return u * mixed.reshape(n, l, GMLP_WIDTH), vn

def _conv_ffn(h, prefix, w_up, w_conv, b_conv, w_down):
    up = h @ w_up
    full = jnp.concatenate([prefix.astype(up.dtype), up], axis=1)
    l = up.shape[1]
    conv = b_conv
    for j in range(CONV_W):
        conv = conv + full[:, j:j + l] * w_conv[j]
    gate, val = jnp.split(conv, 2, axis=-1)
    y = (jax.nn.gelu(gate) * val) @ w_down
    return y, full[:, -(CONV_W - 1):]

def _layer(x, p, S0, conv_prefix, lw):
    n, l, _ = x.shape
    h = _rmsnorm(x, lw['g_mix_pre'])
    proj = h @ lw['w_in']
    q, k, v, r, glr, u, vs = jnp.split(proj, SPLIT_POINTS, axis=-1)
    gate_logit = (glr @ lw['w_gla_gate'] + lw['b_gla_gate']).astype(jnp.float32)
    g = jax.nn.log_sigmoid(gate_logit) / GLA_TAU
    qh = q.astype(jnp.float32).reshape(n, l, GLA_HEADS, GLA_DK) * (GLA_DK ** -0.5)
    kh = k.astype(jnp.float32).reshape(n, l, GLA_HEADS, GLA_DK)
    vh = v.astype(jnp.float32).reshape(n, l, GLA_HEADS, GLA_DV)
    gh = g.reshape(n, l, GLA_HEADS, GLA_DK)
    o, S_new = _gla(qh, kh, vh, gh, S0.astype(jnp.float32))
    o = _rmsnorm(o, lw['g_gla_out']).reshape(n, l, GLA_WIDTH).astype(x.dtype) * jax.nn.silu(r)
    s_out, v_rows = _sgu(jax.nn.gelu(u), jax.nn.gelu(vs), lw['g_sgu_ln'], lw['b_sgu_ln'],
                         lw['w_spatial'], lw['b_spatial'])
    mix = jnp.concatenate([o, s_out], axis=-1) @ lw['w_out']
    x = x + _rmsnorm(mix, lw['g_mix_post'])
    f, conv_new = _conv_ffn(_rmsnorm(x, lw['g_ffn_pre']), conv_prefix, lw['w_up'], lw['w_conv'],
                            lw['b_conv'], lw['w_down'])
    x = x + _rmsnorm(f, lw['g_ffn_post'])
    gate = jax.nn.sigmoid(_rmsnorm(x, lw['g_ple_in']) @ lw['w_ple_gate'])
    x = x + _rmsnorm((p @ lw['w_ple']) * gate, lw['g_ple_post'])
    return x, S_new, conv_new, v_rows

def setup_inputs(seed: int = 0) -> dict:
    key = jax.random.key(seed)
    ks = jax.random.split(key, 32)
    f32 = jnp.float32
    nrm = lambda k, shape, scale: jax.random.normal(k, shape, f32) * scale
    gain = lambda k, dim: 1.0 + 0.02 * jax.random.normal(k, (DEPTH, dim), f32)
    return {
        'x_prompt': nrm(ks[0], (BATCH, SEQ, D_MODEL), 1.0),
        'x_sample': nrm(ks[1], (DEC_BATCH, DEC_SEQ, D_MODEL), 1.0),
        'state_gla': nrm(ks[2], (DEPTH, DEC_BATCH, GLA_HEADS, GLA_DK, GLA_DV), 1.0),
        'state_ffn_conv': nrm(ks[3], (DEPTH, DEC_BATCH, CONV_W - 1, 2 * D_FF), 1.0),
        'p_prompt': nrm(ks[4], (DEPTH, BATCH, SEQ, PLE_DIM), 1.0),
        'p_sample': nrm(ks[5], (DEPTH, DEC_BATCH, DEC_SEQ, PLE_DIM), 1.0),
        'g_mix_pre': gain(ks[6], D_MODEL),
        'w_in': nrm(ks[7], (DEPTH, D_MODEL, IN_COLS), D_MODEL ** -0.5),
        'w_gla_gate': nrm(ks[8], (DEPTH, GLA_GATE_RANK, GLA_KEY), GLA_GATE_RANK ** -0.5),
        'b_gla_gate': nrm(ks[9], (DEPTH, GLA_KEY), 0.1),
        'g_gla_out': gain(ks[10], GLA_DV),
        'g_sgu_ln': gain(ks[11], GMLP_WIDTH),
        'b_sgu_ln': nrm(ks[12], (DEPTH, GMLP_WIDTH), 0.02),
        'w_spatial': nrm(ks[13], (DEPTH, GMLP_HEADS, GMLP_CHUNK, GMLP_CHUNK), GMLP_CHUNK ** -0.5),
        'b_spatial': 1.0 + nrm(ks[14], (DEPTH, GMLP_HEADS, GMLP_CHUNK), 0.02),
        'w_out': nrm(ks[15], (DEPTH, MIX_WIDTH, D_MODEL), MIX_WIDTH ** -0.5),
        'g_mix_post': gain(ks[16], D_MODEL),
        'g_ffn_pre': gain(ks[17], D_MODEL),
        'w_up': nrm(ks[18], (DEPTH, D_MODEL, 2 * D_FF), D_MODEL ** -0.5),
        'w_conv': nrm(ks[19], (DEPTH, CONV_W, 2 * D_FF), CONV_W ** -0.5),
        'b_conv': nrm(ks[20], (DEPTH, 2 * D_FF), 0.02),
        'w_down': nrm(ks[21], (DEPTH, D_FF, D_MODEL), D_FF ** -0.5),
        'g_ffn_post': gain(ks[22], D_MODEL),
        'g_ple_in': gain(ks[23], D_MODEL),
        'w_ple_gate': nrm(ks[24], (DEPTH, D_MODEL, D_MODEL), D_MODEL ** -0.5),
        'w_ple': nrm(ks[25], (DEPTH, PLE_DIM, D_MODEL), PLE_DIM ** -0.5),
        'g_ple_post': gain(ks[26], D_MODEL),
    }

def reference(x_prompt, x_sample, state_gla, state_ffn_conv, p_prompt, p_sample,
              g_mix_pre, w_in, w_gla_gate, b_gla_gate, g_gla_out, g_sgu_ln, b_sgu_ln,
              w_spatial, b_spatial, w_out, g_mix_post, g_ffn_pre, w_up, w_conv, b_conv,
              w_down, g_ffn_post, g_ple_in, w_ple_gate, w_ple, g_ple_post):
    yp, ys = x_prompt, x_sample
    nb = x_prompt.shape[0]
    gla_p, gla_s, conv_p, conv_s, vrows_s = [], [], [], [], []
    for i in range(DEPTH):
        lw = {
            'g_mix_pre': g_mix_pre[i], 'w_in': w_in[i], 'w_gla_gate': w_gla_gate[i],
            'b_gla_gate': b_gla_gate[i], 'g_gla_out': g_gla_out[i], 'g_sgu_ln': g_sgu_ln[i],
            'b_sgu_ln': b_sgu_ln[i], 'w_spatial': w_spatial[i], 'b_spatial': b_spatial[i],
            'w_out': w_out[i], 'g_mix_post': g_mix_post[i], 'g_ffn_pre': g_ffn_pre[i],
            'w_up': w_up[i], 'w_conv': w_conv[i], 'b_conv': b_conv[i], 'w_down': w_down[i],
            'g_ffn_post': g_ffn_post[i], 'g_ple_in': g_ple_in[i], 'w_ple_gate': w_ple_gate[i],
            'w_ple': w_ple[i], 'g_ple_post': g_ple_post[i],
        }
        S0p = jnp.zeros((nb, GLA_HEADS, GLA_DK, GLA_DV), jnp.float32)
        c0p = jnp.zeros((nb, CONV_W - 1, 2 * D_FF), yp.dtype)
        yp, Sp, cp, _ = _layer(yp, p_prompt[i], S0p, c0p, lw)
        ys, Ss, cs, vr = _layer(ys, p_sample[i], state_gla[i], state_ffn_conv[i], lw)
        gla_p.append(Sp)
        gla_s.append(Ss)
        conv_p.append(cp)
        conv_s.append(cs)
        vrows_s.append(vr)
    new_state_gla_prompt = jnp.stack(gla_p)
    new_state_gla_sample = jnp.stack(gla_s)
    new_state_ffn_conv_prompt = jnp.stack(conv_p)
    new_state_ffn_conv_sample = jnp.stack(conv_s)
    new_state_sgu_v_sample = jnp.stack(vrows_s)
    return (yp, ys, new_state_gla_prompt, new_state_gla_sample, new_state_ffn_conv_prompt,
            new_state_ffn_conv_sample, new_state_sgu_v_sample)


_drawn_inputs = setup_inputs


def setup_inputs(seed=0):
    import zlib

    import numpy as np

    out = dict(_drawn_inputs(seed))
    spreads = {}
    factors = {'g_gla_out': 15.155,
     'g_sgu_ln': 20.236,
     'b_sgu_ln': 21.328,
     'b_spatial': 18.517,
     'g_mix_post': 3.902,
     'g_ffn_pre': 2.851,
     'b_conv': 3.882,
     'g_ffn_post': 18.26,
     'g_ple_in': 33.821,
     'g_ple_post': 84.783}
    for name, (base, spread) in spreads.items():
        noise = np.random.default_rng([zlib.crc32(name.encode()), seed]).standard_normal(out[name].shape)
        drawn = base * np.exp(spread * noise) if base else spread * noise
        out[name] = __import__('jax').numpy.asarray(drawn.astype(out[name].dtype))
    for name, factor in factors.items():
        out[name] = (out[name] * factor).astype(out[name].dtype)
    return out
```

```python
import concourse.bass as bass
from concourse import mybir
from contextlib import ExitStack

F32 = mybir.dt.float32
F32R = mybir.dt.float32r
I32 = mybir.dt.int32
ALU = mybir.AluOpType
ACT = mybir.ActivationFunctionType

P = 128
D = 1024
KC = D // P
TP = 2048
SEQS, SL = 8, 4
TS = SEQS * SL
T = TP + TS
NT = TP // P
TB = 416
NBLK = T // TB
H, DK, DV = 4, 64, 128
C = 64
NCH = P // C
RANK = 16
TAU = 16.0
HS = 4
FF = 2816
FC = FF // P
PLE = 256
PC = PLE // P
EPS = 1e-6
COL_QK, COL_V, COL_R, COL_GLR = 0, 512, 1024, 1536
COL_U, COL_VS = 1552, 2064


def ds(start, size):
    return bass.ds(start, size)


def bcast(ap, n):
    return ap.unsqueeze(2).to_broadcast([ap.shape[0], ap.shape[1], n])


def tile_rows(t):
    return P if t < NT else TS


def rows_in_bank(t):
    return slice(0, P) if t < NT else slice(P - TS, P)


def identity_and_ones(nc, ident, ones, made):
    nc.gpsimd.memset(ident[:, :], 0.0).then_inc(made, 1)
    nc.gpsimd.memset(ones[:, :], 1.0).then_inc(made, 1)
    nc.gpsimd.wait_ge(made, 2)
    nc.gpsimd.affine_select(out=ident[:, :], in_=ident[:, :], compare_op=ALU.not_equal, fill=1.0,
                            base=0, pattern=[[-1, P]], channel_multiplier=1).then_inc(made, 1)


def rstd_ops(nc, pool, out, parts, tmp, consts, step, base):
    terms = list(parts) + [consts[:, 0:1]]
    for i in range(1, len(terms)):
        left = terms[0] if i == 1 else tmp
        if i > 1:
            pool.wait_ge(step, base + (i - 1))
        nc.gpsimd.tensor_tensor(tmp, left, terms[i], ALU.add).then_inc(step, 1)
    pool.wait_ge(step, base + len(parts))
    nc.gpsimd.tensor_tensor(out, tmp, consts[:, 1:2], ALU.pow).then_inc(step, 1)


def phase_norm(nc, tag, sources, xh, xl, ident, consts):
    ctx = ExitStack()
    with ctx:
        sb = lambda n, s, d=F32: ctx.enter_context(nc.sbuf_tensor(f"{tag}_{n}", s, d))
        sem = phase_semaphores(nc, ctx, tag)
        x = [sb(f"x{i}", [P, D]) for i in range(2)]
        xn = [sb(f"xn{i}", [P, D]) for i in range(2)]
        square = [sb(f"square{i}", [P, D]) for i in range(2)]
        total = sb("total", [P, 2])
        mean = sb("mean", [P, 2])
        rstd = sb("rstd", [P, 2])
        pt = [[ctx.enter_context(nc.psum_tensor(f"{tag}_pt{i}{h}", [P, 512], F32)) for h in range(2)]
              for i in range(2)]
        loaded = [sem("loaded0"), sem("loaded1")]
        summed, powers, scaled = sem("summed"), sem("powers"), sem("scaled")
        turned, rounded, split = sem("turned"), sem("rounded"), sem("split")
        block = ctx.enter_context(nc.Block())

        def loop(eng, tile):
            tile(0, 0, True)
            tile(1, 1, True)
            with eng.Fori(1, NT // 2) as i:
                tile(i * 2, 0, False)
                tile(i * 2 + 1, 1, False)
            tile(NT, 0, False)

        def rows_of(t):
            return tile_rows(t) if isinstance(t, int) else P

        def turn(t):
            return t // 2 if isinstance(t, int) else t // 2

        @block.sync
        def _(sp):
            def tile(t, s, first):
                n = rows_of(t)
                if not first:
                    sp.wait_ge(scaled, t - 1)
                sp.dma_start(x[s][0:n, :], sources(t)).then_inc(loaded[s], 16)
            loop(sp, tile)

        @block.scalar
        def _(act):
            def sums(t, s, k):
                n = rows_of(t)
                act.wait_ge(loaded[s], k * 16 + 16)
                nc.scalar.activation(square[s][0:n, :], x[s][0:n, :], ACT.Square, scale=D ** -0.5,
                                     accum_out=total[0:n, s:s + 1]).then_inc(summed, 1)

            def rounds(t, s):
                n = rows_of(t)
                for h in range(2):
                    nc.scalar.activation(xh[:, 4 * h:4 * h + 4, ds(t * P, n)],
                                         pt[s][h][:, 0:4 * n].rearrange("p (k t) -> p k t", k=4),
                                         ACT.Copy).then_inc(rounded, 1)

            def step(t, s, i):
                act.wait_ge(turned, t * 2 + 2)
                if not isinstance(t, int) or t + 2 <= NT:
                    sums(t + 2, s, i + 1)
                rounds(t, s)
            sums(0, 0, 0)
            sums(1, 1, 0)
            with act.Fori(0, NT // 2 - 1) as i:
                step(i * 2, 0, i)
                step(i * 2 + 1, 1, i)
            for t in range(NT - 2, NT + 1):
                step(t, t % 2, t // 2)

        @block.gpsimd
        def _(pool):
            def tile(t, s, first):
                n = rows_of(t)
                pool.wait_ge(summed, t + 1)
                if not first:
                    pool.wait_ge(scaled, t - 1)
                rstd_ops(nc, pool, rstd[0:n, s:s + 1], [total[0:n, s:s + 1]], mean[0:n, s:s + 1],
                         consts[0:n, :], powers, t * 2)
            loop(pool, tile)

        @block.vector
        def _(dve):
            def scales(t, s, first):
                n = rows_of(t)
                dve.wait_ge(powers, t * 2 + 2)
                if not first:
                    dve.wait_ge(turned, t * 2 - 2)
                nc.vector.tensor_scalar(xn[s][0:n, :], x[s][0:n, :], rstd[0:n, s:s + 1], None,
                                        ALU.mult).then_inc(scaled, 1)

            def splits(t, s):
                n = rows_of(t)
                for h in range(2):
                    dve.wait_ge(rounded, t * 2 + h + 1)
                    here = (slice(None), slice(4 * h, 4 * h + 4), ds(t * P, n))
                    nc.vector.tensor_tensor(xl[here], pt[s][h][:, 0:4 * n].rearrange("p (k t) -> p k t", k=4),
                                            xh[here].bitcast(F32), ALU.subtract).then_inc(split, 1)
            scales(0, 0, True)
            scales(1, 1, True)
            splits(0, 0)
            with dve.Fori(1, NT // 2) as i:
                scales(i * 2, 0, False)
                splits(i * 2 - 1, 1)
                scales(i * 2 + 1, 1, False)
                splits(i * 2, 0)
            scales(NT, 0, False)
            splits(NT - 1, 1)
            splits(NT, 0)

        @block.tensor
        def _(pe):
            def tile(t, s, first):
                n = rows_of(t)
                pe.wait_ge(scaled, t + 1)
                if not first:
                    pe.wait_ge(split, t * 2 - 2)
                for h in range(2):
                    for k in range(4):
                        f = (4 * h + k) * P
                        last = nc.tensor.transpose(pt[s][h][:, k * n:(k + 1) * n], xn[s][0:n, f:f + P],
                                                   ident[0:n, 0:n])
                    last.then_inc(turned, 1)
            loop(pe, tile)


def phase_in(nc, xh, xl, w_in, gain, pt_scratch, v_scratch, vs_scratch):
    ctx = ExitStack()
    with ctx:
        sb = lambda n, s, d=F32: ctx.enter_context(nc.sbuf_tensor(f"in_{n}", s, d))
        sem = phase_semaphores(nc, ctx, "in")
        BANKS = 5
        SLOTS = 4
        raw = [sb(f"raw{i}", [P, KC, P]) for i in range(2)]
        wh = sb("wh", [P, SLOTS, KC, P], F32R)
        wl = sb("wl", [P, SLOTS, KC, P], F32R)
        out = [sb(f"out{i}", [P, 512]) for i in range(BANKS)]
        acc = [ctx.enter_context(nc.psum_tensor(f"in_acc{i}", [P, 512], F32)) for i in range(BANKS)]
        raw_in = [sem("raw_in0"), sem("raw_in1")]
        gained, high, ready = sem("gained"), sem("high"), sem("ready")
        summed, evacuated = sem("summed"), sem("evacuated")
        stored = [sem(f"stored{i}") for i in range(BANKS)]
        block = ctx.enter_context(nc.Block())

        wide = 2 * 4
        cols = [COL_V + P * i for i in range(4)] + [COL_VS + P * i for i in range(4)]
        cols += [COL_QK + P * i for i in range(4)] + [COL_R + P * i for i in range(4)]
        cols += [COL_U + P * i for i in range(4)] + [COL_GLR]
        n_chunks = len(cols)
        slot = [n % SLOTS if n < wide else n % 2 for n in range(n_chunks)]
        first_bank = 2 * (NT + 1)
        w_view = w_in.rearrange("(k p) n -> p k n", p=P)

        def slot_free(eng, n):
            if 4 <= n < wide:
                eng.wait_ge(summed, NT + 1)
            elif wide <= n < wide + 2:
                eng.wait_ge(summed, first_bank)
            elif n >= wide + 2:
                eng.wait_ge(summed, first_bank + (n - 1 - wide) * NBLK)

        @block.sync
        def _(sp):
            def load(n):
                if n >= 2:
                    sp.wait_ge(ready, n - 1)
                sp.dma_start(raw[n % 2][:, :, :], w_view[:, :, cols[n]:cols[n] + P]).then_inc(raw_in[n % 2], 16)

            def store(m, dst, rows, width):
                sp.wait_ge(evacuated, m + 1)
                sp.dma_start(dst, out[m % BANKS][rows, 0:width]).then_inc(stored[m % BANKS], 16)

            for n in range(6):
                load(n)
            for g, scratch in enumerate((v_scratch, vs_scratch)):
                if g == 1:
                    for n in range(6, wide + 2):
                        load(n)
                for t in range(NT + 1):
                    store(g * (NT + 1) + t, scratch[t * P:t * P + tile_rows(t), :], rows_in_bank(t), 512)
            for n in range(wide, n_chunks):
                if n + 2 < n_chunks:
                    load(n + 2)
                for b in range(NBLK):
                    store(first_bank + (n - wide) * NBLK + b,
                          pt_scratch[(n - wide) * P:(n - wide + 1) * P, b * TB:(b + 1) * TB], slice(0, P), TB)
            total = first_bank + (n_chunks - wide) * NBLK
            for i in range(BANKS):
                sp.wait_ge(stored[i], 16 * len(range(i, total, BANKS)))

        @block.gpsimd
        def _(pool):
            for n in range(n_chunks):
                pool.wait_ge(raw_in[n % 2], 16 * (n // 2 + 1))
                nc.gpsimd.tensor_tensor(raw[n % 2][:, :, :], raw[n % 2][:, :, :], bcast(gain[:, :], P),
                                        ALU.mult).then_inc(gained, 1)

        @block.vector
        def _(dve):
            for n in range(n_chunks):
                dve.wait_ge(high, n + 1)
                nc.vector.tensor_tensor(wl[:, slot[n]], raw[n % 2][:, :, :], wh[:, slot[n]].bitcast(F32),
                                        ALU.subtract).then_inc(ready, 1)

        @block.scalar
        def _(act):
            def round_up(n):
                act.wait_ge(gained, n + 1)
                slot_free(act, n)
                nc.scalar.activation(wh[:, slot[n]], raw[n % 2][:, :, :], ACT.Copy).then_inc(high, 1)

            def evacuate(m, bank, rows, width, func):
                act.wait_ge(summed, m + 1)
                if m >= BANKS:
                    act.wait_ge(stored[bank], m // BANKS * 16)
                nc.scalar.activation(out[bank][rows, 0:width], acc[bank][rows, 0:width], func)\
                    .then_inc(evacuated, 1)

            for n in range(4):
                round_up(n)
            for g, func in enumerate((ACT.Copy, ACT.Gelu_apprx_tanh)):
                for t in range(NT + 1):
                    m = g * (NT + 1) + t
                    evacuate(m, m % BANKS, rows_in_bank(t), 512, func)
                for n in range(4 * g + 4, 4 * g + (8 if g == 0 else 5)):
                    round_up(n)
            for n in range(wide, n_chunks):
                func = ACT.Copy if n < wide + 4 or n == n_chunks - 1 else \
                    (ACT.Silu if n < wide + 8 else ACT.Gelu_apprx_tanh)
                for b in range(NBLK):
                    m = first_bank + (n - wide) * NBLK + b
                    evacuate(m, m % BANKS, slice(0, P), TB, func)
                    if b == 0 and n + 1 < n_chunks:
                        round_up(n + 1)

        @block.tensor
        def _(pe):
            for g in range(2):
                pe.wait_ge(ready, 4 * g + 4)
                for t in range(NT + 1):
                    m = g * (NT + 1) + t
                    first = min(t * P, T - P)
                    if m >= BANKS:
                        pe.wait_ge(evacuated, m - BANKS + 1)
                    for k in range(KC):
                        for p, (x, w) in enumerate(((xh, wh), (xh, wl), (xl, wh))):
                            last = nc.tensor.matmul(acc[m % BANKS][:, :], x[:, k, first:first + P], w[:, :, k, :],
                                                    start=(k == 0 and p == 0), stop=(k == KC - 1 and p == 2))
                    last.then_inc(summed, 1)

            def chunk(c, s, m0):
                pe.wait_ge(ready, c + (wide + 1))
                for b in range(NBLK):
                    m = m0 + b
                    bank = (first_bank + s * NBLK + b) % BANKS
                    pe.wait_ge(evacuated, m - (BANKS - 1))
                    for k in range(KC):
                        for p, (w, x) in enumerate(((wh, xh), (wh, xl), (wl, xh))):
                            last = nc.tensor.matmul(acc[bank][:, 0:TB], w[:, s, k, :],
                                                    x[:, k, b * TB:(b + 1) * TB],
                                                    start=(k == 0 and p == 0), stop=(k == KC - 1 and p == 2))
                    last.then_inc(summed, 1)
            chunk_pairs = (n_chunks - wide) // 2
            with pe.Fori(0, chunk_pairs) as i:
                for s in range(2):
                    chunk(i * 2 + s, s, i * (2 * NBLK) + (first_bank + s * NBLK))
            chunk(2 * chunk_pairs, 0, first_bank + 2 * chunk_pairs * NBLK)


def phase_semaphores(nc, ctx, tag):
    held = []

    def clear():
        nc.clear_and_free_semaphores(held)
        nc.all_engine_barrier()
    ctx.callback(clear)

    def sem(name):
        held.append(nc.alloc_semaphore(name=f"{tag}_{name}"))
        return held[-1]
    return sem


def walk(eng, step):
    step(0, 0, 0)
    step(1, 1, 0)
    with eng.Fori(1, NT // 2 - 1) as i:
        step(i * 2, 0, i)
        step(i * 2 + 1, 1, i)
    step(NT - 2, 0, NT // 2 - 1)
    step(NT - 1, 1, NT // 2 - 1)
    step(NT, 0, NT // 2)


def known(t):
    return isinstance(t, int)


def tokens_of(t):
    return slice(min(t * P, T - P), min(t * P, T - P) + P) if known(t) else ds(t * P, P)


def bank_rows(t):
    return rows_in_bank(t) if known(t) else slice(0, P)


def token_rows(t):
    return slice(t * P, t * P + tile_rows(t)) if known(t) else ds(t * P, P)


def phase_rows(nc, tag, src, kc, w, width, gain=None, first_half=None, residual=None, store=None, scratch=None,
               consts=None):
    ctx = ExitStack()
    with ctx:
        sb = lambda n, s, d=F32: ctx.enter_context(nc.sbuf_tensor(f"{tag}_{n}", s, d))
        sem = phase_semaphores(nc, ctx, tag)
        halves = width // 512
        wraw = [sb(f"wraw{i}", [P, width]) for i in range(2)]
        wh, wl = sb("wh", [P, kc, width], F32R), sb("wl", [P, kc, width], F32R)
        raw = [sb(f"raw{i}", [P, kc, P]) for i in range(2)]
        sh = [sb(f"sh{i}", [P, kc, P], F32R) for i in range(2)]
        sl = [sb(f"sl{i}", [P, kc, P], F32R) for i in range(2)]
        acc = [[ctx.enter_context(nc.psum_tensor(f"{tag}_acc{i}{h}", [P, 512], F32)) for h in range(halves)]
               for i in range(2)]
        y = [sb(f"y{i}", [P, width if gain is None else D]) for i in range(2)]
        wraw_in = [sem("wraw_in0"), sem("wraw_in1")]
        whigh, wready = sem("whigh"), sem("wready")
        src_in = [sem("src_in0"), sem("src_in1")]
        high, split, summed = sem("high"), sem("split"), sem("summed")
        stored = [sem("stored0"), sem("stored1")]
        finished = sem("finished")
        if gain is not None:
            junk = [[sb(f"junk{i}{h}", [P, 512]) for h in range(2)] for i in range(2)]
            gain_rows = sb("gain_rows", [P, D])
            res = [sb(f"res{i}", [P, D]) for i in range(2)]
            part = sb("part", [P, 2, 2])
            mean, rstd = sb("mean", [P, 2]), sb("rstd", [P, 2])
            gain_in = sem("gain_in")
            res_in = [sem("res_in0"), sem("res_in1")]
            squared, powers, added = sem("squared"), sem("powers"), sem("added")
            if first_half is not None:
                half = [sb(f"half{i}", [P, 512]) for i in range(2)]
                half_in = [sem("half_in0"), sem("half_in1")]
        block = ctx.enter_context(nc.Block())
        w_view = w.rearrange("(k p) n -> p k n", p=P)
        src_view = src.rearrange("(k p) t -> p k t", p=P)

        @block.sync
        def _(sp):
            def load_w(k):
                if k >= 2:
                    sp.wait_ge(wready, k - 1)
                sp.dma_start(wraw[k % 2][:, :], w_view[:, k, :]).then_inc(wraw_in[k % 2], 16)

            def load_src(t, s):
                if not known(t) or t >= 2:
                    sp.wait_ge(split, t - 1)
                sp.dma_start(raw[s][:, :, :], src_view[:, :, tokens_of(t)]).then_inc(src_in[s], 16)

            def load_rest(t, s):
                if gain is not None:
                    if not known(t) or t >= 2:
                        sp.wait_ge(added, t - 1)
                    sp.dma_start(res[s][bank_rows(t), :], residual(t)).then_inc(res_in[s], 16)
                    if first_half is not None:
                        sp.dma_start(half[s][bank_rows(t), :], first_half[token_rows(t), :])\
                            .then_inc(half_in[s], 16)

            def step(t, s, i):
                if not known(t) or t + 2 <= NT:
                    load_src(t + 2, s)
                if not known(t) or t < NT:
                    load_rest(t + 1, 1 - s)
                if gain is None:
                    sp.wait_ge(finished, t + 1)
                    sp.dma_start(scratch[token_rows(t), :], y[s][bank_rows(t), :]).then_inc(stored[s], 16)
                else:
                    sp.wait_ge(added, t + 1)
                    sp.dma_start(store(t), y[s][bank_rows(t), :]).then_inc(stored[s], 16)

            if gain is not None:
                sp.dma_start(gain_rows[:, :], gain.partition_broadcast(P)).then_inc(gain_in, 16)
            load_w(0)
            load_w(1)
            load_src(0, 0)
            load_rest(0, 0)
            for k in range(2, kc):
                load_w(k)
            load_src(1, 1)
            walk(sp, step)
            sp.wait_ge(stored[0], 16 * (NT // 2 + 1))
            sp.wait_ge(stored[1], 16 * (NT // 2))

        @block.scalar
        def _(act):
            def rounds(t, s, i):
                act.wait_ge(src_in[s], i * 16 + 16)
                if not known(t) or t >= 2:
                    act.wait_ge(summed, (t - 1) * halves)
                nc.scalar.activation(sh[s][:, :, :], raw[s][:, :, :], ACT.Copy).then_inc(high, 1)

            def step(t, s, i):
                if not known(t) or t < NT:
                    rounds(t + 1, 1 - s, i + s)
                rows = bank_rows(t)
                if gain is None:
                    for h in range(halves):
                        act.wait_ge(summed, t * halves + (h + 1))
                    if not known(t) or t >= 2:
                        act.wait_ge(stored[s], i * 16)
                    nc.scalar.activation(y[s][rows, :], acc[s][0][rows, :], ACT.Copy).then_inc(finished, 1)
                    return
                if not known(t) or t >= 2:
                    act.wait_ge(powers, (t - 1) * 3)
                if first_half is not None:
                    act.wait_ge(half_in[s], i * 16 + 16)
                for h in range(2):
                    if first_half is not None and h == 0:
                        half_row = half[s]
                    else:
                        b = h if halves == 2 else 0
                        act.wait_ge(summed, t * halves + (b + 1))
                        half_row = acc[s][b]
                    nc.scalar.activation(junk[s][h][rows, :], half_row[rows, :], ACT.Square, scale=D ** -0.5,
                                         accum_out=part[rows, s, h:h + 1]).then_inc(squared, 1)

            for k in range(kc):
                act.wait_ge(wraw_in[k % 2], 16 * (k // 2 + 1))
                nc.scalar.activation(wh[:, k, :], wraw[k % 2][:, :], ACT.Copy).then_inc(whigh, 1)
                if k == 1:
                    rounds(0, 0, 0)
            walk(act, step)

        @block.vector
        def _(dve):
            def splits(t, s):
                dve.wait_ge(high, t + 1)
                nc.vector.tensor_tensor(sl[s][:, :, :], raw[s][:, :, :], sh[s][:, :, :].bitcast(F32),
                                        ALU.subtract).then_inc(split, 1)

            def step(t, s, i):
                if not known(t) or t < NT:
                    splits(t + 1, 1 - s)
                if gain is None:
                    return
                rows = bank_rows(t)
                dve.wait_ge(powers, t * 3 + 3)
                if not known(t) or t >= 2:
                    dve.wait_ge(stored[s], i * 16)
                for h in range(2):
                    if first_half is not None and h == 0:
                        half_row = half[s]
                    else:
                        half_row = acc[s][h if halves == 2 else 0]
                    nc.vector.scalar_tensor_tensor(out=y[s][rows, 512 * h:512 * h + 512], in0=half_row[rows, :],
                                                   scalar=rstd[rows, s:s + 1],
                                                   in1=gain_rows[rows, 512 * h:512 * h + 512],
                                                   op0=ALU.mult, op1=ALU.mult).then_inc(finished, 1)

            for k in range(kc):
                dve.wait_ge(whigh, k + 1)
                nc.vector.tensor_tensor(wl[:, k, :], wraw[k % 2][:, :], wh[:, k, :].bitcast(F32),
                                        ALU.subtract).then_inc(wready, 1)
                if k == 1:
                    splits(0, 0)
            if gain is not None:
                dve.wait_ge(gain_in, 16)
            walk(dve, step)

        if gain is not None:
            @block.gpsimd
            def _(pool):
                def step(t, s, i):
                    rows = bank_rows(t)
                    if not known(t) or t >= 1:
                        pool.wait_ge(added, t)
                    pool.wait_ge(squared, t * 2 + 2)
                    if not known(t) or t >= 2:
                        pool.wait_ge(finished, (t - 1) * 2)
                    rstd_ops(nc, pool, rstd[rows, s:s + 1], [part[rows, s, 0:1], part[rows, s, 1:2]],
                             mean[rows, s:s + 1], consts[rows, :], powers, t * 3)
                    pool.wait_ge(res_in[s], i * 16 + 16)
                    pool.wait_ge(finished, t * 2 + 2)
                    nc.gpsimd.tensor_tensor(y[s][rows, :], y[s][rows, :], res[s][rows, :], ALU.add)\
                        .then_inc(added, 1)
                walk(pool, step)

        @block.tensor
        def _(pe):
            def step(t, s, i):
                pe.wait_ge(split, t + 1)
                if not known(t) or t >= 2:
                    pe.wait_ge(finished, (t - 1) * (1 if gain is None else 2))
                for h in range(halves):
                    for k in range(kc):
                        if known(t) and t == 0 and h == 0:
                            pe.wait_ge(wready, k + 1)
                        for p, (x, ww) in enumerate(((sh, wh), (sh, wl), (sl, wh))):
                            last = nc.tensor.matmul(acc[s][h][:, :], x[s][:, k, :],
                                                    ww[:, k, 512 * h:512 * h + 512],
                                                    start=(k == 0 and p == 0), stop=(k == kc - 1 and p == 2))
                    last.then_inc(summed, 1)
            walk(pe, step)


def phase_up(nc, xh, xl, w_up, gain, taps, bias, prefix, tail, h_scratch):
    ctx = ExitStack()
    with ctx:
        sb = lambda n, s, d=F32: ctx.enter_context(nc.sbuf_tensor(f"up_{n}", s, d))
        sem = phase_semaphores(nc, ctx, "up")
        LAST = TB - TS
        raw = [sb(f"raw{i}", [P, KC, P]) for i in range(2)]
        wh = [sb(f"wh{i}", [P, KC, P], F32R) for i in range(2)]
        wl = [sb(f"wl{i}", [P, KC, P], F32R) for i in range(2)]
        up = [sb(f"up{b}", [P, 2 + TB]) for b in range(NBLK)]
        up_s = sb("up_s", [P, SEQS, 2 + SL])
        conv = [sb(f"conv{b}", [P, TB]) for b in range(NBLK)]
        gate = [sb(f"gate{b}", [P, TB]) for b in range(NBLK)]
        acc = [ctx.enter_context(nc.psum_tensor(f"up_acc{b}", [P, 512], F32)) for b in range(NBLK)]
        raw_in = [sem("raw_in0"), sem("raw_in1")]
        gained, high, ready = sem("gained"), sem("high"), sem("ready")
        summed = sem("summed")
        evacuated = sem("evacuated")
        prefixed = sem("prefixed")
        tapped = sem("tapped")
        convolved = sem("convolved")
        gated = sem("gated")
        kept = sem("kept")
        made = sem("made")
        zeroed = sem("zeroed")
        stored = [sem(f"stored{b}") for b in range(NBLK)]
        block = ctx.enter_context(nc.Block())
        w_view = w_up.rearrange("(k p) n -> p k n", p=P)

        @block.sync
        def _(sp):
            def load(j, kind, n, turn):
                if not known(n) or n >= 2:
                    sp.wait_ge(ready, n - 1)
                sp.dma_start(raw[kind][:, :, :], w_view[:, :, ds(j * P + kind * FF, P)]).then_inc(raw_in[kind], 16)

            def store(j):
                for b in range(NBLK):
                    sp.wait_ge(made, j * NBLK + (b + 1))
                    sp.dma_start(h_scratch[ds(j * P, P), b * TB:(b + 1) * TB], conv[b][:, :])\
                        .then_inc(stored[b], 16)
            load(0, 0, 0, 0)
            load(0, 1, 1, 0)
            with sp.Fori(0, FC - 1) as j:
                for kind in range(2):
                    load(j + 1, kind, j * 2 + (2 + kind), j + 1)
                store(j)
            store(FC - 1)
            for b in range(NBLK):
                sp.wait_ge(stored[b], 16 * FC)

        @block.gpsimd
        def _(pool):
            def gains(n, kind, j):
                pool.wait_ge(raw_in[kind], j * 16 + 16)
                nc.gpsimd.tensor_tensor(raw[kind][:, :, :], raw[kind][:, :, :], bcast(gain, P), ALU.mult)\
                    .then_inc(gained, 1)

            def keep(j, kind):
                pool.wait_ge(evacuated, j * (2 * NBLK) + (NBLK * (kind + 1)))
                at = ds(j + kind * FC, 1)
                nc.gpsimd.tensor_copy(tail[:, at, 0:2].rearrange("p a c -> p (a c)"), up[NBLK - 1][:, LAST:LAST + 2])
                nc.gpsimd.tensor_copy(tail[:, at, 2:18].rearrange("p a (q c) -> p (a q) c", c=2),
                                      up_s[:, :, SL:SL + 2]).then_inc(kept, 1)

            def history(j, kind, n):
                if not (known(n) and n == 0):
                    pool.wait_ge(convolved, n * NBLK)
                nc.gpsimd.tensor_copy(up_s[:, :, 0:2], prefix[:, ds(j + kind * FC, 1), :]
                                      .rearrange("p a (q c) -> p (a q) c", c=2)).then_inc(prefixed, 1)

            nc.gpsimd.memset(up[0][:, 0:2], 0.0).then_inc(zeroed, 1)
            gains(0, 0, 0)
            history(0, 0, 0)
            with pool.Fori(0, FC - 1) as j:
                gains(None, 1, j)
                keep(j, 0)
                history(j, 1, j * 2 + 1)
                gains(None, 0, j + 1)
                keep(j, 1)
                history(j + 1, 0, j * 2 + 2)
            gains(None, 1, FC - 1)
            keep(FC - 1, 0)
            history(FC - 1, 1, 2 * FC - 1)
            keep(FC - 1, 1)

        @block.scalar
        def _(act):
            def rounds(n, kind):
                act.wait_ge(gained, n + 1)
                if not known(n) or n >= 2:
                    act.wait_ge(summed, (n - 1) * NBLK)
                nc.scalar.activation(wh[kind][:, :, :], raw[kind][:, :, :], ACT.Copy).then_inc(high, 1)

            def block_out(j, kind, n, b, first):
                act.wait_ge(summed, n * NBLK + (b + 1))
                at = ds(j + kind * FC, 1)
                a = acc[b]
                prompt = TB if b < NBLK - 1 else LAST
                if not first:
                    act.wait_ge(convolved, (n - 1) * NBLK + (min(b + 2, NBLK)))
                    if b == NBLK - 1:
                        act.wait_ge(kept, n)
                if kind == 0:
                    if not first:
                        act.wait_ge(stored[b], j * 16)
                else:
                    act.wait_ge(gated, j * NBLK + (b + 1))
                if b == NBLK - 1:
                    act.wait_ge(prefixed, n + 1)
                nc.scalar.activation(up[b][:, 2:2 + prompt], a[:, 0:prompt], ACT.Copy)
                if b < NBLK - 1:
                    nc.scalar.activation(up[b + 1][:, 0:2], a[:, TB - 2:TB], ACT.Copy)
                else:
                    nc.scalar.activation(up_s[:, :, 2:2 + SL], a[:, LAST:TB].rearrange("p (q c) -> p q c", c=SL),
                                         ACT.Copy)
                nc.scalar.activation(conv[b][:, :], a[:, 0:TB], ACT.Identity,
                                     scale=taps[:, at, 2:3].rearrange("p a c -> p (a c)"),
                                     bias=bias[:, at]).then_inc(evacuated, 1)

            def gelu(j, b, first):
                act.wait_ge(convolved, j * (2 * NBLK) + (b + 1))
                if not first:
                    act.wait_ge(made, (j - 1) * NBLK + (b + 1))
                nc.scalar.activation(gate[b][:, :], conv[b][:, :], ACT.Gelu_apprx_tanh).then_inc(gated, 1)

            def pair(j, first, last):
                for b in range(NBLK):
                    block_out(j, 0, j * 2, b, first)
                    if b == 0:
                        rounds(j * 2 + 1, 1)
                    else:
                        gelu(j, b - 1, first)
                gelu(j, NBLK - 1, first)
                for b in range(NBLK):
                    block_out(j, 1, j * 2 + 1, b, False)
                    if b == 0 and not last:
                        rounds(j * 2 + 2, 0)

            act.wait_ge(zeroed, 1)
            rounds(0, 0)
            pair(0, True, False)
            with act.Fori(1, FC - 1) as j:
                pair(j, False, False)
            pair(FC - 1, False, True)

        @block.vector
        def _(dve):
            def splits(n, kind):
                dve.wait_ge(high, n + 1)
                nc.vector.tensor_tensor(wl[kind][:, :, :], raw[kind][:, :, :], wh[kind][:, :, :].bitcast(F32),
                                        ALU.subtract).then_inc(ready, 1)

            def convolve(j, kind, n, b, base):
                dve.wait_ge(evacuated, n * NBLK + (b + 1))
                at = ds(j + kind * FC, 1)
                prompt = TB if b < NBLK - 1 else LAST
                parts = [(conv[b][:, 0:prompt], lambda c: up[b][:, c:c + prompt])]
                if b == NBLK - 1:
                    parts.append((conv[b][:, LAST:TB].rearrange("p (q c) -> p q c", c=SL),
                                  lambda c: up_s[:, :, c:c + SL]))
                for c in (1, 0):
                    if c == 0:
                        dve.wait_ge(tapped, base + 1)
                    for i, (out, x) in enumerate(parts):
                        last = nc.vector.scalar_tensor_tensor(out=out, in0=x(c), in1=out,
                                                              scalar=taps[:, at, c:c + 1].rearrange("p a c -> p (a c)"),
                                                              op0=ALU.mult, op1=ALU.add)
                    last.then_inc(tapped if c == 1 else convolved, 1)

            def product(j, b):
                dve.wait_ge(convolved, j * (2 * NBLK) + (NBLK + b + 1))
                nc.vector.tensor_tensor(conv[b][:, :], conv[b][:, :], gate[b][:, :], ALU.mult).then_inc(made, 1)

            def pair(j, last):
                for b in range(NBLK):
                    convolve(j, 0, j * 2, b, j * (2 * NBLK) + b)
                    if b == 0:
                        splits(j * 2 + 1, 1)
                for b in range(NBLK):
                    convolve(j, 1, j * 2 + 1, b, j * (2 * NBLK) + (NBLK + b))
                    product(j, b)
                    if b == 0 and not last:
                        splits(j * 2 + 2, 0)

            splits(0, 0)
            with dve.Fori(0, FC - 1) as j:
                pair(j, False)
            pair(FC - 1, True)

        @block.tensor
        def _(pe):
            def pair(j, first):
                for kind in range(2):
                    n = j * 2 + kind
                    pe.wait_ge(ready, n + 1)
                    for b in range(NBLK):
                        if not (first and kind == 0):
                            pe.wait_ge(evacuated, (n - 1) * NBLK + (b + 1))
                        for k in range(KC):
                            for p, (w, x) in enumerate(((wh, xh), (wh, xl), (wl, xh))):
                                last = nc.tensor.matmul(acc[b][:, 0:TB], w[kind][:, k, :],
                                                        x[:, k, b * TB:(b + 1) * TB],
                                                        start=(k == 0 and p == 0), stop=(k == KC - 1 and p == 2))
                        last.then_inc(summed, 1)
            pair(0, True)
            with pe.Fori(1, FC) as j:
                pair(j, False)


def phase_ffn_rows(nc, rows, features, ident):
    n_rows, n_cols = 20, 2 * FC
    per_bank = 512 // n_rows
    ctx = ExitStack()
    with ctx:
        flat = ctx.enter_context(nc.sbuf_tensor("fr_flat", [n_rows, 2 * FF], F32))
        acc = [ctx.enter_context(nc.psum_tensor(f"fr_acc{i}", [P, 512], F32)) for i in range(2)]
        sem = phase_semaphores(nc, ctx, "fr")
        loaded, turned = sem("loaded"), sem("turned")
        block = ctx.enter_context(nc.Block())

        @block.sync
        def _(sp):
            at = 0
            for r in rows:
                sp.dma_start(flat[at:at + r.shape[0], :], r).then_inc(loaded, 16)
                at += r.shape[0]

        @block.tensor
        def _(pe):
            pe.wait_ge(loaded, 16 * len(rows))
            for f in range(n_cols):
                b, q = divmod(f, per_bank)
                nc.tensor.transpose(acc[b][:, q * n_rows:(q + 1) * n_rows], flat[:, f * P:(f + 1) * P],
                                    ident[0:n_rows, 0:n_rows]).then_inc(turned, 1)

        @block.vector
        def _(dve):
            for b in range(2):
                n = min(per_bank, n_cols - b * per_bank)
                dve.wait_ge(turned, b * per_bank + n)
                nc.vector.tensor_copy(features[:, b * per_bank:b * per_bank + n, :],
                                      acc[b][:, 0:n * n_rows].rearrange("p (f r) -> p f r", r=n_rows))


def phase_tail(nc, tail, ident, prompt_out, sample_out):
    n_rows, n_cols = 2 + 2 * SEQS, 2 * FC
    ctx = ExitStack()
    with ctx:
        flat = ctx.enter_context(nc.sbuf_tensor("tail_flat", [n_rows, 2 * FF], F32))
        acc = [ctx.enter_context(nc.psum_tensor(f"tail_acc{i}", [P, 512], F32)) for i in range(4)]
        sem = phase_semaphores(nc, ctx, "tail")
        turned, copied, stored = sem("turned"), sem("copied"), sem("stored")
        block = ctx.enter_context(nc.Block())

        @block.tensor
        def _(pe):
            for g in range(n_cols // 4):
                if g >= 4:
                    pe.wait_ge(copied, g - 3)
                for q in range(4):
                    last = nc.tensor.transpose(acc[g % 4][0:n_rows, q * P:(q + 1) * P], tail[:, 4 * g + q, :],
                                               ident[:, :])
                last.then_inc(turned, 1)

        @block.vector
        def _(dve):
            for g in range(n_cols // 4):
                dve.wait_ge(turned, g + 1)
                nc.vector.tensor_copy(flat[:, g * 512:(g + 1) * 512], acc[g % 4][0:n_rows, :]).then_inc(copied, 1)

        @block.sync
        def _(sp):
            sp.wait_ge(copied, n_cols // 4)
            sp.dma_start(prompt_out, flat[0:2, :]).then_inc(stored, 16)
            sp.dma_start(sample_out, flat[2:n_rows, :]).then_inc(stored, 16)
            sp.wait_ge(stored, 32)


def phase_ple(nc, x, p_tiles, w_gate, gate_gain, w_ple, gain, y_tiles, ident, consts):
    ctx = ExitStack()
    with ctx:
        sb = lambda n, s, d=F32: ctx.enter_context(nc.sbuf_tensor(f"ple_{n}", s, d))
        sem = phase_semaphores(nc, ctx, "ple")
        bank = lambda n: ctx.enter_context(nc.psum_tensor(f"ple_{n}_acc", [P, 512], F32))
        two = lambda n, s, d=F32: [sb(f"{n}{i}", s, d) for i in range(2)]
        K2 = KC + PC
        wraw = two("wraw", [P, D])
        wh, wl = sb("wh", [P, K2, D], F32R), sb("wl", [P, K2, D], F32R)
        xt, pt, xn = two("x", [P, D]), two("p", [P, PLE]), two("xn", [P, D])
        junk = two("junk", [P, D])
        sh, sl = two("sh", [P, K2, P], F32R), two("sl", [P, K2, P], F32R)
        gate, e, y = two("gate", [P, D]), two("e", [P, D]), two("y", [P, D])
        gain_rows = sb("gain_rows", [P, D])
        total, mean, rstd = sb("total", [P, 2]), sb("mean", [P, 2]), sb("rstd", [P, 2])
        total2, mean2, rstd2 = sb("total2", [P, 2]), sb("mean2", [P, 2]), sb("rstd2", [P, 2])
        turn_acc = [bank("turn0"), bank("turn1"), bank("turn2")]
        gate_acc, ple_acc = [bank("gate0"), bank("gate1")], [bank("ple0"), bank("ple1")]
        wraw_in, x_in, p_in = [sem("wraw_in0"), sem("wraw_in1")], [sem("x_in0"), sem("x_in1")], [sem("p_in0"), sem("p_in1")]
        gain_in = sem("gain_in")
        whigh, wready = sem("whigh"), sem("wready")
        summed, powers, scaled = sem("summed"), sem("powers"), sem("scaled")
        turned, high, split = sem("turned"), sem("high"), sem("split")
        gates, ples = sem("gates"), sem("ples")
        opened, gated = sem("opened"), sem("gated")
        squared, powers2, finished, added = sem("squared"), sem("powers2"), sem("finished"), sem("added")
        stored = [sem("stored0"), sem("stored1")]
        block = ctx.enter_context(nc.Block())
        sizes = (4, 4, PC)
        starts = (0, 4, 8)

        @block.sync
        def _(sp):
            def load_w(k):
                if k >= 2:
                    sp.wait_ge(wready, k - 1)
                src = w_gate[k * P:(k + 1) * P, :] if k < KC else w_ple[(k - KC) * P:(k - KC + 1) * P, :]
                sp.dma_start(wraw[k % 2][:, :], src).then_inc(wraw_in[k % 2], 16)

            def load(t, s):
                if not known(t) or t >= 2:
                    sp.wait_ge(added, t - 1)
                    sp.wait_ge(turned, t * 3 - 3)
                sp.dma_start(xt[s][:, :], x[tokens_of(t), :]).then_inc(x_in[s], 16)
                for rows, src in p_tiles(t):
                    sp.dma_start(pt[s][rows, :], src).then_inc(p_in[s], 16)

            def step(t, s, i):
                if not known(t) or t < NT:
                    load(t + 1, 1 - s)
                sp.wait_ge(added, t + 1)
                sp.dma_start(y_tiles(t), y[s][bank_rows(t), :]).then_inc(stored[s], 16)

            sp.dma_start(gain_rows[:, :], gain.partition_broadcast(P)).then_inc(gain_in, 16)
            load(0, 0)
            for k in range(K2):
                load_w(k)
            walk(sp, step)
            sp.wait_ge(stored[0], 16 * (NT // 2 + 1))
            sp.wait_ge(stored[1], 16 * (NT // 2))

        @block.scalar
        def _(act):
            def squares(t, s, i):
                act.wait_ge(x_in[s], i * 16 + 16)
                if not known(t) or t >= 2:
                    act.wait_ge(powers, t * 2 - 2)
                nc.scalar.activation(junk[s][:, :], xt[s][:, :], ACT.Square, scale=D ** -0.5,
                                     accum_out=total[:, s:s + 1]).then_inc(summed, 1)

            def rounds(t, s, i):
                for g in range(3):
                    act.wait_ge(turned, t * 3 + (g + 1))
                    if g == 0 and (not known(t) or t >= 2):
                        act.wait_ge(ples, t * 2 - 2)
                    n = sizes[g]
                    nc.scalar.activation(sh[s][:, starts[g]:starts[g] + n, :],
                                         turn_acc[g][:, 0:n * P].rearrange("p (k t) -> p k t", k=n),
                                         ACT.Copy).then_inc(high, 1)

            def step(t, s, i):
                if not known(t) or t < NT:
                    squares(t + 1, 1 - s, i + s)
                for h in range(2):
                    act.wait_ge(gates, t * 2 + (h + 1))
                    if not known(t) or t >= 2:
                        act.wait_ge(gated, (t - 1) * 2)
                    nc.scalar.activation(gate[s][:, 512 * h:512 * h + 512], gate_acc[h][:, :], ACT.Sigmoid)\
                        .then_inc(opened, 1)
                if not known(t) or t < NT:
                    rounds(t + 1, 1 - s, i + s)
                act.wait_ge(gated, t * 2 + 2)
                if not known(t) or t >= 2:
                    act.wait_ge(powers2, t * 2 - 2)
                nc.scalar.activation(junk[s][:, :], e[s][:, :], ACT.Square, scale=D ** -0.5,
                                     accum_out=total2[:, s:s + 1]).then_inc(squared, 1)

            squares(0, 0, 0)
            for k in range(K2):
                act.wait_ge(wraw_in[k % 2], 16 * (k // 2 + 1))
                scale = gate_gain[:, k:k + 1] if k < KC else 1.0
                nc.scalar.activation(wh[:, k, :], wraw[k % 2][:, :], ACT.Copy, scale=scale).then_inc(whigh, 1)
            rounds(0, 0, 0)
            walk(act, step)

        @block.gpsimd
        def _(pool):
            def inner(t, s):
                pool.wait_ge(summed, t + 1)
                if not known(t) or t >= 2:
                    pool.wait_ge(scaled, t - 1)
                rstd_ops(nc, pool, rstd[:, s:s + 1], [total[:, s:s + 1]], mean[:, s:s + 1], consts, powers, t * 2)

            def step(t, s, i):
                if not known(t) or t < NT:
                    inner(t + 1, 1 - s)
                pool.wait_ge(squared, t + 1)
                if not known(t) or t >= 2:
                    pool.wait_ge(finished, t - 1)
                rstd_ops(nc, pool, rstd2[:, s:s + 1], [total2[:, s:s + 1]], mean2[:, s:s + 1], consts, powers2,
                         t * 2)
                pool.wait_ge(finished, t + 1)
                nc.gpsimd.tensor_tensor(y[s][:, :], y[s][:, :], xt[s][:, :], ALU.add).then_inc(added, 1)
            inner(0, 0)
            walk(pool, step)

        @block.vector
        def _(dve):
            def scale(t, s):
                dve.wait_ge(powers, t * 2 + 2)
                if not known(t) or t >= 2:
                    dve.wait_ge(turned, t * 3 - 3)
                nc.vector.tensor_scalar(xn[s][:, :], xt[s][:, :], rstd[:, s:s + 1], None, ALU.mult)\
                    .then_inc(scaled, 1)

            def splits(t, s):
                for g in range(3):
                    dve.wait_ge(high, t * 3 + (g + 1))
                    n = sizes[g]
                    here = (slice(None), slice(starts[g], starts[g] + n), slice(None))
                    nc.vector.tensor_tensor(sl[s][here], turn_acc[g][:, 0:n * P].rearrange("p (k t) -> p k t", k=n),
                                            sh[s][here].bitcast(F32), ALU.subtract).then_inc(split, 1)

            def step(t, s, i):
                if not known(t) or t < NT:
                    scale(t + 1, 1 - s)
                    splits(t + 1, 1 - s)
                for h in range(2):
                    dve.wait_ge(ples, t * 2 + (h + 1))
                    dve.wait_ge(opened, t * 2 + (h + 1))
                    if not known(t) or t >= 2:
                        dve.wait_ge(finished, t - 1)
                    nc.vector.tensor_tensor(e[s][:, 512 * h:512 * h + 512], ple_acc[h][:, :],
                                            gate[s][:, 512 * h:512 * h + 512], ALU.mult).then_inc(gated, 1)
                dve.wait_ge(powers2, t * 2 + 2)
                if not known(t) or t >= 2:
                    dve.wait_ge(stored[s], i * 16)
                nc.vector.scalar_tensor_tensor(out=y[s][:, :], in0=e[s][:, :], scalar=rstd2[:, s:s + 1],
                                               in1=gain_rows[:, :], op0=ALU.mult, op1=ALU.mult).then_inc(finished, 1)

            scale(0, 0)
            for k in range(K2):
                dve.wait_ge(whigh, k + 1)
                if k < KC:
                    nc.vector.scalar_tensor_tensor(out=wl[:, k, :], in0=wraw[k % 2][:, :], scalar=gate_gain[:, k:k + 1],
                                                   in1=wh[:, k, :].bitcast(F32), op0=ALU.mult, op1=ALU.subtract)\
                        .then_inc(wready, 1)
                else:
                    nc.vector.tensor_tensor(wl[:, k, :], wraw[k % 2][:, :], wh[:, k, :].bitcast(F32), ALU.subtract)\
                        .then_inc(wready, 1)
            splits(0, 0)
            dve.wait_ge(gain_in, 16)
            walk(dve, step)

        @block.tensor
        def _(pe):
            def turns(t, s, i):
                pe.wait_ge(scaled, t + 1)
                pe.wait_ge(p_in[s], i * 16 + 16)
                if known(t) and t == NT:
                    pe.wait_ge(p_in[s], i * 16 + 32)
                if not known(t) or t >= 1:
                    pe.wait_ge(split, t * 3)
                for g in range(3):
                    for k in range(sizes[g]):
                        src = xn[s][:, (starts[g] + k) * P:(starts[g] + k + 1) * P] if g < 2 else \
                            pt[s][:, k * P:(k + 1) * P]
                        last = nc.tensor.transpose(turn_acc[g][:, k * P:(k + 1) * P], src, ident[:, :])
                    last.then_inc(turned, 1)

            def products(t, s, acc, chunks, h, done):
                for k in chunks:
                    if known(t) and t == 0 and h == 0:
                        pe.wait_ge(wready, k + 1)
                    for p, (a, w) in enumerate(((sh, wh), (sh, wl), (sl, wh))):
                        last = nc.tensor.matmul(acc[h][:, :], a[s][:, k, :], w[:, k, 512 * h:512 * h + 512],
                                                start=(k == chunks[0] and p == 0), stop=(k == chunks[-1] and p == 2))
                last.then_inc(done, 1)

            def step(t, s, i):
                pe.wait_ge(split, t * 3 + 3)
                for h in range(2):
                    if not known(t) or t >= 1:
                        pe.wait_ge(opened, t * 2)
                    products(t, s, gate_acc, range(KC), h, gates)
                if not known(t) or t < NT:
                    turns(t + 1, 1 - s, i + s)
                for h in range(2):
                    if not known(t) or t >= 1:
                        pe.wait_ge(gated, t * 2)
                    products(t, s, ple_acc, range(KC, K2), h, ples)
            turns(0, 0, 0)
            walk(pe, step)


class MixerConsts:

    def __init__(self, nc, ctx):
        sb = lambda n, s: ctx.enter_context(nc.sbuf_tensor(f"mc_{n}", s, F32))
        self.average = sb("average", [P, P])
        self.gate_w = sb("gate_w", [RANK, H * DK])
        self.gate_b = sb("gate_b", [P, 2])
        self.gain_out = sb("gain_out", [P, 1])
        self.ln_gain, self.ln_bias = sb("ln_gain", [P, HS * P]), sb("ln_bias", [P, HS * P])
        self.spatial_raw = sb("spatial_raw", [P, HS, P])
        self.spatial = sb("spatial", [P, HS, P])
        self.spatial_b = sb("spatial_b", [P, HS, P])
        self.reset = sb("reset", [P, 2 * P])
        self.causal = sb("causal", [P, C])
        self.spatial_s = sb("spatial_s", [TS, HS, TS])
        self.spatial_b_s = sb("spatial_b_s", [P, HS, TS])
        self.reset_s = sb("reset_s", [P, 2 * TS])
        self.causal_s = sb("causal_s", [P, TS])
        self.own_seq = sb("own_seq", [P, SEQS])


def phase_mixer_consts(nc, a, m, ident):
    ctx = ExitStack()
    with ctx:
        sem = phase_semaphores(nc, ctx, "mc")
        acc = ctx.enter_context(nc.psum_tensor("mc_acc", [P, 512], F32))
        loaded, spatial_in, turned, copied, cut, zeroed = (sem(n) for n in (
            "loaded", "spatial_in", "turned", "copied", "cut", "zeroed"))
        base_in, diag_in, filled = sem("base_in"), sem("diag_in"), sem("filled")
        block = ctx.enter_context(nc.Block())
        b_spatial = a["b_spatial"][0]

        @block.sync
        def _(sp):
            sp.dma_start(m.spatial_raw[:, :, :], a["w_spatial"][0].rearrange("h t s -> t h s")).then_inc(spatial_in, 16)
            n = 0
            with nc.allow_non_contiguous_dma(reason="a few hundred values, features on partitions"):
                for out, src in ((m.gate_w[:, :], a["w_gla_gate"][0]),
                                 (m.gate_b[:, :], a["b_gla_gate"][0].rearrange("(c p) -> p c", p=P)),
                                 (m.gain_out[:, :], a["g_gla_out"][0].rearrange("(p c) -> p c", c=1)),
                                 (m.ln_gain[:, :], a["g_sgu_ln"][0].partition_broadcast(P)),
                                 (m.ln_bias[:, :], a["b_sgu_ln"][0].partition_broadcast(P)),
                                 (m.spatial_b[:, :, :], b_spatial.partition_broadcast(P))):
                    sp.dma_start(out, src).then_inc(loaded, 16)
                    n += 1
            sp.wait_ge(loaded, 16 * n)
            sp.wait_ge(cut, 1)
            sp.wait_ge(zeroed, 1)
            for q in range(SEQS):
                sp.dma_start(m.spatial_s[SL * q:SL * q + SL, :, SL * q:SL * q + SL], m.spatial[0:SL, :, 0:SL])\
                    .then_inc(diag_in, 16)
            sp.wait_ge(diag_in, 16 * SEQS)

        @block.tensor
        def _(pe):
            pe.wait_ge(spatial_in, 16)
            for h in range(HS):
                last = nc.tensor.transpose(acc[:, h * P:(h + 1) * P], m.spatial_raw[:, h, :], ident[:, :])
            last.then_inc(turned, 1)

        @block.vector
        def _(dve):
            dve.wait_ge(turned, 1)
            nc.vector.tensor_copy(m.spatial[:, :, :], acc[:, :].rearrange("p (h t) -> p h t", h=HS)).then_inc(copied, 1)
            nc.vector.memset(m.average[:, :], 1.0 / DV)
            nc.vector.memset(m.reset[:, :], 1.0)
            nc.vector.memset(m.reset_s[:, :], 1.0).then_inc(filled, 1)
            dve.wait_ge(filled, 1)
            nc.vector.memset(m.reset[:, :].rearrange("p (a c) -> p a c", c=C)[:, :, 0:1], 0.0)
            nc.vector.memset(m.reset_s[:, :].rearrange("p (a c) -> p a c", c=SL)[:, :, 0:1], 0.0)
            dve.wait_ge(loaded, 16 * 6)
            nc.vector.tensor_copy(m.spatial_b_s[:, :, :].rearrange("p h (q c) -> p h q c", c=SL),
                                  m.spatial_b[:, :, 0:SL].unsqueeze(2).to_broadcast([P, HS, SEQS, SL]))

        @block.gpsimd
        def _(pool):
            nc.gpsimd.memset(m.spatial_s[:, :, :], 0.0).then_inc(zeroed, 1)
            for x in (m.causal, m.causal_s, m.own_seq):
                nc.gpsimd.memset(x[:, :], 1.0).then_inc(base_in, 1)
            pool.wait_ge(base_in, 3)
            n = 3

            def keep(x, pattern, base, channel):
                nonlocal n
                nc.gpsimd.affine_select(out=x, in_=x, compare_op=ALU.is_ge, fill=0.0, base=base, pattern=pattern,
                                        channel_multiplier=channel).then_inc(base_in, 1)
                n += 1
                pool.wait_ge(base_in, n)

            for f in range(2):
                rows = slice(64 * f, 64 * f + 64)
                keep(m.causal[rows, :], [[1, C]], 0, -1)
                keep(m.causal_s[rows, :], [[1, TS]], 0, -1)
                keep(m.causal_s[rows, :], [[-SL, SEQS], [0, SL]], 0, 1)
                keep(m.own_seq[rows, :], [[-SL, SEQS]], 0, 1)
                keep(m.own_seq[rows, :], [[SL, SEQS]], SL - 1, -1)
            pool.wait_ge(copied, 1)
            nc.gpsimd.affine_select(out=m.spatial[:, :, :], in_=m.spatial[:, :, :], compare_op=ALU.is_ge, fill=0.0,
                                    base=0, pattern=[[0, HS], [1, P]], channel_multiplier=-1).then_inc(cut, 1)


def head_rows(f):
    return slice(64 * f, 64 * f + 64)


def phase_mixers(nc, m, pt_scratch, v_scratch, vs_scratch, mix, state_out, ident, consts):
    ctx = ExitStack()
    with ctx:
        sb = lambda n, s, d=F32: ctx.enter_context(nc.sbuf_tensor(f"gla_{n}", s, d))
        sem = phase_semaphores(nc, ctx, "gla")
        bank = lambda n: ctx.enter_context(nc.psum_tensor(f"gla_{n}_acc", [P, 512], F32))
        two = lambda n, s: [sb(f"{n}{i}", s) for i in range(2)]
        qk = two("qk", [P, 4, P])
        glr = two("glr", [RANK, P])
        vs = two("vs", [P, HS * P])
        v = two("v", [P, NCH, H * DV])
        ru = two("ru", [P, 2 * H, P])
        z, soft, logd = sb("z", [P, 2 * P]), sb("soft", [P, 2 * P]), sb("logd", [P, 2 * P])
        cum, from_mid, to_end = sb("cum", [P, 2 * P]), sb("from_mid", [P, 2 * P]), sb("to_end", [P, 2 * P])
        e_cum = two("e_cum", [P, 2 * P])
        e_q, e_k, e_end = sb("e_q", [P, 2 * P]), sb("e_k", [P, 2 * P]), sb("e_end", [P, 2 * P])
        q_state, q_in, k_in, k_end = (two(n, [P, 2, P]) for n in ("q_state", "q_in", "k_in", "k_end"))
        stats = sb("stats", [P, HS, 6])
        mv = sb("mv", [P, HS, 2])
        v_var, v_rstd = sb("v_var", [P, HS]), sb("v_rstd", [P, HS])
        vn = two("vn", [P, HS * P])
        scores = sb("scores", [P, NCH, 2, C])
        k_tok = sb("k_tok", [P, NCH, 2, DK])
        state = two("state", [P, 2, DV])
        square = sb("square", [P, 2, 2, P])
        inv = sb("inv", [P, 2, 2, P])
        normed = sb("normed", [P, 2, 2, P])
        mixed_b = sb("mixed_b", [P, HS, P])
        out = two("out", [P, 2 * H, P])
        z_acc, s_acc, t_acc, kv_acc = bank("z"), bank("s"), bank("t"), bank("kv")
        o_acc = [bank("o0"), bank("o1")]
        n_acc, m_acc = bank("n"), bank("m")

        a_in, b_in = [sem("a_in0"), sem("a_in1")], [sem("b_in0"), sem("b_in1")]
        logits = sem("logits")
        decays = sem("decays")
        softs = sem("softs")
        factors = sem("factors")
        queries, keys = sem("queries"), sem("keys")
        stat, v_power = sem("stat"), sem("v_power")
        v_normed, v_gained = sem("v_normed"), sem("v_gained")
        scored, masked = sem("scored"), sem("masked")
        k_turned, k_copied = sem("k_turned"), sem("k_copied")
        kv_made = sem("kv_made")
        states = sem("states")
        outputs = sem("outputs")
        squared, averaged, inverse = sem("squared"), sem("averaged"), sem("inverse")
        spatials = sem("spatials")
        gla_outs = sem("gla_outs")
        sgu_outs = sem("sgu_outs")
        zeroed = sem("zeroed")
        stored = [sem("stored0"), sem("stored1")]
        state_stored = sem("state_stored")
        block = ctx.enter_context(nc.Block())
        pt_view = pt_scratch.rearrange("(k p) t -> p k t", p=P)
        mix_view = mix.rearrange("(k p) t -> p k t", p=P)

        def walk_prompt(eng, step):
            step(0, 0, 0)
            step(1, 1, 0)
            with eng.Fori(1, NT // 2 - 1) as i:
                step(i * 2, 0, i)
                step(i * 2 + 1, 1, i)
            step(NT - 2, 0, NT // 2 - 1)
            step(NT - 1, 1, NT // 2 - 1)

        def more(t):
            return not known(t) or t + 1 < NT

        def old(t):
            return not known(t) or t >= 2

        def later(t):
            return not known(t) or t >= 1

        @block.sync
        def _(sp):
            def load_first(t, s):
                here = ds(t * P, P)
                if old(t):
                    sp.wait_ge(queries, t * 2 - 2)
                    sp.wait_ge(keys, t * 2 - 2)
                    sp.wait_ge(v_normed, t * 4 - 4)
                sp.dma_start(qk[s][:, :, :], pt_view[:, 0:4, here]).then_inc(a_in[s], 16)
                sp.dma_start(glr[s][:, :], pt_scratch[12 * P:12 * P + RANK, here]).then_inc(a_in[s], 16)
                sp.dma_start(vs[s][:, :], vs_scratch[here, :]).then_inc(a_in[s], 16)

            def load_second(t, s):
                here = ds(t * P, P)
                if old(t):
                    sp.wait_ge(outputs, t * 2 - 2)
                    sp.wait_ge(sgu_outs, t * 2 - 2)
                    sp.wait_ge(gla_outs, t * 4 - 4)
                for f in range(2):
                    sp.dma_start(v[s][head_rows(f), :, :], v_scratch[here, :].rearrange("(c p) n -> p c n", p=C))\
                        .then_inc(b_in[s], 16)
                sp.dma_start(ru[s][:, :, :], pt_view[:, 4:12, here]).then_inc(b_in[s], 16)

            def store(t, s):
                sp.wait_ge(sgu_outs, t * 2 + 2)
                sp.wait_ge(gla_outs, t * 4 + 4)
                sp.dma_start(mix_view[:, :, ds(t * P, P)], out[s][:, :, :]).then_inc(stored[s], 16)

            def step(t, s, i):
                if not known(t) or t + 2 < NT:
                    load_first(t + 2, s)
                if more(t):
                    load_second(t + 1, 1 - s)
                if later(t):
                    store(t - 1, 1 - s)
            load_first(0, 0)
            load_second(0, 0)
            load_first(1, 1)
            walk_prompt(sp, step)
            store(NT - 1, 1)
            sp.wait_ge(states, 4 * NT)
            for f in range(2):
                sp.dma_start(state_out.rearrange("(q f) d e -> f d q e", f=2)[f], state[0][head_rows(f), :, :])\
                    .then_inc(state_stored, 16)
            sp.wait_ge(state_stored, 32)
            for s in range(2):
                sp.wait_ge(stored[s], 16 * (NT // 2))

        @block.tensor
        def _(pe):
            def gate_logits(t, s, i):
                pe.wait_ge(a_in[s], i * 48 + 48)
                if later(t):
                    pe.wait_ge(decays, t * 5 - 4)
                for q in range(2):
                    last = nc.tensor.matmul(z_acc[:, q * P:(q + 1) * P], m.gate_w[:, q * P:(q + 1) * P], glr[s][:, :],
                                            start=True, stop=True)
                last.then_inc(logits, 1)

            def mean(t):
                pe.wait_ge(squared, t * 2 + 2)
                if later(t):
                    pe.wait_ge(inverse, t * 2 - 1)
                nc.tensor.matmul(n_acc[:, :], m.average[:, :], square[:, :, :, :].rearrange("p f q t -> p (f q t)"),
                                 start=True, stop=True).then_inc(averaged, 1)

            def step(t, s, i):
                pe.wait_ge(queries, t * 2 + 2)
                pe.wait_ge(keys, t * 2 + 2)
                if later(t):
                    pe.wait_ge(masked, t)
                    pe.wait_ge(k_copied, t)
                if more(t):
                    gate_logits(t + 1, 1 - s, i + s)
                for c in range(NCH):
                    cols = slice(c * C, c * C + C)
                    for q in range(2):
                        for f in range(2):
                            at = c * 2 + q
                            last = nc.tensor.matmul(s_acc[head_rows(f), at * C:(at + 1) * C],
                                                    k_in[s][head_rows(f), q, cols], q_in[s][head_rows(f), q, cols],
                                                    start=True, stop=True)
                last.then_inc(scored, 1)
                for c in range(NCH):
                    cols = slice(c * C, c * C + C)
                    for q in range(2):
                        for f in range(2):
                            at = c * 2 + q
                            last = nc.tensor.matmul(t_acc[head_rows(f), at * DK:(at + 1) * DK],
                                                    k_end[s][head_rows(f), q, cols],
                                                    ident[head_rows(f), 64 * f:64 * f + 64], start=True, stop=True)
                last.then_inc(k_turned, 1)
                if later(t):
                    mean(t - 1)
                pe.wait_ge(v_gained, t * 2 + 2)
                if later(t):
                    pe.wait_ge(sgu_outs, t * 2)
                for h in range(HS):
                    if h == HS // 2:
                        pe.wait_ge(b_in[s], i * 48 + 48)
                        pe.wait_ge(k_copied, t + 1)
                        if later(t):
                            pe.wait_ge(states, t * 4)
                    last = nc.tensor.matmul(m_acc[:, h * P:(h + 1) * P], vn[s][:, h * P:(h + 1) * P],
                                            m.spatial[:, h, :], start=True, stop=True)
                last.then_inc(spatials, 1)
                for c in range(NCH):
                    for q in range(2):
                        for f in range(2):
                            at, h = c * 2 + q, 2 * q + f
                            last = nc.tensor.matmul(kv_acc[head_rows(f), at * DV:(at + 1) * DV],
                                                    k_tok[head_rows(f), c, q, :],
                                                    v[s][head_rows(f), c, h * DV:(h + 1) * DV], start=True, stop=True)
                    last.then_inc(kv_made, 1)
                pe.wait_ge(masked, t + 1)
                if later(t):
                    pe.wait_ge(gla_outs, t * 4 - 2)
                for c in range(NCH):
                    if c > 0:
                        pe.wait_ge(states, t * 4 + 2)
                    cols = slice(c * C, c * C + C)
                    for q in range(2):
                        for f in range(2):
                            h = 2 * q + f
                            o = o_acc[f][:, q * P + c * C:q * P + (c + 1) * C]
                            nc.tensor.matmul(o, state[c][head_rows(f), q, :], q_state[s][head_rows(f), q, cols],
                                             start=True, stop=False)
                            last = nc.tensor.matmul(o, v[s][head_rows(f), c, h * DV:(h + 1) * DV],
                                                    scores[head_rows(f), c, q, :], start=False, stop=True)
                    last.then_inc(outputs, 1)
            pe.wait_ge(zeroed, 2)
            gate_logits(0, 0, 0)
            walk_prompt(pe, step)
            mean(NT - 1)

        @block.scalar
        def _(act):
            def soft_logs(t, s):
                act.wait_ge(decays, t * 5 + 1)
                nc.scalar.activation(soft[:, :], z[:, :], ACT.Abs).then_inc(softs, 1)
                act.wait_ge(softs, t * 3 + 1)
                nc.scalar.activation(soft[:, :], soft[:, :], ACT.Exp, scale=-1.0).then_inc(softs, 1)
                act.wait_ge(softs, t * 3 + 2)
                nc.scalar.activation(soft[:, :], soft[:, :], ACT.Ln, bias=1.0).then_inc(softs, 1)

            def exps(t, s):
                act.wait_ge(decays, t * 5 + 5)
                if old(t):
                    act.wait_ge(states, t * 4 - 4)
                if later(t):
                    act.wait_ge(queries, t * 2)
                    act.wait_ge(keys, t * 2)
                for out_, in_, sign in ((e_k, from_mid, -1.0), (e_end, to_end, 1.0), (e_q, from_mid, 1.0),
                                        (e_cum[s], cum, 1.0)):
                    nc.scalar.activation(out_[:, :], in_[:, :], ACT.Exp, scale=sign / TAU).then_inc(factors, 1)

            def inverse_norm(t):
                act.wait_ge(averaged, t + 1)
                if later(t):
                    act.wait_ge(gla_outs, t * 4 - 2)
                flat = inv[:, :, :, :].rearrange("p f q t -> p (f q t)")
                nc.scalar.activation(flat, n_acc[:, :], ACT.Ln, bias=consts[:, 0:1]).then_inc(inverse, 1)
                act.wait_ge(inverse, t * 2 + 1)
                nc.scalar.activation(flat, flat, ACT.Exp, scale=-0.5).then_inc(inverse, 1)

            def step(t, s, i):
                if more(t):
                    soft_logs(t + 1, 1 - s)
                act.wait_ge(k_turned, t + 1)
                if later(t):
                    act.wait_ge(kv_made, t * 2)
                nc.scalar.activation(k_tok[:, :, :, :].rearrange("p c q d -> p (c q d)"), t_acc[:, 0:NCH * 2 * DK],
                                     ACT.Copy).then_inc(k_copied, 1)
                if later(t):
                    inverse_norm(t - 1)
                if more(t):
                    exps(t + 1, 1 - s)
                act.wait_ge(outputs, t * 2 + 2)
                if later(t):
                    act.wait_ge(averaged, t)
                for f in range(2):
                    nc.scalar.activation(square[:, f].rearrange("p q t -> p (q t)"), o_acc[f][:, 0:2 * P],
                                         ACT.Square).then_inc(squared, 1)
            act.preload_act_table_set("natural_log_exp_and_others")
            soft_logs(0, 0)
            exps(0, 0)
            walk_prompt(act, step)
            inverse_norm(NT - 1)

        @block.gpsimd
        def _(pool):
            def make_keys(t, s):
                if old(t):
                    pool.wait_ge(outputs, t * 2 - 2)
                for i, (out_, e) in enumerate(((k_in[s], e_k), (k_end[s], e_end))):
                    pool.wait_ge(factors, t * 4 + (i + 1))
                    nc.gpsimd.tensor_tensor(out_[:, :, :], qk[s][:, 2:4, :],
                                            e[:, :].rearrange("p (q t) -> p q t", q=2), ALU.mult).then_inc(keys, 1)

            def v_tail(t, s):
                pool.wait_ge(v_normed, t * 4 + 4)
                nc.gpsimd.tensor_tensor(vn[s][:, :], vn[s][:, :], m.ln_gain[:, :], ALU.mult).then_inc(v_gained, 1)
                pool.wait_ge(v_gained, t * 2 + 1)
                nc.gpsimd.tensor_tensor(vn[s][:, :], vn[s][:, :], m.ln_bias[:, :], ALU.add).then_inc(v_gained, 1)

            def v_scale(t):
                pool.wait_ge(stat, t * 8 + 8)
                nc.gpsimd.tensor_tensor(v_var[:, :], mv[:, :, 1:2].rearrange("p h a -> p (h a)"),
                                        consts[:, 0:1].to_broadcast([P, HS]), ALU.add).then_inc(v_power, 1)
                pool.wait_ge(v_power, t * 2 + 1)
                nc.gpsimd.tensor_tensor(v_rstd[:, :], v_var[:, :], consts[:, 1:2].to_broadcast([P, HS]), ALU.pow)\
                    .then_inc(v_power, 1)

            def first(t, s):
                v_scale(t)
                make_keys(t, s)
                v_tail(t, s)
            first(0, 0)
            walk_prompt(pool, lambda t, s, i: first(t + 1, 1 - s) if more(t) else None)

        @block.vector
        def _(dve):
            def z_out(t, s):
                dve.wait_ge(logits, t + 1)
                nc.vector.tensor_tensor(z[:, :].rearrange("p (q t) -> p q t", q=2),
                                        z_acc[:, 0:2 * P].rearrange("p (q t) -> p q t", q=2),
                                        bcast(m.gate_b[:, :], P), ALU.add).then_inc(decays, 1)

            def chunks(x):
                return x[:, :].rearrange("p (a c) -> p a c", c=C)

            def log_decays(t, s):
                dve.wait_ge(stat, t * 8 + 4)
                dve.wait_ge(softs, t * 3 + 3)
                nc.vector.scalar_tensor_tensor(out=logd[:, :], in0=z[:, :], scalar=0.0, in1=soft[:, :],
                                               op0=ALU.min, op1=ALU.subtract).then_inc(decays, 1)
                for h in range(HS):
                    nc.vector.bn_aggr(mv[:, h, :], stats[:, h, :]).then_inc(stat, 1)
                dve.wait_ge(decays, t * 5 + 2)
                nc.vector.tensor_tensor_scan(out=cum[:, :], data0=m.reset[:, :], data1=logd[:, :], initial=0.0,
                                             op0=ALU.mult, op1=ALU.add).then_inc(decays, 1)
                dve.wait_ge(decays, t * 5 + 3)
                c = chunks(cum)
                nc.vector.tensor_tensor(chunks(from_mid), c, c[:, :, C // 2 - 1:C // 2].to_broadcast([P, 2 * NCH, C]),
                                        ALU.subtract).then_inc(decays, 1)
                nc.vector.tensor_tensor(chunks(to_end), c[:, :, C - 1:C].to_broadcast([P, 2 * NCH, C]), c,
                                        ALU.subtract).then_inc(decays, 1)

            def make_queries(t, s):
                if old(t):
                    dve.wait_ge(outputs, t * 2 - 2)
                for i, (out_, e) in enumerate(((q_in[s], e_q), (q_state[s], e_cum[s]))):
                    dve.wait_ge(factors, t * 4 + (i + 3))
                    nc.vector.scalar_tensor_tensor(out=out_[:, :, :].rearrange("p q t -> p (q t)"),
                                                   in0=qk[s][:, 0:2, :].rearrange("p q t -> p (q t)"),
                                                   scalar=DK ** -0.5, in1=e[:, :], op0=ALU.mult, op1=ALU.mult)\
                        .then_inc(queries, 1)

            def v_stats(t, s, i):
                dve.wait_ge(a_in[s], i * 48 + 48)
                if later(t):
                    dve.wait_ge(v_normed, t * 4)
                for h in range(HS):
                    nc.vector.bn_stats(stats[:, h, :], vs[s][:, h * P:(h + 1) * P]).then_inc(stat, 1)

            def v_norm(t, s):
                dve.wait_ge(v_power, t * 2 + 2)
                if old(t):
                    dve.wait_ge(spatials, t - 1)
                for h in range(HS):
                    nc.vector.tensor_scalar(vn[s][:, h * P:(h + 1) * P], vs[s][:, h * P:(h + 1) * P],
                                            mv[:, h, 0:1], v_rstd[:, h:h + 1], ALU.subtract, ALU.mult)\
                        .then_inc(v_normed, 1)

            def mask(t):
                nc.vector.copy_predicated(scores[:, :, :, :].rearrange("p c q i -> p (c q) i"),
                                          m.causal[:, :].bitcast(I32).unsqueeze(1).to_broadcast([P, 2 * NCH, C]),
                                          s_acc[:, 0:2 * NCH * C].rearrange("p (a i) -> p a i", i=C))\
                    .then_inc(masked, 1)

            def advance(t, s, c):
                dve.wait_ge(kv_made, t * 2 + 2)
                if c == 1:
                    dve.wait_ge(outputs, t * 2 + 1)
                elif later(t):
                    dve.wait_ge(outputs, t * 2)
                    dve.wait_ge(states, t * 4)
                if c == 1:
                    dve.wait_ge(states, t * 4 + 2)
                decay = e_cum[s][:, :].rearrange("p (q t) -> p q t", q=2)[:, :, (c + 1) * C - 1:(c + 1) * C]
                nc.vector.tensor_tensor(state[1 - c][:, :, :], state[c][:, :, :], decay.to_broadcast([P, 2, DV]),
                                        ALU.mult).then_inc(states, 1)
                dve.wait_ge(states, t * 4 + (2 * c + 1))
                nc.vector.tensor_tensor(state[1 - c][:, :, :], state[1 - c][:, :, :],
                                        kv_acc[:, c * 2 * DV:(c + 1) * 2 * DV].rearrange("p (q e) -> p q e", q=2),
                                        ALU.add).then_inc(states, 1)

            def finish_gla(t, s):
                dve.wait_ge(inverse, t * 2 + 2)
                for f in range(2):
                    nc.vector.tensor_tensor(normed[:, f], o_acc[f][:, 0:2 * P].rearrange("p (q t) -> p q t", q=2),
                                            inv[:, f], ALU.mult).then_inc(gla_outs, 1)
                for f in range(2):
                    dve.wait_ge(gla_outs, t * 4 + (f + 1))
                    heads = lambda x: x[s][:, 0:H, :].rearrange("p (q f) t -> p f q t", f=2)[:, f]
                    nc.vector.scalar_tensor_tensor(out=heads(out), in0=normed[:, f], scalar=m.gain_out[:, 0:1],
                                                   in1=heads(ru), op0=ALU.mult, op1=ALU.mult).then_inc(gla_outs, 1)

            def finish_sgu(t, s, i):
                if old(t):
                    dve.wait_ge(stored[s], i * 16)
                dve.wait_ge(spatials, t + 1)
                nc.vector.tensor_tensor(mixed_b[:, :, :], m_acc[:, :].rearrange("p (h t) -> p h t", h=HS),
                                        m.spatial_b[:, :, :], ALU.add).then_inc(sgu_outs, 1)
                dve.wait_ge(sgu_outs, t * 2 + 1)
                nc.vector.tensor_tensor(out[s][:, H:2 * H, :], mixed_b[:, :, :], ru[s][:, H:2 * H, :], ALU.mult)\
                    .then_inc(sgu_outs, 1)

            def step(t, s, i):
                dve.wait_ge(scored, t + 1)
                if later(t):
                    dve.wait_ge(outputs, t * 2)
                if more(t):
                    z_out(t + 1, 1 - s)
                mask(t)
                if more(t):
                    v_stats(t + 1, 1 - s, i + s)
                    log_decays(t + 1, 1 - s)
                if later(t):
                    finish_gla(t - 1, 1 - s)
                if more(t):
                    make_queries(t + 1, 1 - s)
                advance(t, s, 0)
                finish_sgu(t, s, i)
                advance(t, s, 1)
                if more(t):
                    v_norm(t + 1, 1 - s)

            nc.vector.memset(scores[:, :, :, :], 0.0).then_inc(zeroed, 1)
            nc.vector.memset(state[0][:, :, :], 0.0).then_inc(zeroed, 1)
            dve.wait_ge(zeroed, 2)
            z_out(0, 0)
            v_stats(0, 0, 0)
            log_decays(0, 0)
            v_norm(0, 0)
            make_queries(0, 0)
            walk_prompt(dve, step)
            finish_gla(NT - 1, 1)


def phase_mixers_sample(nc, m, pt_scratch, v_scratch, vs_scratch, mix, state_in, state_out, vn_out, ident, consts):
    ctx = ExitStack()
    with ctx:
        sb = lambda n, s, d=F32: ctx.enter_context(nc.sbuf_tensor(f"sm_{n}", s, d))
        sem = phase_semaphores(nc, ctx, "sm")
        bank = lambda n: ctx.enter_context(nc.psum_tensor(f"sm_{n}_acc", [P, 512], F32))
        W = 2 * TS
        qk, ru = sb("qk", [P, 4, TS]), sb("ru", [P, 2 * H, TS])
        glr = sb("glr", [RANK, TS])
        vs = sb("vs", [TS, HS * P])
        v = sb("v", [P, H * DV])
        state = sb("state", [P, SEQS, 2, DV])
        new_state = sb("new_state", [P, SEQS, 2, DV])
        z, soft, logd, cum = sb("z", [P, W]), sb("soft", [P, W]), sb("logd", [P, W]), sb("cum", [P, W])
        from_mid, to_end = sb("from_mid", [P, W]), sb("to_end", [P, W])
        e_cum, e_q, e_k, e_end = sb("e_cum", [P, W]), sb("e_q", [P, W]), sb("e_k", [P, W]), sb("e_end", [P, W])
        q_state, q_in, k_in, k_end = (sb(n, [P, 2, TS]) for n in ("q_state", "q_in", "k_in", "k_end"))
        stats, mv = sb("stats", [TS, HS, 6]), sb("mv", [TS, HS, 2])
        v_var, v_rstd = sb("v_var", [TS, HS]), sb("v_rstd", [TS, HS])
        vn = sb("vn", [TS, HS * P])
        scores = sb("scores", [P, 2, TS])
        k_tok = sb("k_tok", [P, 2, DK])
        k_seq = sb("k_seq", [P, 2, SEQS, DK])
        square, inv, normed = (sb(n, [P, 2, 2, TS]) for n in ("square", "inv", "normed"))
        mixed_b, out = sb("mixed_b", [P, HS, TS]), sb("out", [P, 2 * H, TS])
        kv_acc = [bank(f"kv{i}") for i in range(SEQS // 2)]
        z_acc, s_acc, t_acc, m_acc = kv_acc
        o_acc, n_acc = [bank("o0"), bank("o1")], bank("n")
        (loaded, zeroed, logits, decays, softs, factors, queries, keys, stat, v_power, v_normed, v_gained, scored,
         masked, k_turned, k_copied, k_split, kv_made, states, outputs, squared, averaged, inverse, spatials, outs,
         stored) = (sem(n) for n in (
             "loaded", "zeroed", "logits", "decays", "softs", "factors", "queries", "keys", "stat", "v_power",
             "v_normed", "v_gained", "scored", "masked", "k_turned", "k_copied", "k_split", "kv_made", "states",
             "outputs", "squared", "averaged", "inverse", "spatials", "outs", "stored"))
        state_in_sem = sem("state_in")
        block = ctx.enter_context(nc.Block())
        pt_view = pt_scratch.rearrange("(k p) t -> p k t", p=P)
        tokens = slice(TP, T)
        by_half = lambda x: x.rearrange("b (q f) d e -> f d b q e", f=2)
        LOADS = 6

        def tok_rows(f):
            return slice(64 * f, 64 * f + TS)

        @block.sync
        def _(sp):
            sp.dma_start(qk[:, :, :], pt_view[:, 0:4, tokens]).then_inc(loaded, 16)
            sp.dma_start(glr[:, :], pt_scratch[12 * P:12 * P + RANK, tokens]).then_inc(loaded, 16)
            sp.dma_start(vs[:, :], vs_scratch[tokens, :]).then_inc(loaded, 16)
            sp.dma_start(ru[:, :, :], pt_view[:, 4:12, tokens]).then_inc(loaded, 16)
            sp.wait_ge(zeroed, 1)
            for f in range(2):
                sp.dma_start(v[tok_rows(f), :], v_scratch[tokens, :]).then_inc(loaded, 16)
            for f in range(2):
                for b in range(SEQS):
                    sp.dma_start(state[head_rows(f), b, :, :], by_half(state_in)[f][:, b]).then_inc(state_in_sem, 16)
            sp.wait_ge(v_gained, 2)
            sp.dma_start(vn_out, vn[:, :]).then_inc(stored, 16)
            sp.wait_ge(states, 1 + SEQS // 2)
            for f in range(2):
                for b in range(SEQS):
                    sp.dma_start(by_half(state_out)[f][:, b], new_state[head_rows(f), b, :, :]).then_inc(stored, 16)
            sp.wait_ge(outs, 6)
            sp.dma_start(mix.rearrange("(k p) t -> p k t", p=P)[:, :, tokens], out[:, :, :]).then_inc(stored, 16)
            sp.wait_ge(stored, 16 * (2 + 2 * SEQS))

        @block.tensor
        def _(pe):
            pe.wait_ge(loaded, 16 * LOADS)
            for q in range(2):
                last = nc.tensor.matmul(z_acc[:, q * TS:(q + 1) * TS], m.gate_w[:, q * P:(q + 1) * P], glr[:, :],
                                        start=True, stop=True)
            last.then_inc(logits, 1)
            pe.wait_ge(queries, 2)
            pe.wait_ge(keys, 2)
            for q in range(2):
                for f in range(2):
                    last = nc.tensor.matmul(s_acc[tok_rows(f), q * TS:(q + 1) * TS], k_in[head_rows(f), q, :],
                                            q_in[head_rows(f), q, :], start=True, stop=True)
            last.then_inc(scored, 1)
            for q in range(2):
                for f in range(2):
                    last = nc.tensor.matmul(t_acc[tok_rows(f), q * DK:(q + 1) * DK], k_end[head_rows(f), q, :],
                                            ident[head_rows(f), 64 * f:64 * f + 64], start=True, stop=True)
            last.then_inc(k_turned, 1)
            pe.wait_ge(v_gained, 2)
            for h in range(HS):
                last = nc.tensor.matmul(m_acc[:, h * TS:(h + 1) * TS], vn[:, h * P:(h + 1) * P],
                                        m.spatial_s[:, h, :], start=True, stop=True)
            last.then_inc(spatials, 1)
            pe.wait_ge(masked, 2)
            pe.wait_ge(state_in_sem, 16 * 2 * SEQS)
            for q in range(2):
                for f in range(2):
                    h = 2 * q + f
                    nc.tensor.matmul(o_acc[f][:, q * TS:(q + 1) * TS], v[head_rows(f), h * DV:(h + 1) * DV],
                                     scores[head_rows(f), q, :], start=True, stop=False)
                    for b in range(SEQS):
                        cols = slice(b * SL, (b + 1) * SL)
                        last = nc.tensor.matmul(o_acc[f][:, q * TS + b * SL:q * TS + (b + 1) * SL],
                                                state[head_rows(f), b, q, :], q_state[head_rows(f), q, cols],
                                                start=False, stop=(b == SEQS - 1))
            last.then_inc(outputs, 1)
            pe.wait_ge(k_split, 2)
            pe.wait_ge(outs, 1)
            for b in range(SEQS):
                for q in range(2):
                    for f in range(2):
                        h, at = 2 * q + f, (b % 2) * 2 + q
                        last = nc.tensor.matmul(kv_acc[b // 2][head_rows(f), at * DV:(at + 1) * DV],
                                                k_seq[tok_rows(f), q, b, :], v[tok_rows(f), h * DV:(h + 1) * DV],
                                                start=True, stop=True)
            last.then_inc(kv_made, 1)
            pe.wait_ge(squared, 2)
            nc.tensor.matmul(n_acc[:, 0:4 * TS], m.average[:, :], square[:, :, :, :].rearrange("p f q t -> p (f q t)"),
                             start=True, stop=True).then_inc(averaged, 1)

        @block.scalar
        def _(act):
            act.preload_act_table_set("natural_log_exp_and_others")
            act.wait_ge(decays, 1)
            nc.scalar.activation(soft[:, :], z[:, :], ACT.Abs).then_inc(softs, 1)
            act.wait_ge(softs, 1)
            nc.scalar.activation(soft[:, :], soft[:, :], ACT.Exp, scale=-1.0).then_inc(softs, 1)
            act.wait_ge(softs, 2)
            nc.scalar.activation(soft[:, :], soft[:, :], ACT.Ln, bias=1.0).then_inc(softs, 1)
            act.wait_ge(decays, 5)
            for out_, in_, sign in ((e_k, from_mid, -1.0), (e_end, to_end, 1.0), (e_q, from_mid, 1.0),
                                    (e_cum, cum, 1.0)):
                nc.scalar.activation(out_[:, :], in_[:, :], ACT.Exp, scale=sign / TAU).then_inc(factors, 1)
            act.wait_ge(k_turned, 1)
            for f in range(2):
                nc.scalar.activation(k_tok[tok_rows(f), :, :].rearrange("p q d -> p (q d)"),
                                     t_acc[tok_rows(f), 0:2 * DK], ACT.Copy).then_inc(k_copied, 1)
            act.wait_ge(outputs, 1)
            for f in range(2):
                nc.scalar.activation(square[:, f].rearrange("p q t -> p (q t)"), o_acc[f][:, 0:2 * TS],
                                     ACT.Square).then_inc(squared, 1)
            act.wait_ge(averaged, 1)
            flat = inv[:, :, :, :].rearrange("p f q t -> p (f q t)")
            nc.scalar.activation(flat, n_acc[:, 0:4 * TS], ACT.Ln, bias=consts[:, 0:1]).then_inc(inverse, 1)
            act.wait_ge(inverse, 1)
            nc.scalar.activation(flat, flat, ACT.Exp, scale=-0.5).then_inc(inverse, 1)

        @block.gpsimd
        def _(pool):
            pool.wait_ge(stat, 2 * HS)
            nc.gpsimd.tensor_tensor(v_var[:, :], mv[:, :, 1:2].rearrange("p h a -> p (h a)"),
                                    consts[0:TS, 0:1].to_broadcast([TS, HS]), ALU.add).then_inc(v_power, 1)
            pool.wait_ge(v_power, 1)
            nc.gpsimd.tensor_tensor(v_rstd[:, :], v_var[:, :], consts[0:TS, 1:2].to_broadcast([TS, HS]), ALU.pow)\
                .then_inc(v_power, 1)
            pool.wait_ge(v_normed, HS)
            nc.gpsimd.tensor_tensor(vn[:, :], vn[:, :], m.ln_gain[0:TS, :], ALU.mult).then_inc(v_gained, 1)
            pool.wait_ge(v_gained, 1)
            nc.gpsimd.tensor_tensor(vn[:, :], vn[:, :], m.ln_bias[0:TS, :], ALU.add).then_inc(v_gained, 1)
            for i, (out_, e) in enumerate(((k_in, e_k), (k_end, e_end))):
                pool.wait_ge(factors, i + 1)
                nc.gpsimd.tensor_tensor(out_[:, :, :], qk[:, 2:4, :], e[:, :].rearrange("p (q t) -> p q t", q=2),
                                        ALU.mult).then_inc(keys, 1)

        @block.vector
        def _(dve):
            nc.vector.memset(v[:, :], 0.0).then_inc(zeroed, 1)
            nc.vector.memset(scores[:, :, :], 0.0).then_inc(zeroed, 1)
            dve.wait_ge(logits, 1)
            nc.vector.tensor_tensor(z[:, :].rearrange("p (q t) -> p q t", q=2),
                                    z_acc[:, 0:W].rearrange("p (q t) -> p q t", q=2),
                                    bcast(m.gate_b[:, :], TS), ALU.add).then_inc(decays, 1)
            dve.wait_ge(loaded, 16 * LOADS)
            for h in range(HS):
                nc.vector.bn_stats(stats[:, h, :], vs[:, h * P:(h + 1) * P]).then_inc(stat, 1)
            dve.wait_ge(stat, HS)
            for h in range(HS):
                nc.vector.bn_aggr(mv[:, h, :], stats[:, h, :]).then_inc(stat, 1)
            dve.wait_ge(softs, 3)
            nc.vector.scalar_tensor_tensor(out=logd[:, :], in0=z[:, :], scalar=0.0, in1=soft[:, :],
                                           op0=ALU.min, op1=ALU.subtract).then_inc(decays, 1)
            dve.wait_ge(decays, 2)
            nc.vector.tensor_tensor_scan(out=cum[:, :], data0=m.reset_s[:, :], data1=logd[:, :], initial=0.0,
                                         op0=ALU.mult, op1=ALU.add).then_inc(decays, 1)
            dve.wait_ge(decays, 3)
            chunks = lambda x: x[:, :].rearrange("p (a c) -> p a c", c=SL)
            c = chunks(cum)
            nc.vector.tensor_tensor(chunks(from_mid), c, c[:, :, SL // 2 - 1:SL // 2].to_broadcast([P, 2 * SEQS, SL]),
                                    ALU.subtract).then_inc(decays, 1)
            nc.vector.tensor_tensor(chunks(to_end), c[:, :, SL - 1:SL].to_broadcast([P, 2 * SEQS, SL]), c,
                                    ALU.subtract).then_inc(decays, 1)
            dve.wait_ge(v_power, 2)
            for h in range(HS):
                nc.vector.tensor_scalar(vn[:, h * P:(h + 1) * P], vs[:, h * P:(h + 1) * P], mv[:, h, 0:1],
                                        v_rstd[:, h:h + 1], ALU.subtract, ALU.mult).then_inc(v_normed, 1)
            for i, (out_, e) in enumerate(((q_in, e_q), (q_state, e_cum))):
                dve.wait_ge(factors, i + 3)
                nc.vector.scalar_tensor_tensor(out=out_[:, :, :].rearrange("p q t -> p (q t)"),
                                               in0=qk[:, 0:2, :].rearrange("p q t -> p (q t)"),
                                               scalar=DK ** -0.5, in1=e[:, :], op0=ALU.mult, op1=ALU.mult)\
                    .then_inc(queries, 1)
            dve.wait_ge(scored, 1)
            dve.wait_ge(zeroed, 2)
            for f in range(2):
                rows = tok_rows(f)
                nc.vector.copy_predicated(scores[rows, :, :],
                                          m.causal_s[rows, :].bitcast(I32).unsqueeze(1).to_broadcast([TS, 2, TS]),
                                          s_acc[rows, 0:W].rearrange("p (q i) -> p q i", q=2)).then_inc(masked, 1)
            dve.wait_ge(spatials, 1)
            nc.vector.tensor_tensor(mixed_b[:, :, :], m_acc[:, 0:HS * TS].rearrange("p (h t) -> p h t", h=HS),
                                    m.spatial_b_s[:, :, :], ALU.add).then_inc(outs, 1)
            dve.wait_ge(outs, 1)
            nc.vector.tensor_tensor(out[:, H:2 * H, :], mixed_b[:, :, :], ru[:, H:2 * H, :], ALU.mult).then_inc(outs, 1)
            for f in range(2):
                rows = tok_rows(f)
                dve.wait_ge(k_copied, f + 1)
                for q in range(2):
                    last = nc.vector.tensor_tensor(k_seq[rows, q], k_tok[rows, q].unsqueeze(1).to_broadcast([TS, SEQS, DK]),
                                                   bcast(m.own_seq[rows, :], DK), ALU.mult)
                last.then_inc(k_split, 1)
            dve.wait_ge(state_in_sem, 16 * 2 * SEQS)
            decay = e_cum[:, :].rearrange("p (q b c) -> p b q c", q=2, c=SL)[:, :, :, SL - 1:SL]
            nc.vector.tensor_tensor(new_state[:, :, :, :], state[:, :, :, :], decay.to_broadcast([P, SEQS, 2, DV]),
                                    ALU.mult).then_inc(states, 1)
            dve.wait_ge(kv_made, 1)
            dve.wait_ge(states, 1)
            for i in range(SEQS // 2):
                part = new_state[:, 2 * i:2 * i + 2].rearrange("p b q e -> p (b q e)")
                nc.vector.tensor_tensor(part, part, kv_acc[i][:, :], ALU.add).then_inc(states, 1)
            dve.wait_ge(inverse, 2)
            for f in range(2):
                nc.vector.tensor_tensor(normed[:, f], o_acc[f][:, 0:W].rearrange("p (q t) -> p q t", q=2),
                                        inv[:, f], ALU.mult).then_inc(outs, 1)
            for f in range(2):
                dve.wait_ge(outs, 3 + f)
                heads = lambda x: x[:, 0:H, :].rearrange("p (q f) t -> p f q t", f=2)[:, f]
                nc.vector.scalar_tensor_tensor(out=heads(out), in0=normed[:, f], scalar=m.gain_out[:, 0:1],
                                               in1=heads(ru), op0=ALU.mult, op1=ALU.mult).then_inc(outs, 1)


def build(nc, a, outs):
    dram = lambda n, s: nc.dram_tensor(n, s, F32).ap()
    pt = dram("proj_features", [13 * P, T])
    v_s = dram("proj_v", [T, H * DV])
    vs_s = dram("proj_vs", [T, HS * P])
    mix = a["dbg_mix"] if "dbg_mix" in a else dram("mix", [D, T])
    x1, x2 = dram("x1", [T, D]), dram("x2", [T, D])
    hidden = dram("hidden", [FF, T])
    down0 = dram("down0", [T, 512])
    x_p = a["x_prompt"][0]
    x_s = a["x_sample"].rearrange("b t d -> (b t) d")

    def x_tiles(t):
        return x_s if isinstance(t, int) and t == NT else x_p[ds(t * P, P), :]

    ctx = ExitStack()
    with ctx:
        ident = ctx.enter_context(nc.sbuf_tensor("ident", [P, P], F32))
        ones = ctx.enter_context(nc.sbuf_tensor("ones", [P, P], F32))
        consts = ctx.enter_context(nc.sbuf_tensor("consts", [P, 2], F32))
        gains = ctx.enter_context(nc.sbuf_tensor("gains", [P, 3, KC], F32))
        made = ctx.enter_context(nc.semaphore("made"))
        gains_in = ctx.enter_context(nc.semaphore("gains_in"))
        with nc.Block() as block:
            @block.gpsimd
            def _(pool):
                identity_and_ones(nc, ident, ones, made)
                nc.gpsimd.memset(consts[:, 0:1], EPS)
                nc.gpsimd.memset(consts[:, 1:2], -0.5)

            @block.sync
            def _(sp):
                with nc.allow_non_contiguous_dma(reason="a gain's 1024 values, features on partitions"):
                    for i, g in enumerate(("g_mix_pre", "g_ffn_pre", "g_ple_in")):
                        sp.dma_start(gains[:, i, :], a[g][0].rearrange("(k p) -> p k", p=P)).then_inc(gains_in, 16)
                sp.wait_ge(gains_in, 48)

        with nc.sbuf_tensor("xh", [P, KC, T], F32R) as xh, nc.sbuf_tensor("xl", [P, KC, T], F32R) as xl:
            phase_norm(nc, "n1", x_tiles, xh, xl, ident, consts)
            phase_in(nc, xh, xl, a["w_in"][0], gains[:, 0, :], pt, v_s, vs_s)

        with ExitStack() as held:
            m = MixerConsts(nc, held)
            phase_mixer_consts(nc, a, m, ident)
            phase_mixers(nc, m, pt, v_s, vs_s, mix, outs[2][0, 0], ident, consts)
            phase_mixers_sample(nc, m, pt, v_s, vs_s, mix, a["state_gla"][0], outs[3][0],
                                outs[6][0].rearrange("b t n -> (b t) n"), ident, consts)

        x1_of = lambda t: x1[token_rows(t), :]
        phase_rows(nc, "out", mix, KC, a["w_out"][0], D, gain=a["g_mix_post"][0], residual=x_tiles, store=x1_of,
                   consts=consts)
        with nc.sbuf_tensor("ffn_features", [P, 2 * FC, 20], F32) as ffn, \
                nc.sbuf_tensor("tail", [P, 2 * FC, 2 + 2 * SEQS], F32) as tail:
            phase_ffn_rows(nc, [a["state_ffn_conv"][0].rearrange("b c n -> (b c) n"), a["w_conv"][0], a["b_conv"]],
                           ffn, ident)
            with nc.sbuf_tensor("xh2", [P, KC, T], F32R) as xh, nc.sbuf_tensor("xl2", [P, KC, T], F32R) as xl:
                phase_norm(nc, "n2", x1_of, xh, xl, ident, consts)
                phase_up(nc, xh, xl, a["w_up"][0], gains[:, 1, :], ffn[:, :, 16:19], ffn[:, :, 19], ffn[:, :, 0:16],
                         tail, hidden)
            phase_tail(nc, tail, ident, outs[4][0, 0], outs[5][0].rearrange("b c n -> (b c) n"))
        w_down = a["w_down"][0]
        phase_rows(nc, "dn0", hidden, FC, w_down[:, 0:512], 512, scratch=down0)
        phase_rows(nc, "dn1", hidden, FC, w_down[:, 512:1024], 512, gain=a["g_ffn_post"][0], first_half=down0,
                   residual=x1_of, store=lambda t: x2[token_rows(t), :], consts=consts)

        def p_tiles(t):
            if known(t) and t == NT:
                return ((slice(0, P - TS), a["p_prompt"][0, 0][TP - P + TS:TP, :]),
                        (slice(P - TS, P), a["p_sample"][0].rearrange("b t d -> (b t) d")))
            return ((slice(0, P), a["p_prompt"][0, 0][token_rows(t), :]),)

        def y_tiles(t):
            if known(t) and t == NT:
                return outs[1].rearrange("b t d -> (b t) d")
            return outs[0][0][token_rows(t), :]
        phase_ple(nc, x2, p_tiles, a["w_ple_gate"][0], gains[:, 2, :], a["w_ple"][0], a["g_ple_post"][0], y_tiles,
                  ident, consts)


_OUTS = [(1, TP, D), (SEQS, SL, D), (1, 1, H, DK, DV), (1, SEQS, H, DK, DV), (1, 1, 2, 2 * FF),
         (1, SEQS, 2, 2 * FF), (1, SEQS, SL, HS * P)]


def kernel(**inputs):
    import numpy as np
    import concourse.bacc as bacc
    from concourse.bass_utils import run_bass_kernel_spmd

    nc = bacc.Bacc("TRN2", target_bir_lowering=False, num_devices=1)
    arrays, a = {}, {}
    for name, value in inputs.items():
        value = np.ascontiguousarray(value)
        arrays[f"in_{name}"] = value
        a[name] = nc.dram_tensor(f"in_{name}", value.shape, F32, kind="ExternalInput").ap()
    outs = [nc.dram_tensor(f"out_{i}", shape, F32, kind="ExternalOutput").ap() for i, shape in enumerate(_OUTS)]
    build(nc, a, outs)
    got = run_bass_kernel_spmd(nc, [arrays], core_ids=[0])
    return tuple(got.results[0][f"out_{i}"] for i in range(len(outs)))
```

```python
import concourse.bass as bass
from concourse import mybir
from contextlib import ExitStack

F32 = mybir.dt.float32
F32R = mybir.dt.float32r
I32 = mybir.dt.int32
ALU = mybir.AluOpType
ACT = mybir.ActivationFunctionType

P = 128
D = 1024
KC = D // P
TP = 2048
SEQS, SL = 8, 4
TS = SEQS * SL
T = TP + TS
NT = TP // P
TB = 416
NBLK = T // TB
H, DK, DV = 4, 64, 128
C = 64
NCH = P // C
RANK = 16
TAU = 16.0
HS = 4
FF = 2816
FC = FF // P
PLE = 256
PC = PLE // P
EPS = 1e-6
COL_QK, COL_V, COL_R, COL_GLR = 0, 512, 1024, 1536
COL_U, COL_VS = 1552, 2064


def ds(start, size):
    return bass.ds(start, size)


def bcast(ap, n):
    return ap.unsqueeze(2).to_broadcast([ap.shape[0], ap.shape[1], n])


def tile_rows(t):
    return P if t < NT else TS


def rows_in_bank(t):
    return slice(0, P) if t < NT else slice(P - TS, P)


def identity(nc, ident, made):
    nc.gpsimd.memset(ident[:, :], 0.0).then_inc(made, 1)
    nc.gpsimd.wait_ge(made, 1)
    nc.gpsimd.affine_select(out=ident[:, :], in_=ident[:, :], compare_op=ALU.not_equal, fill=1.0,
                            base=0, pattern=[[-1, P]], channel_multiplier=1).then_inc(made, 1)


def rstd_ops(nc, pool, out, parts, tmp, consts, step, base):
    terms = list(parts) + [consts[:, 0:1]]
    for i in range(1, len(terms)):
        left = terms[0] if i == 1 else tmp
        if i > 1:
            pool.wait_ge(step, base + (i - 1))
        nc.gpsimd.tensor_tensor(tmp, left, terms[i], ALU.add).then_inc(step, 1)
    pool.wait_ge(step, base + len(parts))
    nc.gpsimd.tensor_tensor(out, tmp, consts[:, 1:2], ALU.pow).then_inc(step, 1)


def phase_norm(nc, tag, sources, xh, xl, ident, consts, ahead=()):
    ctx = ExitStack()
    with ctx:
        sb = lambda n, s, d=F32: ctx.enter_context(nc.sbuf_tensor(f"{tag}_{n}", s, d))
        sem = phase_semaphores(nc, ctx, tag)
        x = [sb(f"x{i}", [P, D]) for i in range(4)]
        xn = [sb(f"xn{i}", [P, D]) for i in range(2)]
        square = [sb(f"square{i}", [P, D]) for i in range(2)]
        total, mean, rstd = sb("total", [P, 4]), sb("mean", [P, 4]), sb("rstd", [P, 4])
        pt = [[ctx.enter_context(nc.psum_tensor(f"{tag}_pt{i}{h}", [P, 512], F32)) for h in range(2)]
              for i in range(2)]
        loaded = [sem(f"loaded{i}") for i in range(4)]
        summed, powers, scaled = sem("summed"), sem("powers"), sem("scaled")
        turned, rounded, split = sem("turned"), sem("rounded"), sem("split")
        block = ctx.enter_context(nc.Block())

        def rows_of(t):
            return tile_rows(t) if known(t) else P

        @block.sync
        def _(sp):
            def step(t, q, j):
                if not known(t) or t >= 4:
                    sp.wait_ge(scaled, t - 3)
                sp.dma_start(x[q][0:rows_of(t), :], sources(t)).then_inc(loaded[q], 16)
            walk_by_four(sp, step)
            for dst, src, arrived in ahead:
                sp.dma_start(dst, src).then_inc(arrived, 16)

        @block.scalar
        def _(act):
            def sums(t, q, j):
                n = rows_of(t)
                act.wait_ge(loaded[q], j * 16 + 16)
                if not known(t) or t >= 2:
                    act.wait_ge(powers, t * 2 - 2)
                nc.scalar.activation(square[q % 2][0:n, :], x[q][0:n, :], ACT.Square, scale=D ** -0.5,
                                     accum_out=total[0:n, q:q + 1]).then_inc(summed, 1)

            def step(t, q, j):
                if not known(t) or t + 3 <= NT:
                    sums(t + 3, (q + 3) % 4, j + (q + 3) // 4)
                n = rows_of(t)
                for h in range(2):
                    act.wait_ge(turned, t * 2 + (h + 1))
                    nc.scalar.activation(xh[:, 4 * h:4 * h + 4, ds(t * P, n)],
                                         pt[q % 2][h][:, 0:4 * n].rearrange("p (k t) -> p k t", k=4),
                                         ACT.Copy).then_inc(rounded, 1)
            for t in range(3):
                sums(t, t, 0)
            walk_by_four(act, step)

        @block.gpsimd
        def _(pool):
            def step(t, q, j):
                n = rows_of(t)
                pool.wait_ge(summed, t + 1)
                if not known(t) or t >= 4:
                    pool.wait_ge(scaled, t - 3)
                rstd_ops(nc, pool, rstd[0:n, q:q + 1], [total[0:n, q:q + 1]], mean[0:n, q:q + 1],
                         consts[0:n, :], powers, t * 2)
            walk_by_four(pool, step)

        @block.vector
        def _(dve):
            def scales(t, q):
                n = rows_of(t)
                dve.wait_ge(powers, t * 2 + 2)
                if not known(t) or t >= 2:
                    dve.wait_ge(turned, t * 2 - 2)
                nc.vector.tensor_scalar(xn[q % 2][0:n, :], x[q][0:n, :], rstd[0:n, q:q + 1], None,
                                        ALU.mult).then_inc(scaled, 1)

            def step(t, q, j):
                if not known(t) or t + 2 <= NT:
                    scales(t + 2, (q + 2) % 4)
                n = rows_of(t)
                for h in range(2):
                    dve.wait_ge(rounded, t * 2 + (h + 1))
                    here = (slice(None), slice(4 * h, 4 * h + 4), ds(t * P, n))
                    nc.vector.tensor_tensor(xl[here], pt[q % 2][h][:, 0:4 * n].rearrange("p (k t) -> p k t", k=4),
                                            xh[here].bitcast(F32), ALU.subtract).then_inc(split, 1)
            scales(0, 0)
            scales(1, 1)
            walk_by_four(dve, step)

        @block.tensor
        def _(pe):
            def step(t, q, j):
                n = rows_of(t)
                pe.wait_ge(scaled, t + 1)
                if not known(t) or t >= 2:
                    pe.wait_ge(split, t * 2 - 2)
                for h in range(2):
                    for k in range(4):
                        f = (4 * h + k) * P
                        last = nc.tensor.transpose(pt[q % 2][h][:, k * n:(k + 1) * n], xn[q % 2][0:n, f:f + P],
                                                   ident[0:n, 0:n])
                    last.then_inc(turned, 1)
            walk_by_four(pe, step)


def in_chunks():
    cols = [COL_V + P * i for i in range(4)] + [COL_VS + P * i for i in (2, 3, 0, 1)]
    cols += [COL_QK + P * i for i in range(4)] + [COL_R + P * i for i in range(4)]
    return cols + [COL_U + P * i for i in range(4)] + [COL_GLR]


def phase_in(nc, xh, xl, w_in, gain, pt_scratch, v_scratch, vs_scratch, raw, raw_in):
    ctx = ExitStack()
    with ctx:
        sb = lambda n, s, d=F32: ctx.enter_context(nc.sbuf_tensor(f"in_{n}", s, d))
        sem = phase_semaphores(nc, ctx, "in")
        BANKS = 5
        SLOTS = 6
        wh = sb("wh", [P, SLOTS, KC, P], F32R)
        wl = sb("wl", [P, SLOTS, KC, P], F32R)
        out = [sb(f"out{i}", [P, 512]) for i in range(BANKS)]
        acc = [ctx.enter_context(nc.psum_tensor(f"in_acc{i}", [P, 512], F32)) for i in range(BANKS)]
        gained, gained_early, high, ready = sem("gained"), sem("gained_early"), sem("high"), sem("ready")
        summed, evacuated = sem("summed"), sem("evacuated")
        stored = [sem(f"stored{i}") for i in range(BANKS)]
        block = ctx.enter_context(nc.Block())

        wide = 2 * 4
        cols = in_chunks()
        n_chunks = len(cols)
        slot = [0, 1, 2, 3, 4, 5, 2, 3] + [n % 2 for n in range(wide, n_chunks)]
        by_vector = (1, 3)
        first_bank = 2 * (NT + 1)
        w_view = w_in.rearrange("(k p) n -> p k n", p=P)

        def slot_free(eng, n):
            if 6 <= n < wide + 2:
                eng.wait_ge(summed, NT + 1)
            elif n >= wide + 2:
                eng.wait_ge(summed, first_bank + (n - 1 - wide) * NBLK)

        @block.sync
        def _(sp):
            def load(n):
                if n >= 2:
                    sp.wait_ge(ready, n - 1)
                sp.dma_start(raw[n % 2][:, :, :], w_view[:, :, cols[n]:cols[n] + P]).then_inc(raw_in[n % 2], 16)

            def store(m, dst, rows, width):
                sp.wait_ge(evacuated, m + 1)
                sp.dma_start(dst, out[m % BANKS][rows, 0:width]).then_inc(stored[m % BANKS], 16)

            for n in range(2, 6):
                load(n)
            for g, scratch in enumerate((v_scratch, vs_scratch)):
                for t in range(NT + 1):
                    if t in ((8, 9), (1, 2))[g]:
                        load(6 + 2 * g + (t + g) % 2)
                    store(g * (NT + 1) + t, scratch[t * P:t * P + tile_rows(t), :], rows_in_bank(t), 512)
            for n in range(wide, n_chunks):
                if n + 2 < n_chunks:
                    load(n + 2)
                for b in range(NBLK):
                    store(first_bank + (n - wide) * NBLK + b,
                          pt_scratch[(n - wide) * P:(n - wide + 1) * P, b * TB:(b + 1) * TB], slice(0, P), TB)
            total = first_bank + (n_chunks - wide) * NBLK
            for i in range(BANKS):
                sp.wait_ge(stored[i], 16 * len(range(i, total, BANKS)))

        @block.gpsimd
        def _(pool):
            for n in range(n_chunks):
                if n in by_vector:
                    continue
                pool.wait_ge(raw_in[n % 2], 16 * (n // 2 + 1))
                nc.gpsimd.tensor_tensor(raw[n % 2][:, :, :], raw[n % 2][:, :, :], bcast(gain[:, :], P),
                                        ALU.mult).then_inc(gained, 1)

        @block.vector
        def _(dve):
            def early_gain(n):
                dve.wait_ge(raw_in[n % 2], 16 * (n // 2 + 1))
                nc.vector.tensor_tensor(raw[n % 2][:, :, :], raw[n % 2][:, :, :], bcast(gain[:, :], P),
                                        ALU.mult).then_inc(gained_early, 1)

            early_gain(by_vector[0])
            for n in range(n_chunks):
                if n + 1 in by_vector[1:]:
                    early_gain(n + 1)
                dve.wait_ge(high, n + 1)
                nc.vector.tensor_tensor(wl[:, slot[n]], raw[n % 2][:, :, :], wh[:, slot[n]].bitcast(F32),
                                        ALU.subtract).then_inc(ready, 1)

        @block.scalar
        def _(act):
            def round_up(n):
                if n in by_vector:
                    act.wait_ge(gained_early, by_vector.index(n) + 1)
                else:
                    act.wait_ge(gained, n + 1 - sum(i < n for i in by_vector))
                slot_free(act, n)
                nc.scalar.activation(wh[:, slot[n]], raw[n % 2][:, :, :], ACT.Copy).then_inc(high, 1)

            def evacuate(m, bank, rows, width, func):
                act.wait_ge(summed, m + 1)
                if m >= BANKS:
                    act.wait_ge(stored[bank], m // BANKS * 16)
                nc.scalar.activation(out[bank][rows, 0:width], acc[bank][rows, 0:width], func)\
                    .then_inc(evacuated, 1)

            for n in range(4):
                round_up(n)
            for g, func in enumerate((ACT.Copy, ACT.Gelu_apprx_tanh)):
                for t in range(NT + 1):
                    m = g * (NT + 1) + t
                    if g == 0 and t == NT:
                        round_up(6)
                        round_up(7)
                    evacuate(m, m % BANKS, rows_in_bank(t), 512, func)
                    if g == 0 and t in (3, 5):
                        round_up(4 if t == 3 else 5)
                    if g == 1 and t == 3:
                        round_up(wide)
            for n in range(wide, n_chunks):
                func = ACT.Copy if n < wide + 4 or n == n_chunks - 1 else \
                    (ACT.Silu if n < wide + 8 else ACT.Gelu_apprx_tanh)
                for b in range(NBLK):
                    m = first_bank + (n - wide) * NBLK + b
                    evacuate(m, m % BANKS, slice(0, P), TB, func)
                    if b == 0 and n + 1 < n_chunks:
                        round_up(n + 1)

        @block.tensor
        def _(pe):
            for g in range(2):
                pe.wait_ge(ready, 4 * g + 4)
                for t in range(NT + 1):
                    m = g * (NT + 1) + t
                    first = min(t * P, T - P)
                    if m >= BANKS:
                        pe.wait_ge(evacuated, m - BANKS + 1)
                    for k in range(KC):
                        for p, (x, w) in enumerate(((xh, wh), (xh, wl), (xl, wh))):
                            last = nc.tensor.matmul(acc[m % BANKS][:, :], x[:, k, first:first + P],
                                                    w[:, 2 * g:2 * g + 4, k, :],
                                                    start=(k == 0 and p == 0), stop=(k == KC - 1 and p == 2))
                    last.then_inc(summed, 1)

            def chunk(c, s, m0):
                pe.wait_ge(ready, c + (wide + 1))
                for b in range(NBLK):
                    m = m0 + b
                    bank = (first_bank + s * NBLK + b) % BANKS
                    pe.wait_ge(evacuated, m - (BANKS - 1))
                    for k in range(KC):
                        for p, (w, x) in enumerate(((wh, xh), (wh, xl), (wl, xh))):
                            last = nc.tensor.matmul(acc[bank][:, 0:TB], w[:, s, k, :],
                                                    x[:, k, b * TB:(b + 1) * TB],
                                                    start=(k == 0 and p == 0), stop=(k == KC - 1 and p == 2))
                    last.then_inc(summed, 1)
            chunk_pairs = (n_chunks - wide) // 2
            with pe.Fori(0, chunk_pairs) as i:
                for s in range(2):
                    chunk(i * 2 + s, s, i * (2 * NBLK) + (first_bank + s * NBLK))
            chunk(2 * chunk_pairs, 0, first_bank + 2 * chunk_pairs * NBLK)


def phase_semaphores(nc, ctx, tag):
    held = []

    def clear():
        nc.clear_and_free_semaphores(held)
        nc.all_engine_barrier()
    ctx.callback(clear)

    def sem(name):
        held.append(nc.alloc_semaphore(name=f"{tag}_{name}"))
        return held[-1]
    return sem


def walk(eng, step):
    step(0, 0, 0)
    step(1, 1, 0)
    with eng.Fori(1, NT // 2 - 1) as i:
        step(i * 2, 0, i)
        step(i * 2 + 1, 1, i)
    step(NT - 2, 0, NT // 2 - 1)
    step(NT - 1, 1, NT // 2 - 1)
    step(NT, 0, NT // 2)


def walk_by_four(eng, step):
    for t in range(4):
        step(t, t, 0)
    with eng.Fori(1, NT // 4 - 1) as j:
        for q in range(4):
            step(j * 4 + q, q, j)
    for t in range(NT - 4, NT + 1):
        step(t, t % 4, t // 4)


def known(t):
    return isinstance(t, int)


def tokens_of(t):
    return slice(min(t * P, T - P), min(t * P, T - P) + P) if known(t) else ds(t * P, P)


def bank_rows(t):
    return rows_in_bank(t) if known(t) else slice(0, P)


def token_rows(t):
    return slice(t * P, t * P + tile_rows(t)) if known(t) else ds(t * P, P)


def phase_rows(nc, tag, src, kc, w, width, gain=None, first_half=None, residual=None, store=None, scratch=None,
               consts=None):
    ctx = ExitStack()
    with ctx:
        sb = lambda n, s, d=F32: ctx.enter_context(nc.sbuf_tensor(f"{tag}_{n}", s, d))
        sem = phase_semaphores(nc, ctx, tag)
        halves = width // 512
        wraw = [sb(f"wraw{i}", [P, width]) for i in range(2)]
        wh, wl = sb("wh", [P, kc, width], F32R), sb("wl", [P, kc, width], F32R)
        raw = [sb(f"raw{i}", [P, kc, P]) for i in range(2)]
        sh = [sb(f"sh{i}", [P, kc, P], F32R) for i in range(2)]
        sl = [sb(f"sl{i}", [P, kc, P], F32R) for i in range(2)]
        acc = [[ctx.enter_context(nc.psum_tensor(f"{tag}_acc{i}{h}", [P, 512], F32)) for h in range(halves)]
               for i in range(2)]
        y = [sb(f"y{i}", [P, width if gain is None else D]) for i in range(2)]
        wraw_in = [sem("wraw_in0"), sem("wraw_in1")]
        whigh, wready = sem("whigh"), sem("wready")
        src_in = [sem("src_in0"), sem("src_in1")]
        high, split, summed = sem("high"), sem("split"), sem("summed")
        stored = [sem("stored0"), sem("stored1")]
        finished = sem("finished")
        if gain is not None:
            junk = [[sb(f"junk{i}{h}", [P, 512]) for h in range(2)] for i in range(2)]
            gain_rows = sb("gain_rows", [P, D])
            res = [sb(f"res{i}", [P, D]) for i in range(2)]
            part = sb("part", [P, 2, 2])
            mean, rstd = sb("mean", [P, 2]), sb("rstd", [P, 2])
            gain_in = sem("gain_in")
            res_in = [sem("res_in0"), sem("res_in1")]
            squared, powers, added = sem("squared"), sem("powers"), sem("added")
            if first_half is not None:
                half = [sb(f"half{i}", [P, 512]) for i in range(2)]
                half_in = [sem("half_in0"), sem("half_in1")]
        block = ctx.enter_context(nc.Block())
        w_view = w.rearrange("(k p) n -> p k n", p=P)
        src_view = src.rearrange("(k p) t -> p k t", p=P)

        @block.sync
        def _(sp):
            def load_w(k):
                if k >= 2:
                    sp.wait_ge(wready, k - 1)
                sp.dma_start(wraw[k % 2][:, :], w_view[:, k, :]).then_inc(wraw_in[k % 2], 16)

            def load_src(t, s):
                if not known(t) or t >= 2:
                    sp.wait_ge(split, t - 1)
                sp.dma_start(raw[s][:, :, :], src_view[:, :, tokens_of(t)]).then_inc(src_in[s], 16)

            def load_rest(t, s):
                if gain is not None:
                    if not known(t) or t >= 2:
                        sp.wait_ge(added, t - 1)
                    sp.dma_start(res[s][bank_rows(t), :], residual(t)).then_inc(res_in[s], 16)
                    if first_half is not None:
                        sp.dma_start(half[s][bank_rows(t), :], first_half[token_rows(t), :])\
                            .then_inc(half_in[s], 16)

            def step(t, s, i):
                if not known(t) or t + 2 <= NT:
                    load_src(t + 2, s)
                if not known(t) or t < NT:
                    load_rest(t + 1, 1 - s)
                if gain is None:
                    sp.wait_ge(finished, t + 1)
                    sp.dma_start(scratch[token_rows(t), :], y[s][bank_rows(t), :]).then_inc(stored[s], 16)
                else:
                    sp.wait_ge(added, t + 1)
                    sp.dma_start(store(t), y[s][bank_rows(t), :]).then_inc(stored[s], 16)

            if gain is not None:
                sp.dma_start(gain_rows[:, :], gain.partition_broadcast(P)).then_inc(gain_in, 16)
            load_w(0)
            load_w(1)
            load_src(0, 0)
            load_rest(0, 0)
            for k in range(2, kc):
                load_w(k)
            load_src(1, 1)
            walk(sp, step)
            sp.wait_ge(stored[0], 16 * (NT // 2 + 1))
            sp.wait_ge(stored[1], 16 * (NT // 2))

        @block.scalar
        def _(act):
            def rounds(t, s, i):
                act.wait_ge(src_in[s], i * 16 + 16)
                if not known(t) or t >= 2:
                    act.wait_ge(summed, (t - 1) * halves)
                nc.scalar.activation(sh[s][:, :, :], raw[s][:, :, :], ACT.Copy).then_inc(high, 1)

            def step(t, s, i):
                if not known(t) or t < NT:
                    rounds(t + 1, 1 - s, i + s)
                rows = bank_rows(t)
                if gain is None:
                    for h in range(halves):
                        act.wait_ge(summed, t * halves + (h + 1))
                    if not known(t) or t >= 2:
                        act.wait_ge(stored[s], i * 16)
                    nc.scalar.activation(y[s][rows, :], acc[s][0][rows, :], ACT.Copy).then_inc(finished, 1)
                    return
                if not known(t) or t >= 2:
                    act.wait_ge(powers, (t - 1) * 3)
                if first_half is not None:
                    act.wait_ge(half_in[s], i * 16 + 16)
                for h in range(2):
                    if first_half is not None and h == 0:
                        half_row = half[s]
                    else:
                        b = h if halves == 2 else 0
                        act.wait_ge(summed, t * halves + (b + 1))
                        half_row = acc[s][b]
                    nc.scalar.activation(junk[s][h][rows, :], half_row[rows, :], ACT.Square, scale=D ** -0.5,
                                         accum_out=part[rows, s, h:h + 1]).then_inc(squared, 1)

            for k in range(kc):
                act.wait_ge(wraw_in[k % 2], 16 * (k // 2 + 1))
                nc.scalar.activation(wh[:, k, :], wraw[k % 2][:, :], ACT.Copy).then_inc(whigh, 1)
                if k == 1:
                    rounds(0, 0, 0)
            walk(act, step)

        @block.vector
        def _(dve):
            def splits(t, s):
                dve.wait_ge(high, t + 1)
                nc.vector.tensor_tensor(sl[s][:, :, :], raw[s][:, :, :], sh[s][:, :, :].bitcast(F32),
                                        ALU.subtract).then_inc(split, 1)

            def step(t, s, i):
                if not known(t) or t < NT:
                    splits(t + 1, 1 - s)
                if gain is None:
                    return
                rows = bank_rows(t)
                dve.wait_ge(powers, t * 3 + 3)
                if not known(t) or t >= 2:
                    dve.wait_ge(stored[s], i * 16)
                for h in range(2):
                    if first_half is not None and h == 0:
                        half_row = half[s]
                    else:
                        half_row = acc[s][h if halves == 2 else 0]
                    nc.vector.scalar_tensor_tensor(out=y[s][rows, 512 * h:512 * h + 512], in0=half_row[rows, :],
                                                   scalar=rstd[rows, s:s + 1],
                                                   in1=gain_rows[rows, 512 * h:512 * h + 512],
                                                   op0=ALU.mult, op1=ALU.mult).then_inc(finished, 1)

            for k in range(kc):
                dve.wait_ge(whigh, k + 1)
                nc.vector.tensor_tensor(wl[:, k, :], wraw[k % 2][:, :], wh[:, k, :].bitcast(F32),
                                        ALU.subtract).then_inc(wready, 1)
                if k == 1:
                    splits(0, 0)
            if gain is not None:
                dve.wait_ge(gain_in, 16)
            walk(dve, step)

        if gain is not None:
            @block.gpsimd
            def _(pool):
                def step(t, s, i):
                    rows = bank_rows(t)
                    if not known(t) or t >= 1:
                        pool.wait_ge(added, t)
                    pool.wait_ge(squared, t * 2 + 2)
                    if not known(t) or t >= 2:
                        pool.wait_ge(finished, (t - 1) * 2)
                    rstd_ops(nc, pool, rstd[rows, s:s + 1], [part[rows, s, 0:1], part[rows, s, 1:2]],
                             mean[rows, s:s + 1], consts[rows, :], powers, t * 3)
                    pool.wait_ge(res_in[s], i * 16 + 16)
                    pool.wait_ge(finished, t * 2 + 2)
                    nc.gpsimd.tensor_tensor(y[s][rows, :], y[s][rows, :], res[s][rows, :], ALU.add)\
                        .then_inc(added, 1)
                walk(pool, step)

        @block.tensor
        def _(pe):
            def step(t, s, i):
                pe.wait_ge(split, t + 1)
                if not known(t) or t >= 2:
                    pe.wait_ge(finished, (t - 1) * (1 if gain is None else 2))
                for h in range(halves):
                    for k in range(kc):
                        if known(t) and t == 0 and h == 0:
                            pe.wait_ge(wready, k + 1)
                        for p, (x, ww) in enumerate(((sh, wh), (sh, wl), (sl, wh))):
                            last = nc.tensor.matmul(acc[s][h][:, :], x[s][:, k, :],
                                                    ww[:, k, 512 * h:512 * h + 512],
                                                    start=(k == 0 and p == 0), stop=(k == kc - 1 and p == 2))
                    last.then_inc(summed, 1)
            walk(pe, step)


def phase_up(nc, xh, xl, w_up, gain, taps, bias, prefix, tail, h_scratch, ahead):
    ctx = ExitStack()
    with ctx:
        sb = lambda n, s, d=F32: ctx.enter_context(nc.sbuf_tensor(f"up_{n}", s, d))
        sem = phase_semaphores(nc, ctx, "up")
        LAST = TB - TS
        raw = [sb(f"raw{i}", [P, KC, P]) for i in range(2)]
        wh = [sb(f"wh{i}", [P, KC, P], F32R) for i in range(2)]
        wl = [sb(f"wl{i}", [P, KC, P], F32R) for i in range(2)]
        up = [sb(f"up{b}", [P, 2 + TB]) for b in range(NBLK)]
        up_s = sb("up_s", [P, SEQS, 2 + SL])
        conv = [sb(f"conv{b}", [P, TB]) for b in range(NBLK)]
        gate = [sb(f"gate{b}", [P, TB]) for b in range(NBLK)]
        acc = [ctx.enter_context(nc.psum_tensor(f"up_acc{b}", [P, 512], F32)) for b in range(NBLK)]
        raw_in = [sem("raw_in0"), sem("raw_in1")]
        gained, high, ready = sem("gained"), sem("high"), sem("ready")
        summed = sem("summed")
        evacuated = sem("evacuated")
        prefixed = sem("prefixed")
        tapped = sem("tapped")
        convolved = sem("convolved")
        gated = sem("gated")
        kept = sem("kept")
        made = sem("made")
        zeroed = sem("zeroed")
        stored = [sem(f"stored{b}") for b in range(NBLK)]
        block = ctx.enter_context(nc.Block())
        w_view = w_up.rearrange("(k p) n -> p k n", p=P)

        @block.sync
        def _(sp):
            def load(j, kind, n, turn):
                if not known(n) or n >= 2:
                    sp.wait_ge(ready, n - 1)
                sp.dma_start(raw[kind][:, :, :], w_view[:, :, ds(j * P + kind * FF, P)]).then_inc(raw_in[kind], 16)

            def store(j):
                for b in range(NBLK):
                    sp.wait_ge(made, j * NBLK + (b + 1))
                    sp.dma_start(h_scratch[ds(j * P, P), b * TB:(b + 1) * TB], conv[b][:, :])\
                        .then_inc(stored[b], 16)
            load(0, 0, 0, 0)
            load(0, 1, 1, 0)
            with sp.Fori(0, FC - 1) as j:
                for kind in range(2):
                    load(j + 1, kind, j * 2 + (2 + kind), j + 1)
                store(j)
            for dst, src, arrived in ahead:
                sp.dma_start(dst, src).then_inc(arrived, 16)
            store(FC - 1)
            for b in range(NBLK):
                sp.wait_ge(stored[b], 16 * FC)

        @block.gpsimd
        def _(pool):
            def gains(n, kind, j):
                pool.wait_ge(raw_in[kind], j * 16 + 16)
                nc.gpsimd.tensor_tensor(raw[kind][:, :, :], raw[kind][:, :, :], bcast(gain, P), ALU.mult)\
                    .then_inc(gained, 1)

            def keep(j, kind):
                pool.wait_ge(evacuated, j * (2 * NBLK) + (NBLK * (kind + 1)))
                at = ds(j + kind * FC, 1)
                nc.gpsimd.tensor_copy(tail[:, at, 0:2].rearrange("p a c -> p (a c)"), up[NBLK - 1][:, LAST:LAST + 2])
                nc.gpsimd.tensor_copy(tail[:, at, 2:18].rearrange("p a (q c) -> p (a q) c", c=2),
                                      up_s[:, :, SL:SL + 2]).then_inc(kept, 1)

            def history(j, kind, n):
                if not (known(n) and n == 0):
                    pool.wait_ge(convolved, n * NBLK)
                nc.gpsimd.tensor_copy(up_s[:, :, 0:2], prefix[:, ds(j + kind * FC, 1), :]
                                      .rearrange("p a (q c) -> p (a q) c", c=2)).then_inc(prefixed, 1)

            nc.gpsimd.memset(up[0][:, 0:2], 0.0).then_inc(zeroed, 1)
            gains(0, 0, 0)
            history(0, 0, 0)
            with pool.Fori(0, FC - 1) as j:
                gains(None, 1, j)
                keep(j, 0)
                history(j, 1, j * 2 + 1)
                gains(None, 0, j + 1)
                keep(j, 1)
                history(j + 1, 0, j * 2 + 2)
            gains(None, 1, FC - 1)
            keep(FC - 1, 0)
            history(FC - 1, 1, 2 * FC - 1)
            keep(FC - 1, 1)

        @block.scalar
        def _(act):
            def rounds(n, kind):
                act.wait_ge(gained, n + 1)
                if not known(n) or n >= 2:
                    act.wait_ge(summed, (n - 1) * NBLK)
                nc.scalar.activation(wh[kind][:, :, :], raw[kind][:, :, :], ACT.Copy).then_inc(high, 1)

            def block_out(j, kind, n, b, first):
                act.wait_ge(summed, n * NBLK + (b + 1))
                at = ds(j + kind * FC, 1)
                a = acc[b]
                prompt = TB if b < NBLK - 1 else LAST
                if not first:
                    act.wait_ge(convolved, (n - 1) * NBLK + (min(b + 2, NBLK)))
                    if b == NBLK - 1:
                        act.wait_ge(kept, n)
                if kind == 0:
                    if not first:
                        act.wait_ge(stored[b], j * 16)
                else:
                    act.wait_ge(gated, j * NBLK + (b + 1))
                if b == NBLK - 1:
                    act.wait_ge(prefixed, n + 1)
                nc.scalar.activation(up[b][:, 2:2 + prompt], a[:, 0:prompt], ACT.Copy)
                if b < NBLK - 1:
                    nc.scalar.activation(up[b + 1][:, 0:2], a[:, TB - 2:TB], ACT.Copy)
                else:
                    nc.scalar.activation(up_s[:, :, 2:2 + SL], a[:, LAST:TB].rearrange("p (q c) -> p q c", c=SL),
                                         ACT.Copy)
                nc.scalar.activation(conv[b][:, :], a[:, 0:TB], ACT.Identity,
                                     scale=taps[:, at, 2:3].rearrange("p a c -> p (a c)"),
                                     bias=bias[:, at]).then_inc(evacuated, 1)

            def gelu(j, b, first):
                act.wait_ge(convolved, j * (2 * NBLK) + (b + 1))
                if not first:
                    act.wait_ge(made, (j - 1) * NBLK + (b + 1))
                nc.scalar.activation(gate[b][:, :], conv[b][:, :], ACT.Gelu_apprx_tanh).then_inc(gated, 1)

            def pair(j, first, last):
                for b in range(NBLK):
                    block_out(j, 0, j * 2, b, first)
                    if b == 0:
                        rounds(j * 2 + 1, 1)
                    else:
                        gelu(j, b - 1, first)
                gelu(j, NBLK - 1, first)
                for b in range(NBLK):
                    block_out(j, 1, j * 2 + 1, b, False)
                    if b == 0 and not last:
                        rounds(j * 2 + 2, 0)

            act.wait_ge(zeroed, 1)
            rounds(0, 0)
            pair(0, True, False)
            with act.Fori(1, FC - 1) as j:
                pair(j, False, False)
            pair(FC - 1, False, True)

        @block.vector
        def _(dve):
            def splits(n, kind):
                dve.wait_ge(high, n + 1)
                nc.vector.tensor_tensor(wl[kind][:, :, :], raw[kind][:, :, :], wh[kind][:, :, :].bitcast(F32),
                                        ALU.subtract).then_inc(ready, 1)

            def convolve(j, kind, n, b, base):
                dve.wait_ge(evacuated, n * NBLK + (b + 1))
                at = ds(j + kind * FC, 1)
                prompt = TB if b < NBLK - 1 else LAST
                parts = [(conv[b][:, 0:prompt], lambda c: up[b][:, c:c + prompt])]
                if b == NBLK - 1:
                    parts.append((conv[b][:, LAST:TB].rearrange("p (q c) -> p q c", c=SL),
                                  lambda c: up_s[:, :, c:c + SL]))
                for c in (1, 0):
                    if c == 0:
                        dve.wait_ge(tapped, base + 1)
                    for i, (out, x) in enumerate(parts):
                        last = nc.vector.scalar_tensor_tensor(out=out, in0=x(c), in1=out,
                                                              scalar=taps[:, at, c:c + 1].rearrange("p a c -> p (a c)"),
                                                              op0=ALU.mult, op1=ALU.add)
                    last.then_inc(tapped if c == 1 else convolved, 1)

            def product(j, b):
                dve.wait_ge(convolved, j * (2 * NBLK) + (NBLK + b + 1))
                nc.vector.tensor_tensor(conv[b][:, :], conv[b][:, :], gate[b][:, :], ALU.mult).then_inc(made, 1)

            def pair(j, last):
                for b in range(NBLK):
                    convolve(j, 0, j * 2, b, j * (2 * NBLK) + b)
                    if b == 0:
                        splits(j * 2 + 1, 1)
                for b in range(NBLK):
                    convolve(j, 1, j * 2 + 1, b, j * (2 * NBLK) + (NBLK + b))
                    product(j, b)
                    if b == 0 and not last:
                        splits(j * 2 + 2, 0)

            splits(0, 0)
            with dve.Fori(0, FC - 1) as j:
                pair(j, False)
            pair(FC - 1, True)

        @block.tensor
        def _(pe):
            def pair(j, first):
                for kind in range(2):
                    n = j * 2 + kind
                    pe.wait_ge(ready, n + 1)
                    for b in range(NBLK):
                        if not (first and kind == 0):
                            pe.wait_ge(evacuated, (n - 1) * NBLK + (b + 1))
                        for k in range(KC):
                            for p, (w, x) in enumerate(((wh, xh), (wh, xl), (wl, xh))):
                                last = nc.tensor.matmul(acc[b][:, 0:TB], w[kind][:, k, :],
                                                        x[:, k, b * TB:(b + 1) * TB],
                                                        start=(k == 0 and p == 0), stop=(k == KC - 1 and p == 2))
                        last.then_inc(summed, 1)
            pair(0, True)
            with pe.Fori(1, FC) as j:
                pair(j, False)


def phase_ffn_rows(nc, rows, features, ident):
    n_rows, n_cols = 20, 2 * FC
    per_bank = 512 // n_rows
    ctx = ExitStack()
    with ctx:
        flat = ctx.enter_context(nc.sbuf_tensor("fr_flat", [n_rows, 2 * FF], F32))
        acc = [ctx.enter_context(nc.psum_tensor(f"fr_acc{i}", [P, 512], F32)) for i in range(2)]
        sem = phase_semaphores(nc, ctx, "fr")
        loaded, turned = sem("loaded"), sem("turned")
        block = ctx.enter_context(nc.Block())

        @block.sync
        def _(sp):
            at = 0
            for r in rows:
                sp.dma_start(flat[at:at + r.shape[0], :], r).then_inc(loaded, 16)
                at += r.shape[0]

        @block.tensor
        def _(pe):
            pe.wait_ge(loaded, 16 * len(rows))
            for f in range(n_cols):
                b, q = divmod(f, per_bank)
                nc.tensor.transpose(acc[b][:, q * n_rows:(q + 1) * n_rows], flat[:, f * P:(f + 1) * P],
                                    ident[0:n_rows, 0:n_rows]).then_inc(turned, 1)

        @block.vector
        def _(dve):
            for b in range(2):
                n = min(per_bank, n_cols - b * per_bank)
                dve.wait_ge(turned, b * per_bank + n)
                nc.vector.tensor_copy(features[:, b * per_bank:b * per_bank + n, :],
                                      acc[b][:, 0:n * n_rows].rearrange("p (f r) -> p f r", r=n_rows))


def walk_twice(eng, step, between):
    walk(eng, lambda t, s, i: step(0, t, t, s, i))
    between()
    walk(eng, lambda t, s, i: step(1, t, t + (NT + 1), 1 - s, i + (NT // 2 + s)))


DOWN_AHEAD = 8


def phase_down(nc, hidden, w, tail, prompt_out, sample_out, scratch, gain, residual, store, wraw, wraw_in,
               ident, consts):
    ctx = ExitStack()
    with ctx:
        sb = lambda n, s, d=F32: ctx.enter_context(nc.sbuf_tensor(f"down_{n}", s, d))
        bank = lambda n: ctx.enter_context(nc.psum_tensor(f"down_{n}", [P, 512], F32))
        sem = phase_semaphores(nc, ctx, "down")
        W = 512
        wraw, wraw_in = wraw + [sb("wraw", [P, W])], wraw_in + [sem("wraw_in")]
        R = len(wraw)
        wh, wl = sb("wh", [P, FC, W], F32R), sb("wl", [P, FC, W], F32R)
        raw = [sb(f"raw{i}", [P, FC, P]) for i in range(2)]
        sh = [sb(f"sh{i}", [P, FC, P], F32R) for i in range(2)]
        sl = [sb(f"sl{i}", [P, FC, P], F32R) for i in range(2)]
        y = [sb(f"y{i}", [P, D]) for i in range(2)]
        area = sb("area", [P, 2 * FF])
        n_rows, groups = 2 + 2 * SEQS, 2 * FC // 4
        tail_rows = area[0:n_rows, :]
        res = [area[:, i * D:(i + 1) * D] for i in range(2)]
        half = [area[:, 2 * D + i * W:2 * D + (i + 1) * W] for i in range(2)]
        junk = [area[:, 3 * D + i * W:3 * D + (i + 1) * W] for i in range(2)]
        gain_rows = area[:, 4 * D:5 * D]
        part = sb("part", [P, 2, 2])
        mean, rstd = sb("mean", [P, 2]), sb("rstd", [P, 2])
        acc, tail_acc = [bank("acc0"), bank("acc1")], [bank(f"tail_acc{i}") for i in range(4)]
        whigh, wready, used = sem("whigh"), sem("wready"), sem("used")
        src_in = [sem("src_in0"), sem("src_in1")]
        high, split, summed = sem("high"), sem("split"), sem("summed")
        copied = sem("copied")
        stored = [sem("stored0"), sem("stored1")]
        tail_turned, tail_copied, tail_stored = sem("tail_turned"), sem("tail_copied"), sem("tail_stored")
        gain_in = sem("gain_in")
        res_in, half_in = [sem("res_in0"), sem("res_in1")], [sem("half_in0"), sem("half_in1")]
        squared, powers = sem("squared"), sem("powers")
        finished = sem("finished")
        added = sem("added")
        block = ctx.enter_context(nc.Block())
        w_view = w.rearrange("(k p) n -> p k n", p=P)
        src_view = hidden.rearrange("(k p) t -> p k t", p=P)

        def two_back(half_no, t):
            return half_no == 1 or not known(t) or t >= 2

        def tail_groups(t):
            return {0: range(0, 4), 1: range(4, 8), NT - 2: range(8, groups)}.get(t, ()) if known(t) else ()

        def products_done(eng, half_no, t, g):
            if half_no == 0 and known(t) and t == NT:
                eng.wait_ge(used, FC)
            else:
                eng.wait_ge(summed, g + 1 if half_no == 0 else g)

        @block.sync
        def _(sp):
            def load_w(n):
                if n >= R:
                    sp.wait_ge(wready, n - (R - 1))
                c = n // FC * W
                sp.dma_start(wraw[n % R][:, :], w_view[:, n % FC, c:c + W]).then_inc(wraw_in[n % R], 16)

            def load_src(t, g, s):
                if not known(g) or g >= 2:
                    sp.wait_ge(split, g - 1)
                sp.dma_start(raw[s][:, :, :], src_view[:, :, tokens_of(t)]).then_inc(src_in[s], 16)

            def load_rest(t, s):
                if not known(t) or t >= 2:
                    sp.wait_ge(added, t - 1)
                sp.dma_start(res[s][bank_rows(t), :], residual(t)).then_inc(res_in[s], 16)
                sp.dma_start(half[s][bank_rows(t), :], scratch[token_rows(t), :]).then_inc(half_in[s], 16)

            def step(half_no, t, g, s, u):
                if not known(t) or t + 2 <= NT:
                    load_src(t + 2, g + 2, s)
                elif half_no == 0:
                    load_src(t + 1 - NT, g + 2, s)
                if half_no == 0:
                    if known(t) and t == NT - 1:
                        sp.wait_ge(tail_copied, groups)
                        sp.dma_start(prompt_out, tail_rows[0:2, :]).then_inc(tail_stored, 16)
                        sp.dma_start(sample_out, tail_rows[2:n_rows, :]).then_inc(tail_stored, 16)
                    if known(t) and t == 1:
                        for n in range(FC, FC + R):
                            load_w(n)
                    if known(t) and t == NT:
                        for n in range(FC + R, 2 * FC):
                            load_w(n)
                    sp.wait_ge(copied, t + 1)
                    sp.dma_start(scratch[token_rows(t), :], y[s][bank_rows(t), 0:W]).then_inc(stored[s], 16)
                else:
                    if not known(t) or t < NT:
                        load_rest(t + 1, s)
                    sp.wait_ge(added, t + 1)
                    sp.dma_start(store(t), y[s][bank_rows(t), :]).then_inc(stored[s], 16)

            def between():
                sp.wait_ge(tail_stored, 32)
                sp.dma_start(gain_rows, gain.partition_broadcast(P)).then_inc(gain_in, 16)
                sp.wait_ge(stored[0], 16 * (NT // 2 + 1))
                sp.wait_ge(stored[1], 16 * (NT // 2))
                load_rest(0, 0)

            load_src(0, 0, 0)
            for n in range(DOWN_AHEAD, FC):
                load_w(n)
            load_src(1, 1, 1)
            walk_twice(sp, step, between)
            sp.wait_ge(stored[0], 16 * (NT + 1))
            sp.wait_ge(stored[1], 16 * (NT + 1))

        @block.scalar
        def _(act):
            def round_w(n):
                act.wait_ge(wraw_in[n % R], 16 * (n // R + 1))
                if n >= FC:
                    act.wait_ge(used, n - (FC - 1))
                nc.scalar.activation(wh[:, n % FC, :], wraw[n % R][:, :], ACT.Copy).then_inc(whigh, 1)

            def rounds(half_no, t, g, s, u):
                act.wait_ge(src_in[s], u * 16 + 16)
                if two_back(half_no, t):
                    if half_no == 1 and known(t) and t < 2:
                        products_done(act, 0, NT - 1 + t, g - 2)
                    else:
                        products_done(act, half_no, t - 2, g - 2)
                nc.scalar.activation(sh[s][:, :, :], raw[s][:, :, :], ACT.Copy).then_inc(high, 1)

            def step(half_no, t, g, s, u):
                if not known(t) or t < NT:
                    rounds(half_no, t + 1, g + 1, 1 - s, u + s)
                elif half_no == 0:
                    rounds(1, 0, g + 1, 1 - s, u + s)
                    for n in range(FC, 2 * FC):
                        round_w(n)
                rows = bank_rows(t)
                if half_no == 0:
                    products_done(act, 0, t, g)
                    if two_back(half_no, t):
                        act.wait_ge(stored[s], u * 16)
                    nc.scalar.activation(y[s][rows, 0:W], acc[s][rows, :], ACT.Copy).then_inc(copied, 1)
                    return
                q = 1 - s
                if not known(t) or t >= 1:
                    act.wait_ge(powers, t * 3)
                act.wait_ge(half_in[q], (u - NT // 2 - q) * 16 + 16)
                nc.scalar.activation(junk[0][rows, :], half[q][rows, :], ACT.Square, scale=D ** -0.5,
                                     accum_out=part[rows, q, 0:1]).then_inc(squared, 1)
                products_done(act, 1, t, g)
                nc.scalar.activation(junk[1][rows, :], acc[s][rows, :], ACT.Square, scale=D ** -0.5,
                                     accum_out=part[rows, q, 1:2]).then_inc(squared, 1)

            for n in range(FC):
                round_w(n)
                if n == 1:
                    rounds(0, 0, 0, 0, 0)
            walk_twice(act, step, lambda: act.wait_ge(tail_stored, 32))

        @block.vector
        def _(dve):
            def split_w(n):
                dve.wait_ge(whigh, n + 1)
                nc.vector.tensor_tensor(wl[:, n % FC, :], wraw[n % R][:, :], wh[:, n % FC, :].bitcast(F32),
                                        ALU.subtract).then_inc(wready, 1)

            def splits(g, s):
                dve.wait_ge(high, g + 1)
                nc.vector.tensor_tensor(sl[s][:, :, :], raw[s][:, :, :], sh[s][:, :, :].bitcast(F32),
                                        ALU.subtract).then_inc(split, 1)

            def step(half_no, t, g, s, u):
                if not known(t) or t < NT or half_no == 0:
                    splits(g + 1, 1 - s)
                if half_no == 0:
                    for gr in tail_groups(t):
                        dve.wait_ge(tail_turned, gr + 1)
                        nc.vector.tensor_copy(tail_rows[:, gr * 512:(gr + 1) * 512],
                                              tail_acc[gr % 4][0:n_rows, :]).then_inc(tail_copied, 1)
                    if known(t) and t == NT:
                        for n in range(FC, 2 * FC):
                            split_w(n)
                    return
                rows, q = bank_rows(t), 1 - s
                dve.wait_ge(powers, t * 3 + 3)
                dve.wait_ge(stored[s], u * 16)
                for h, half_row in enumerate((half[q], acc[s])):
                    nc.vector.scalar_tensor_tensor(out=y[s][rows, W * h:W * h + W], in0=half_row[rows, :],
                                                   scalar=rstd[rows, q:q + 1],
                                                   in1=gain_rows[rows, W * h:W * h + W],
                                                   op0=ALU.mult, op1=ALU.mult).then_inc(finished, 1)

            split_w(0)
            split_w(1)
            splits(0, 0)
            for n in range(2, FC):
                split_w(n)
            walk_twice(dve, step, lambda: dve.wait_ge(gain_in, 16))

        @block.gpsimd
        def _(pool):
            def step(t, q, i):
                rows = bank_rows(t)
                s = 1 - q
                if not known(t) or t >= 1:
                    pool.wait_ge(added, t)
                pool.wait_ge(squared, t * 2 + 2)
                if not known(t) or t >= 2:
                    pool.wait_ge(finished, (t - 1) * 2)
                rstd_ops(nc, pool, rstd[rows, q:q + 1], [part[rows, q, 0:1], part[rows, q, 1:2]],
                         mean[rows, q:q + 1], consts[rows, :], powers, t * 3)
                pool.wait_ge(res_in[q], i * 16 + 16)
                pool.wait_ge(finished, t * 2 + 2)
                nc.gpsimd.tensor_tensor(y[s][rows, :], y[s][rows, :], res[q][rows, :], ALU.add)\
                    .then_inc(added, 1)
            walk(pool, step)

        @block.tensor
        def _(pe):
            def step(half_no, t, g, s, u):
                pe.wait_ge(split, g + 1)
                if half_no == 0 and two_back(0, t):
                    pe.wait_ge(copied, g - 1)
                elif half_no == 1 and known(t) and t < 2:
                    pe.wait_ge(copied, g - 1)
                elif half_no == 1:
                    pe.wait_ge(finished, (t - 1) * 2)
                first, last_left = known(t) and t == 0, half_no == 0 and known(t) and t == NT
                for k in range(FC):
                    if first:
                        pe.wait_ge(wready, half_no * FC + k + 1)
                    for p, (x, ww) in enumerate(((sh, wh), (sh, wl), (sl, wh))):
                        last = nc.tensor.matmul(acc[s][:, :], x[s][:, k, :], ww[:, k, :],
                                                start=(k == 0 and p == 0), stop=(k == FC - 1 and p == 2))
                    if last_left:
                        last.then_inc(used, 1)
                if not last_left:
                    last.then_inc(summed, 1)
                for gr in tail_groups(t) if half_no == 0 else ():
                    if gr >= 4:
                        pe.wait_ge(tail_copied, gr - 3)
                    for q in range(4):
                        last = nc.tensor.transpose(tail_acc[gr % 4][0:n_rows, q * P:(q + 1) * P],
                                                   tail[:, 4 * gr + q, :], ident[:, :])
                    last.then_inc(tail_turned, 1)
            walk_twice(pe, step, lambda: None)


def phase_ple(nc, x, p_tiles, w_gate, gate_gain, w_ple, gain, y_tiles, ident, consts):
    ctx = ExitStack()
    with ctx:
        sb = lambda n, s, d=F32: ctx.enter_context(nc.sbuf_tensor(f"ple_{n}", s, d))
        sem = phase_semaphores(nc, ctx, "ple")
        bank = lambda n: ctx.enter_context(nc.psum_tensor(f"ple_{n}_acc", [P, 512], F32))
        two = lambda n, s, d=F32: [sb(f"{n}{i}", s, d) for i in range(2)]
        K2 = KC + PC
        wraw = two("wraw", [P, D])
        wh, wl = sb("wh", [P, K2, D], F32R), sb("wl", [P, K2, D], F32R)
        xt = [sb(f"x{i}", [P, D]) for i in range(4)]
        pt, xn = two("p", [P, PLE]), two("xn", [P, D])
        junk = two("junk", [P, D])
        sh, sl = two("sh", [P, K2, P], F32R), two("sl", [P, K2, P], F32R)
        gate, e, y = two("gate", [P, D]), two("e", [P, D]), two("y", [P, D])
        gain_rows = sb("gain_rows", [P, D])
        total, mean, rstd = sb("total", [P, 2]), sb("mean", [P, 2]), sb("rstd", [P, 2])
        total2, mean2, rstd2 = sb("total2", [P, 2]), sb("mean2", [P, 2]), sb("rstd2", [P, 2])
        turn_acc = [bank("turn0"), bank("turn1"), bank("turn2")]
        gate_acc, ple_acc = [bank("gate0"), bank("gate1")], [bank("ple0"), bank("ple1")]
        wraw_in, x_in, p_in = [sem("wraw_in0"), sem("wraw_in1")], [sem(f"x_in{i}") for i in range(4)], [sem("p_in0"), sem("p_in1")]
        gain_in = sem("gain_in")
        whigh, wready = sem("whigh"), sem("wready")
        summed, powers, scaled = sem("summed"), sem("powers"), sem("scaled")
        turned, high, split = sem("turned"), sem("high"), sem("split")
        gates, ples = sem("gates"), sem("ples")
        opened, gated = sem("opened"), sem("gated")
        squared, powers2, finished, added = sem("squared"), sem("powers2"), sem("finished"), sem("added")
        stored = [sem("stored0"), sem("stored1")]
        block = ctx.enter_context(nc.Block())
        sizes = (4, 4, PC)
        starts = (0, 4, 8)

        @block.sync
        def _(sp):
            def load_w(k):
                if k >= 2:
                    sp.wait_ge(wready, k - 1)
                src = w_gate[k * P:(k + 1) * P, :] if k < KC else w_ple[(k - KC) * P:(k - KC + 1) * P, :]
                sp.dma_start(wraw[k % 2][:, :], src).then_inc(wraw_in[k % 2], 16)

            def load(t, q):
                if not known(t) or t >= 4:
                    sp.wait_ge(added, t - 3)
                sp.dma_start(xt[q][:, :], x[tokens_of(t), :]).then_inc(x_in[q], 16)
                if not known(t) or t >= 2:
                    sp.wait_ge(turned, t * 3 - 3)
                for rows, src in p_tiles(t):
                    sp.dma_start(pt[q % 2][rows, :], src).then_inc(p_in[q % 2], 16)

            def step(t, q, j):
                s = q % 2
                if not known(t) or t + 3 <= NT:
                    load(t + 3, (q + 3) % 4)
                sp.wait_ge(added, t + 1)
                sp.dma_start(y_tiles(t), y[s][bank_rows(t), :]).then_inc(stored[s], 16)

            sp.dma_start(gain_rows[:, :], gain.partition_broadcast(P)).then_inc(gain_in, 16)
            load(0, 0)
            load_w(0)
            load_w(1)
            load(1, 1)
            for k in range(2, K2):
                load_w(k)
            load(2, 2)
            walk_by_four(sp, step)
            sp.wait_ge(stored[0], 16 * (NT // 2 + 1))
            sp.wait_ge(stored[1], 16 * (NT // 2))

        @block.scalar
        def _(act):
            def squares(t, q, j):
                s = q % 2
                act.wait_ge(x_in[q], j * 16 + 16)
                if not known(t) or t >= 2:
                    act.wait_ge(powers, t * 2 - 2)
                nc.scalar.activation(junk[s][:, :], xt[q][:, :], ACT.Square, scale=D ** -0.5,
                                     accum_out=total[:, s:s + 1]).then_inc(summed, 1)

            def rounds(t, s):
                for g in range(3):
                    act.wait_ge(turned, t * 3 + (g + 1))
                    if g == 0 and (not known(t) or t >= 2):
                        act.wait_ge(ples, t * 2 - 2)
                    n = sizes[g]
                    nc.scalar.activation(sh[s][:, starts[g]:starts[g] + n, :],
                                         turn_acc[g][:, 0:n * P].rearrange("p (k t) -> p k t", k=n),
                                         ACT.Copy).then_inc(high, 1)

            def open_gate(t, s, h):
                act.wait_ge(gates, t * 2 + (h + 1))
                if not known(t) or t >= 2:
                    act.wait_ge(gated, (t - 1) * 2)
                nc.scalar.activation(gate[s][:, 512 * h:512 * h + 512], gate_acc[h][:, :], ACT.Sigmoid)\
                    .then_inc(opened, 1)

            def step(t, q, j):
                s = q % 2
                if not known(t) or t + 2 <= NT:
                    squares(t + 2, (q + 2) % 4, j + q // 2)
                open_gate(t, s, 0)
                if not known(t) or t < NT:
                    rounds(t + 1, 1 - s)
                open_gate(t, s, 1)
                act.wait_ge(gated, t * 2 + 2)
                if not known(t) or t >= 2:
                    act.wait_ge(powers2, t * 2 - 2)
                nc.scalar.activation(junk[s][:, :], e[s][:, :], ACT.Square, scale=D ** -0.5,
                                     accum_out=total2[:, s:s + 1]).then_inc(squared, 1)

            squares(0, 0, 0)
            for k in range(K2):
                act.wait_ge(wraw_in[k % 2], 16 * (k // 2 + 1))
                scale = gate_gain[:, k:k + 1] if k < KC else 1.0
                nc.scalar.activation(wh[:, k, :], wraw[k % 2][:, :], ACT.Copy, scale=scale).then_inc(whigh, 1)
                if k == 1:
                    rounds(0, 0)
                    squares(1, 1, 0)
            walk_by_four(act, step)

        @block.gpsimd
        def _(pool):
            def inner(t, s):
                pool.wait_ge(summed, t + 1)
                if not known(t) or t >= 2:
                    pool.wait_ge(scaled, t - 1)
                rstd_ops(nc, pool, rstd[:, s:s + 1], [total[:, s:s + 1]], mean[:, s:s + 1], consts, powers, t * 2)

            def step(t, q, j):
                s = q % 2
                if not known(t) or t + 2 <= NT:
                    inner(t + 2, s)
                pool.wait_ge(squared, t + 1)
                if not known(t) or t >= 2:
                    pool.wait_ge(finished, t - 1)
                rstd_ops(nc, pool, rstd2[:, s:s + 1], [total2[:, s:s + 1]], mean2[:, s:s + 1], consts, powers2,
                         t * 2)
                pool.wait_ge(finished, t + 1)
                nc.gpsimd.tensor_tensor(y[s][:, :], y[s][:, :], xt[q][:, :], ALU.add).then_inc(added, 1)
            inner(0, 0)
            inner(1, 1)
            walk_by_four(pool, step)

        @block.vector
        def _(dve):
            def scale(t, q):
                s = q % 2
                dve.wait_ge(powers, t * 2 + 2)
                if not known(t) or t >= 2:
                    dve.wait_ge(turned, t * 3 - 3)
                nc.vector.tensor_scalar(xn[s][:, :], xt[q][:, :], rstd[:, s:s + 1], None, ALU.mult)\
                    .then_inc(scaled, 1)

            def splits(t, s):
                for g in range(3):
                    dve.wait_ge(high, t * 3 + (g + 1))
                    n = sizes[g]
                    here = (slice(None), slice(starts[g], starts[g] + n), slice(None))
                    nc.vector.tensor_tensor(sl[s][here], turn_acc[g][:, 0:n * P].rearrange("p (k t) -> p k t", k=n),
                                            sh[s][here].bitcast(F32), ALU.subtract).then_inc(split, 1)

            def step(t, q, j):
                s = q % 2
                if not known(t) or t + 2 <= NT:
                    scale(t + 2, (q + 2) % 4)
                if not known(t) or t < NT:
                    splits(t + 1, 1 - s)
                for h in range(2):
                    dve.wait_ge(ples, t * 2 + (h + 1))
                    dve.wait_ge(opened, t * 2 + (h + 1))
                    if not known(t) or t >= 2:
                        dve.wait_ge(finished, t - 1)
                    nc.vector.tensor_tensor(e[s][:, 512 * h:512 * h + 512], ple_acc[h][:, :],
                                            gate[s][:, 512 * h:512 * h + 512], ALU.mult).then_inc(gated, 1)
                dve.wait_ge(powers2, t * 2 + 2)
                if not known(t) or t >= 2:
                    dve.wait_ge(stored[s], j * 32 + (q // 2) * 16)
                nc.vector.scalar_tensor_tensor(out=y[s][:, :], in0=e[s][:, :], scalar=rstd2[:, s:s + 1],
                                               in1=gain_rows[:, :], op0=ALU.mult, op1=ALU.mult).then_inc(finished, 1)

            scale(0, 0)
            for k in range(K2):
                dve.wait_ge(whigh, k + 1)
                if k < KC:
                    nc.vector.scalar_tensor_tensor(out=wl[:, k, :], in0=wraw[k % 2][:, :], scalar=gate_gain[:, k:k + 1],
                                                   in1=wh[:, k, :].bitcast(F32), op0=ALU.mult, op1=ALU.subtract)\
                        .then_inc(wready, 1)
                    if k == 1:
                        splits(0, 0)
                        scale(1, 1)
                else:
                    nc.vector.tensor_tensor(wl[:, k, :], wraw[k % 2][:, :], wh[:, k, :].bitcast(F32), ALU.subtract)\
                        .then_inc(wready, 1)
            dve.wait_ge(gain_in, 16)
            walk_by_four(dve, step)

        @block.tensor
        def _(pe):
            def turns(t, s, i):
                pe.wait_ge(scaled, t + 1)
                pe.wait_ge(p_in[s], i * 16 + 16)
                if known(t) and t == NT:
                    pe.wait_ge(p_in[s], i * 16 + 32)
                if not known(t) or t >= 1:
                    pe.wait_ge(split, t * 3)
                for g in range(3):
                    for k in range(sizes[g]):
                        src = xn[s][:, (starts[g] + k) * P:(starts[g] + k + 1) * P] if g < 2 else \
                            pt[s][:, k * P:(k + 1) * P]
                        last = nc.tensor.transpose(turn_acc[g][:, k * P:(k + 1) * P], src, ident[:, :])
                    last.then_inc(turned, 1)

            def products(t, s, acc, chunks, h, done):
                for k in chunks:
                    if known(t) and t == 0 and h == 0:
                        pe.wait_ge(wready, k + 1)
                    for p, (a, w) in enumerate(((sh, wh), (sh, wl), (sl, wh))):
                        last = nc.tensor.matmul(acc[h][:, :], a[s][:, k, :], w[:, k, 512 * h:512 * h + 512],
                                                start=(k == chunks[0] and p == 0), stop=(k == chunks[-1] and p == 2))
                last.then_inc(done, 1)

            def step(t, s, i):
                pe.wait_ge(split, t * 3 + 3)
                for h in range(2):
                    if not known(t) or t >= 1:
                        pe.wait_ge(opened, t * 2)
                    products(t, s, gate_acc, range(KC), h, gates)
                    if h == 0 and (not known(t) or t < NT):
                        turns(t + 1, 1 - s, i + s)
                for h in range(2):
                    if not known(t) or t >= 1:
                        pe.wait_ge(gated, t * 2)
                    products(t, s, ple_acc, range(KC, K2), h, ples)
            turns(0, 0, 0)
            walk(pe, step)


class MixerConsts:

    def __init__(self, nc, ctx):
        sb = lambda n, s: ctx.enter_context(nc.sbuf_tensor(f"mc_{n}", s, F32))
        self.average = sb("average", [P, P])
        self.gate_w = sb("gate_w", [RANK, H * DK])
        self.gate_b = sb("gate_b", [P, 2])
        self.gain_out = sb("gain_out", [P, 1])
        self.ln_gain, self.ln_bias = sb("ln_gain", [P, HS * P]), sb("ln_bias", [P, HS * P])
        self.spatial_raw = sb("spatial_raw", [P, HS, P])
        self.spatial = sb("spatial", [P, HS, P])
        self.spatial_b = sb("spatial_b", [P, HS, P])
        self.reset = sb("reset", [P, 2 * P])
        self.causal = sb("causal", [P, C])
        self.spatial_s = sb("spatial_s", [TS, HS, TS])
        self.spatial_b_s = sb("spatial_b_s", [P, HS, TS])
        self.reset_s = sb("reset_s", [P, 2 * TS])
        self.causal_s = sb("causal_s", [P, TS])
        self.own_seq = sb("own_seq", [P, SEQS])


def phase_mixer_consts(nc, a, m, ident):
    ctx = ExitStack()
    with ctx:
        sem = phase_semaphores(nc, ctx, "mc")
        acc = ctx.enter_context(nc.psum_tensor("mc_acc", [P, 512], F32))
        loaded, spatial_in, turned, copied, cut, zeroed = (sem(n) for n in (
            "loaded", "spatial_in", "turned", "copied", "cut", "zeroed"))
        base_in, diag_in, filled = sem("base_in"), sem("diag_in"), sem("filled")
        block = ctx.enter_context(nc.Block())
        b_spatial = a["b_spatial"][0]

        @block.sync
        def _(sp):
            sp.dma_start(m.spatial_raw[:, :, :], a["w_spatial"][0].rearrange("h t s -> t h s")).then_inc(spatial_in, 16)
            n = 0
            with nc.allow_non_contiguous_dma(reason="a few hundred values, features on partitions"):
                for out, src in ((m.gate_w[:, :], a["w_gla_gate"][0]),
                                 (m.gate_b[:, :], a["b_gla_gate"][0].rearrange("(c p) -> p c", p=P)),
                                 (m.gain_out[:, :], a["g_gla_out"][0].rearrange("(p c) -> p c", c=1)),
                                 (m.ln_gain[:, :], a["g_sgu_ln"][0].partition_broadcast(P)),
                                 (m.ln_bias[:, :], a["b_sgu_ln"][0].partition_broadcast(P)),
                                 (m.spatial_b[:, :, :], b_spatial.partition_broadcast(P))):
                    sp.dma_start(out, src).then_inc(loaded, 16)
                    n += 1
            sp.wait_ge(loaded, 16 * n)
            sp.wait_ge(cut, 1)
            sp.wait_ge(zeroed, 1)
            for q in range(SEQS):
                sp.dma_start(m.spatial_s[SL * q:SL * q + SL, :, SL * q:SL * q + SL], m.spatial[0:SL, :, 0:SL])\
                    .then_inc(diag_in, 16)
            sp.wait_ge(diag_in, 16 * SEQS)

        @block.tensor
        def _(pe):
            pe.wait_ge(spatial_in, 16)
            for h in range(HS):
                last = nc.tensor.transpose(acc[:, h * P:(h + 1) * P], m.spatial_raw[:, h, :], ident[:, :])
            last.then_inc(turned, 1)

        @block.vector
        def _(dve):
            dve.wait_ge(turned, 1)
            nc.vector.tensor_copy(m.spatial[:, :, :], acc[:, :].rearrange("p (h t) -> p h t", h=HS)).then_inc(copied, 1)
            nc.vector.memset(m.average[:, :], 1.0 / DV)
            nc.vector.memset(m.reset[:, :], 1.0)
            nc.vector.memset(m.reset_s[:, :], 1.0).then_inc(filled, 1)
            dve.wait_ge(filled, 1)
            nc.vector.memset(m.reset[:, :].rearrange("p (a c) -> p a c", c=C)[:, :, 0:1], 0.0)
            nc.vector.memset(m.reset_s[:, :].rearrange("p (a c) -> p a c", c=SL)[:, :, 0:1], 0.0)
            dve.wait_ge(loaded, 16 * 6)
            nc.vector.tensor_copy(m.spatial_b_s[:, :, :].rearrange("p h (q c) -> p h q c", c=SL),
                                  m.spatial_b[:, :, 0:SL].unsqueeze(2).to_broadcast([P, HS, SEQS, SL]))

        @block.gpsimd
        def _(pool):
            nc.gpsimd.memset(m.spatial_s[:, :, :], 0.0).then_inc(zeroed, 1)
            for x in (m.causal, m.causal_s, m.own_seq):
                nc.gpsimd.memset(x[:, :], 1.0).then_inc(base_in, 1)
            pool.wait_ge(base_in, 3)
            n = 3

            def keep(x, pattern, base, channel):
                nonlocal n
                nc.gpsimd.affine_select(out=x, in_=x, compare_op=ALU.is_ge, fill=0.0, base=base, pattern=pattern,
                                        channel_multiplier=channel).then_inc(base_in, 1)
                n += 1
                pool.wait_ge(base_in, n)

            for f in range(2):
                rows = slice(64 * f, 64 * f + 64)
                keep(m.causal[rows, :], [[1, C]], 0, -1)
                keep(m.causal_s[rows, :], [[1, TS]], 0, -1)
                keep(m.causal_s[rows, :], [[-SL, SEQS], [0, SL]], 0, 1)
                keep(m.own_seq[rows, :], [[-SL, SEQS]], 0, 1)
                keep(m.own_seq[rows, :], [[SL, SEQS]], SL - 1, -1)
            pool.wait_ge(copied, 1)
            nc.gpsimd.affine_select(out=m.spatial[:, :, :], in_=m.spatial[:, :, :], compare_op=ALU.is_ge, fill=0.0,
                                    base=0, pattern=[[0, HS], [1, P]], channel_multiplier=-1).then_inc(cut, 1)


def head_rows(f):
    return slice(64 * f, 64 * f + 64)


def phase_mixers(nc, m, pt_scratch, v_scratch, vs_scratch, mix, state_out, ident, consts):
    ctx = ExitStack()
    with ctx:
        sb = lambda n, s, d=F32: ctx.enter_context(nc.sbuf_tensor(f"gla_{n}", s, d))
        sem = phase_semaphores(nc, ctx, "gla")
        bank = lambda n: ctx.enter_context(nc.psum_tensor(f"gla_{n}_acc", [P, 512], F32))
        two = lambda n, s: [sb(f"{n}{i}", s) for i in range(2)]
        qk = two("qk", [P, 4, P])
        glr = two("glr", [RANK, P])
        vs = two("vs", [P, HS * P])
        v = two("v", [P, NCH, H * DV])
        ru = two("ru", [P, 2 * H, P])
        z, soft, logd = sb("z", [P, 2 * P]), sb("soft", [P, 2 * P]), sb("logd", [P, 2 * P])
        cum, from_mid, to_end = sb("cum", [P, 2 * P]), sb("from_mid", [P, 2 * P]), sb("to_end", [P, 2 * P])
        e_cum = two("e_cum", [P, 2 * P])
        e_q, e_k, e_end = sb("e_q", [P, 2 * P]), sb("e_k", [P, 2 * P]), sb("e_end", [P, 2 * P])
        q_state, q_in, k_in, k_end = (two(n, [P, 2, P]) for n in ("q_state", "q_in", "k_in", "k_end"))
        stats = sb("stats", [P, HS, 6])
        mv = sb("mv", [P, HS, 2])
        v_var, v_rstd = sb("v_var", [P, HS]), sb("v_rstd", [P, HS])
        vn = two("vn", [P, HS * P])
        scores = sb("scores", [P, NCH, 2, C])
        k_tok = sb("k_tok", [P, NCH, 2, DK])
        state = two("state", [P, 2, DV])
        square = sb("square", [P, 2, 2, P])
        inv = sb("inv", [P, 2, 2, P])
        normed = sb("normed", [P, 2, 2, P])
        mixed_b = sb("mixed_b", [P, HS, P])
        out = two("out", [P, 2 * H, P])
        z_acc, s_acc, t_acc, kv_acc = bank("z"), bank("s"), bank("t"), bank("kv")
        o_acc = [bank("o0"), bank("o1")]
        n_acc, m_acc = bank("n"), bank("m")

        a_in, b_in = [sem("a_in0"), sem("a_in1")], [sem("b_in0"), sem("b_in1")]
        logits = sem("logits")
        decays = sem("decays")
        softs = sem("softs")
        factors = sem("factors")
        queries, keys = sem("queries"), sem("keys")
        stat, v_power = sem("stat"), sem("v_power")
        v_normed, v_gained = sem("v_normed"), sem("v_gained")
        scored, masked = sem("scored"), sem("masked")
        k_turned, k_copied = sem("k_turned"), sem("k_copied")
        kv_made = sem("kv_made")
        states = sem("states")
        outputs = sem("outputs")
        squared, averaged, inverse = sem("squared"), sem("averaged"), sem("inverse")
        spatials = sem("spatials")
        gla_outs = sem("gla_outs")
        sgu_outs = sem("sgu_outs")
        zeroed = sem("zeroed")
        stored = [sem("stored0"), sem("stored1")]
        state_stored = sem("state_stored")
        block = ctx.enter_context(nc.Block())
        pt_view = pt_scratch.rearrange("(k p) t -> p k t", p=P)
        mix_view = mix.rearrange("(k p) t -> p k t", p=P)

        def walk_prompt(eng, step):
            step(0, 0, 0)
            step(1, 1, 0)
            with eng.Fori(1, NT // 2 - 1) as i:
                step(i * 2, 0, i)
                step(i * 2 + 1, 1, i)
            step(NT - 2, 0, NT // 2 - 1)
            step(NT - 1, 1, NT // 2 - 1)

        def more(t):
            return not known(t) or t + 1 < NT

        def old(t):
            return not known(t) or t >= 2

        def later(t):
            return not known(t) or t >= 1

        @block.sync
        def _(sp):
            def load_first(t, s):
                here = ds(t * P, P)
                if old(t):
                    sp.wait_ge(queries, t * 2 - 2)
                    sp.wait_ge(keys, t * 2 - 2)
                    sp.wait_ge(v_normed, t * 4 - 4)
                sp.dma_start(qk[s][:, :, :], pt_view[:, 0:4, here]).then_inc(a_in[s], 16)
                sp.dma_start(glr[s][:, :], pt_scratch[12 * P:12 * P + RANK, here]).then_inc(a_in[s], 16)
                sp.dma_start(vs[s][:, :], vs_scratch[here, :]).then_inc(a_in[s], 16)

            def load_second(t, s):
                here = ds(t * P, P)
                if old(t):
                    sp.wait_ge(outputs, t * 2 - 2)
                    sp.wait_ge(sgu_outs, t * 2 - 2)
                    sp.wait_ge(gla_outs, t * 4 - 4)
                for f in range(2):
                    sp.dma_start(v[s][head_rows(f), :, :], v_scratch[here, :].rearrange("(c p) n -> p c n", p=C))\
                        .then_inc(b_in[s], 16)
                sp.dma_start(ru[s][:, :, :], pt_view[:, 4:12, here]).then_inc(b_in[s], 16)

            def store(t, s):
                sp.wait_ge(sgu_outs, t * 2 + 2)
                sp.wait_ge(gla_outs, t * 4 + 4)
                sp.dma_start(mix_view[:, :, ds(t * P, P)], out[s][:, :, :]).then_inc(stored[s], 16)

            def step(t, s, i):
                if not known(t) or t + 2 < NT:
                    load_first(t + 2, s)
                if more(t):
                    load_second(t + 1, 1 - s)
                if later(t):
                    store(t - 1, 1 - s)
            load_first(0, 0)
            load_second(0, 0)
            load_first(1, 1)
            walk_prompt(sp, step)
            store(NT - 1, 1)
            sp.wait_ge(states, 4 * NT)
            for f in range(2):
                sp.dma_start(state_out.rearrange("(q f) d e -> f d q e", f=2)[f], state[0][head_rows(f), :, :])\
                    .then_inc(state_stored, 16)
            sp.wait_ge(state_stored, 32)
            for s in range(2):
                sp.wait_ge(stored[s], 16 * (NT // 2))

        @block.tensor
        def _(pe):
            def gate_logits(t, s, i):
                pe.wait_ge(a_in[s], i * 48 + 48)
                if later(t):
                    pe.wait_ge(decays, t * 5 - 4)
                for q in range(2):
                    last = nc.tensor.matmul(z_acc[:, q * P:(q + 1) * P], m.gate_w[:, q * P:(q + 1) * P], glr[s][:, :],
                                            start=True, stop=True)
                last.then_inc(logits, 1)

            def mean(t):
                pe.wait_ge(squared, t * 2 + 2)
                if later(t):
                    pe.wait_ge(inverse, t * 2 - 1)
                nc.tensor.matmul(n_acc[:, :], m.average[:, :], square[:, :, :, :].rearrange("p f q t -> p (f q t)"),
                                 start=True, stop=True).then_inc(averaged, 1)

            def step(t, s, i):
                pe.wait_ge(queries, t * 2 + 2)
                pe.wait_ge(keys, t * 2 + 2)
                if later(t):
                    pe.wait_ge(masked, t)
                    pe.wait_ge(k_copied, t)
                if more(t):
                    gate_logits(t + 1, 1 - s, i + s)
                for c in range(NCH):
                    cols = slice(c * C, c * C + C)
                    for q in range(2):
                        for f in range(2):
                            at = c * 2 + q
                            last = nc.tensor.matmul(s_acc[head_rows(f), at * C:(at + 1) * C],
                                                    k_in[s][head_rows(f), q, cols], q_in[s][head_rows(f), q, cols],
                                                    start=True, stop=True)
                last.then_inc(scored, 1)
                for c in range(NCH):
                    cols = slice(c * C, c * C + C)
                    for q in range(2):
                        for f in range(2):
                            at = c * 2 + q
                            last = nc.tensor.matmul(t_acc[head_rows(f), at * DK:(at + 1) * DK],
                                                    k_end[s][head_rows(f), q, cols],
                                                    ident[head_rows(f), 64 * f:64 * f + 64], start=True, stop=True)
                last.then_inc(k_turned, 1)
                if later(t):
                    mean(t - 1)
                pe.wait_ge(v_gained, t * 2 + 2)
                if later(t):
                    pe.wait_ge(sgu_outs, t * 2)
                for h in range(HS):
                    if h == HS // 2:
                        pe.wait_ge(b_in[s], i * 48 + 48)
                        pe.wait_ge(k_copied, t + 1)
                        if later(t):
                            pe.wait_ge(states, t * 4)
                    last = nc.tensor.matmul(m_acc[:, h * P:(h + 1) * P], vn[s][:, h * P:(h + 1) * P],
                                            m.spatial[:, h, :], start=True, stop=True)
                last.then_inc(spatials, 1)
                for c in range(NCH):
                    for q in range(2):
                        for f in range(2):
                            at, h = c * 2 + q, 2 * q + f
                            last = nc.tensor.matmul(kv_acc[head_rows(f), at * DV:(at + 1) * DV],
                                                    k_tok[head_rows(f), c, q, :],
                                                    v[s][head_rows(f), c, h * DV:(h + 1) * DV], start=True, stop=True)
                    last.then_inc(kv_made, 1)
                pe.wait_ge(masked, t + 1)
                if later(t):
                    pe.wait_ge(gla_outs, t * 4 - 2)
                for c in range(NCH):
                    if c > 0:
                        pe.wait_ge(states, t * 4 + 2)
                    cols = slice(c * C, c * C + C)
                    for q in range(2):
                        for f in range(2):
                            h = 2 * q + f
                            o = o_acc[f][:, q * P + c * C:q * P + (c + 1) * C]
                            nc.tensor.matmul(o, state[c][head_rows(f), q, :], q_state[s][head_rows(f), q, cols],
                                             start=True, stop=False)
                            last = nc.tensor.matmul(o, v[s][head_rows(f), c, h * DV:(h + 1) * DV],
                                                    scores[head_rows(f), c, q, :], start=False, stop=True)
                    last.then_inc(outputs, 1)
            pe.wait_ge(zeroed, 2)
            gate_logits(0, 0, 0)
            walk_prompt(pe, step)
            mean(NT - 1)

        @block.scalar
        def _(act):
            def soft_logs(t, s):
                act.wait_ge(decays, t * 5 + 1)
                nc.scalar.activation(soft[:, :], z[:, :], ACT.Abs).then_inc(softs, 1)
                act.wait_ge(softs, t * 3 + 1)
                nc.scalar.activation(soft[:, :], soft[:, :], ACT.Exp, scale=-1.0).then_inc(softs, 1)
                act.wait_ge(softs, t * 3 + 2)
                nc.scalar.activation(soft[:, :], soft[:, :], ACT.Ln, bias=1.0).then_inc(softs, 1)

            def exps(t, s):
                act.wait_ge(decays, t * 5 + 5)
                if old(t):
                    act.wait_ge(states, t * 4 - 4)
                if later(t):
                    act.wait_ge(queries, t * 2)
                    act.wait_ge(keys, t * 2)
                for out_, in_, sign in ((e_k, from_mid, -1.0), (e_end, to_end, 1.0), (e_q, from_mid, 1.0),
                                        (e_cum[s], cum, 1.0)):
                    nc.scalar.activation(out_[:, :], in_[:, :], ACT.Exp, scale=sign / TAU).then_inc(factors, 1)

            def inverse_norm(t):
                act.wait_ge(averaged, t + 1)
                if later(t):
                    act.wait_ge(gla_outs, t * 4 - 2)
                flat = inv[:, :, :, :].rearrange("p f q t -> p (f q t)")
                nc.scalar.activation(flat, n_acc[:, :], ACT.Ln, bias=consts[:, 0:1]).then_inc(inverse, 1)
                act.wait_ge(inverse, t * 2 + 1)
                nc.scalar.activation(flat, flat, ACT.Exp, scale=-0.5).then_inc(inverse, 1)

            def step(t, s, i):
                if more(t):
                    soft_logs(t + 1, 1 - s)
                act.wait_ge(k_turned, t + 1)
                if later(t):
                    act.wait_ge(kv_made, t * 2)
                nc.scalar.activation(k_tok[:, :, :, :].rearrange("p c q d -> p (c q d)"), t_acc[:, 0:NCH * 2 * DK],
                                     ACT.Copy).then_inc(k_copied, 1)
                if later(t):
                    inverse_norm(t - 1)
                if more(t):
                    exps(t + 1, 1 - s)
                act.wait_ge(outputs, t * 2 + 2)
                if later(t):
                    act.wait_ge(averaged, t)
                for f in range(2):
                    nc.scalar.activation(square[:, f].rearrange("p q t -> p (q t)"), o_acc[f][:, 0:2 * P],
                                         ACT.Square).then_inc(squared, 1)
            act.preload_act_table_set("natural_log_exp_and_others")
            soft_logs(0, 0)
            exps(0, 0)
            walk_prompt(act, step)
            inverse_norm(NT - 1)

        @block.gpsimd
        def _(pool):
            def make_keys(t, s):
                if old(t):
                    pool.wait_ge(outputs, t * 2 - 2)
                for i, (out_, e) in enumerate(((k_in[s], e_k), (k_end[s], e_end))):
                    pool.wait_ge(factors, t * 4 + (i + 1))
                    nc.gpsimd.tensor_tensor(out_[:, :, :], qk[s][:, 2:4, :],
                                            e[:, :].rearrange("p (q t) -> p q t", q=2), ALU.mult).then_inc(keys, 1)

            def v_tail(t, s):
                pool.wait_ge(v_normed, t * 4 + 4)
                nc.gpsimd.tensor_tensor(vn[s][:, :], vn[s][:, :], m.ln_gain[:, :], ALU.mult).then_inc(v_gained, 1)
                pool.wait_ge(v_gained, t * 2 + 1)
                nc.gpsimd.tensor_tensor(vn[s][:, :], vn[s][:, :], m.ln_bias[:, :], ALU.add).then_inc(v_gained, 1)

            def v_scale(t):
                pool.wait_ge(stat, t * 8 + 8)
                nc.gpsimd.tensor_tensor(v_var[:, :], mv[:, :, 1:2].rearrange("p h a -> p (h a)"),
                                        consts[:, 0:1].to_broadcast([P, HS]), ALU.add).then_inc(v_power, 1)
                pool.wait_ge(v_power, t * 2 + 1)
                nc.gpsimd.tensor_tensor(v_rstd[:, :], v_var[:, :], consts[:, 1:2].to_broadcast([P, HS]), ALU.pow)\
                    .then_inc(v_power, 1)

            def first(t, s):
                v_scale(t)
                make_keys(t, s)
                v_tail(t, s)
            first(0, 0)
            walk_prompt(pool, lambda t, s, i: first(t + 1, 1 - s) if more(t) else None)

        @block.vector
        def _(dve):
            def z_out(t, s):
                dve.wait_ge(logits, t + 1)
                nc.vector.tensor_tensor(z[:, :].rearrange("p (q t) -> p q t", q=2),
                                        z_acc[:, 0:2 * P].rearrange("p (q t) -> p q t", q=2),
                                        bcast(m.gate_b[:, :], P), ALU.add).then_inc(decays, 1)

            def chunks(x):
                return x[:, :].rearrange("p (a c) -> p a c", c=C)

            def log_decays(t, s):
                dve.wait_ge(stat, t * 8 + 4)
                dve.wait_ge(softs, t * 3 + 3)
                nc.vector.scalar_tensor_tensor(out=logd[:, :], in0=z[:, :], scalar=0.0, in1=soft[:, :],
                                               op0=ALU.min, op1=ALU.subtract).then_inc(decays, 1)
                for h in range(HS):
                    nc.vector.bn_aggr(mv[:, h, :], stats[:, h, :]).then_inc(stat, 1)
                dve.wait_ge(decays, t * 5 + 2)
                nc.vector.tensor_tensor_scan(out=cum[:, :], data0=m.reset[:, :], data1=logd[:, :], initial=0.0,
                                             op0=ALU.mult, op1=ALU.add).then_inc(decays, 1)
                dve.wait_ge(decays, t * 5 + 3)
                c = chunks(cum)
                nc.vector.tensor_tensor(chunks(from_mid), c, c[:, :, C // 2 - 1:C // 2].to_broadcast([P, 2 * NCH, C]),
                                        ALU.subtract).then_inc(decays, 1)
                nc.vector.tensor_tensor(chunks(to_end), c[:, :, C - 1:C].to_broadcast([P, 2 * NCH, C]), c,
                                        ALU.subtract).then_inc(decays, 1)

            def make_queries(t, s):
                if old(t):
                    dve.wait_ge(outputs, t * 2 - 2)
                for i, (out_, e) in enumerate(((q_in[s], e_q), (q_state[s], e_cum[s]))):
                    dve.wait_ge(factors, t * 4 + (i + 3))
                    nc.vector.scalar_tensor_tensor(out=out_[:, :, :].rearrange("p q t -> p (q t)"),
                                                   in0=qk[s][:, 0:2, :].rearrange("p q t -> p (q t)"),
                                                   scalar=DK ** -0.5, in1=e[:, :], op0=ALU.mult, op1=ALU.mult)\
                        .then_inc(queries, 1)

            def v_stats(t, s, i):
                dve.wait_ge(a_in[s], i * 48 + 48)
                if later(t):
                    dve.wait_ge(v_normed, t * 4)
                for h in range(HS):
                    nc.vector.bn_stats(stats[:, h, :], vs[s][:, h * P:(h + 1) * P]).then_inc(stat, 1)

            def v_norm(t, s):
                dve.wait_ge(v_power, t * 2 + 2)
                if old(t):
                    dve.wait_ge(spatials, t - 1)
                for h in range(HS):
                    nc.vector.tensor_scalar(vn[s][:, h * P:(h + 1) * P], vs[s][:, h * P:(h + 1) * P],
                                            mv[:, h, 0:1], v_rstd[:, h:h + 1], ALU.subtract, ALU.mult)\
                        .then_inc(v_normed, 1)

            def mask(t):
                nc.vector.copy_predicated(scores[:, :, :, :].rearrange("p c q i -> p (c q) i"),
                                          m.causal[:, :].bitcast(I32).unsqueeze(1).to_broadcast([P, 2 * NCH, C]),
                                          s_acc[:, 0:2 * NCH * C].rearrange("p (a i) -> p a i", i=C))\
                    .then_inc(masked, 1)

            def advance(t, s, c):
                dve.wait_ge(kv_made, t * 2 + 2)
                if c == 1:
                    dve.wait_ge(outputs, t * 2 + 1)
                elif later(t):
                    dve.wait_ge(outputs, t * 2)
                    dve.wait_ge(states, t * 4)
                if c == 1:
                    dve.wait_ge(states, t * 4 + 2)
                decay = e_cum[s][:, :].rearrange("p (q t) -> p q t", q=2)[:, :, (c + 1) * C - 1:(c + 1) * C]
                nc.vector.tensor_tensor(state[1 - c][:, :, :], state[c][:, :, :], decay.to_broadcast([P, 2, DV]),
                                        ALU.mult).then_inc(states, 1)
                dve.wait_ge(states, t * 4 + (2 * c + 1))
                nc.vector.tensor_tensor(state[1 - c][:, :, :], state[1 - c][:, :, :],
                                        kv_acc[:, c * 2 * DV:(c + 1) * 2 * DV].rearrange("p (q e) -> p q e", q=2),
                                        ALU.add).then_inc(states, 1)

            def finish_gla(t, s):
                dve.wait_ge(inverse, t * 2 + 2)
                for f in range(2):
                    nc.vector.tensor_tensor(normed[:, f], o_acc[f][:, 0:2 * P].rearrange("p (q t) -> p q t", q=2),
                                            inv[:, f], ALU.mult).then_inc(gla_outs, 1)
                for f in range(2):
                    dve.wait_ge(gla_outs, t * 4 + (f + 1))
                    heads = lambda x: x[s][:, 0:H, :].rearrange("p (q f) t -> p f q t", f=2)[:, f]
                    nc.vector.scalar_tensor_tensor(out=heads(out), in0=normed[:, f], scalar=m.gain_out[:, 0:1],
                                                   in1=heads(ru), op0=ALU.mult, op1=ALU.mult).then_inc(gla_outs, 1)

            def finish_sgu(t, s, i):
                if old(t):
                    dve.wait_ge(stored[s], i * 16)
                dve.wait_ge(spatials, t + 1)
                nc.vector.tensor_tensor(mixed_b[:, :, :], m_acc[:, :].rearrange("p (h t) -> p h t", h=HS),
                                        m.spatial_b[:, :, :], ALU.add).then_inc(sgu_outs, 1)
                dve.wait_ge(sgu_outs, t * 2 + 1)
                nc.vector.tensor_tensor(out[s][:, H:2 * H, :], mixed_b[:, :, :], ru[s][:, H:2 * H, :], ALU.mult)\
                    .then_inc(sgu_outs, 1)

            def step(t, s, i):
                dve.wait_ge(scored, t + 1)
                if later(t):
                    dve.wait_ge(outputs, t * 2)
                if more(t):
                    z_out(t + 1, 1 - s)
                mask(t)
                if more(t):
                    v_stats(t + 1, 1 - s, i + s)
                    log_decays(t + 1, 1 - s)
                if later(t):
                    finish_gla(t - 1, 1 - s)
                if more(t):
                    make_queries(t + 1, 1 - s)
                advance(t, s, 0)
                finish_sgu(t, s, i)
                advance(t, s, 1)
                if more(t):
                    v_norm(t + 1, 1 - s)

            nc.vector.memset(scores[:, :, :, :], 0.0).then_inc(zeroed, 1)
            nc.vector.memset(state[0][:, :, :], 0.0).then_inc(zeroed, 1)
            dve.wait_ge(zeroed, 2)
            z_out(0, 0)
            v_stats(0, 0, 0)
            log_decays(0, 0)
            v_norm(0, 0)
            make_queries(0, 0)
            walk_prompt(dve, step)
            finish_gla(NT - 1, 1)


def phase_mixers_sample(nc, m, pt_scratch, v_scratch, vs_scratch, mix, state_in, state_out, vn_out, ident, consts):
    ctx = ExitStack()
    with ctx:
        sb = lambda n, s, d=F32: ctx.enter_context(nc.sbuf_tensor(f"sm_{n}", s, d))
        sem = phase_semaphores(nc, ctx, "sm")
        bank = lambda n: ctx.enter_context(nc.psum_tensor(f"sm_{n}_acc", [P, 512], F32))
        W = 2 * TS
        qk, ru = sb("qk", [P, 4, TS]), sb("ru", [P, 2 * H, TS])
        glr = sb("glr", [RANK, TS])
        vs = sb("vs", [TS, HS * P])
        v = sb("v", [P, H * DV])
        state = sb("state", [P, SEQS, 2, DV])
        new_state = sb("new_state", [P, SEQS, 2, DV])
        z, soft, logd, cum = sb("z", [P, W]), sb("soft", [P, W]), sb("logd", [P, W]), sb("cum", [P, W])
        from_mid, to_end = sb("from_mid", [P, W]), sb("to_end", [P, W])
        e_cum, e_q, e_k, e_end = sb("e_cum", [P, W]), sb("e_q", [P, W]), sb("e_k", [P, W]), sb("e_end", [P, W])
        q_state, q_in, k_in, k_end = (sb(n, [P, 2, TS]) for n in ("q_state", "q_in", "k_in", "k_end"))
        stats, mv = sb("stats", [TS, HS, 6]), sb("mv", [TS, HS, 2])
        v_var, v_rstd = sb("v_var", [TS, HS]), sb("v_rstd", [TS, HS])
        vn = sb("vn", [TS, HS * P])
        scores = sb("scores", [P, 2, TS])
        k_tok = sb("k_tok", [P, 2, DK])
        k_seq = sb("k_seq", [P, 2, SEQS, DK])
        square, inv, normed = (sb(n, [P, 2, 2, TS]) for n in ("square", "inv", "normed"))
        mixed_b, out = sb("mixed_b", [P, HS, TS]), sb("out", [P, 2 * H, TS])
        kv_acc = [bank(f"kv{i}") for i in range(SEQS // 2)]
        z_acc, s_acc, t_acc, m_acc = kv_acc
        o_acc, n_acc = [bank("o0"), bank("o1")], bank("n")
        (loaded, zeroed, logits, decays, softs, factors, queries, keys, stat, v_power, v_normed, v_gained, scored,
         masked, k_turned, k_copied, k_split, kv_made, states, outputs, squared, averaged, inverse, spatials, outs,
         stored) = (sem(n) for n in (
             "loaded", "zeroed", "logits", "decays", "softs", "factors", "queries", "keys", "stat", "v_power",
             "v_normed", "v_gained", "scored", "masked", "k_turned", "k_copied", "k_split", "kv_made", "states",
             "outputs", "squared", "averaged", "inverse", "spatials", "outs", "stored"))
        state_in_sem = sem("state_in")
        block = ctx.enter_context(nc.Block())
        pt_view = pt_scratch.rearrange("(k p) t -> p k t", p=P)
        tokens = slice(TP, T)
        by_half = lambda x: x.rearrange("b (q f) d e -> f d b q e", f=2)
        LOADS = 6

        def tok_rows(f):
            return slice(64 * f, 64 * f + TS)

        @block.sync
        def _(sp):
            sp.dma_start(qk[:, :, :], pt_view[:, 0:4, tokens]).then_inc(loaded, 16)
            sp.dma_start(glr[:, :], pt_scratch[12 * P:12 * P + RANK, tokens]).then_inc(loaded, 16)
            sp.dma_start(vs[:, :], vs_scratch[tokens, :]).then_inc(loaded, 16)
            sp.dma_start(ru[:, :, :], pt_view[:, 4:12, tokens]).then_inc(loaded, 16)
            sp.wait_ge(zeroed, 1)
            for f in range(2):
                sp.dma_start(v[tok_rows(f), :], v_scratch[tokens, :]).then_inc(loaded, 16)
            for f in range(2):
                for b in range(SEQS):
                    sp.dma_start(state[head_rows(f), b, :, :], by_half(state_in)[f][:, b]).then_inc(state_in_sem, 16)
            sp.wait_ge(v_gained, 2)
            sp.dma_start(vn_out, vn[:, :]).then_inc(stored, 16)
            sp.wait_ge(states, 1 + SEQS // 2)
            for f in range(2):
                for b in range(SEQS):
                    sp.dma_start(by_half(state_out)[f][:, b], new_state[head_rows(f), b, :, :]).then_inc(stored, 16)
            sp.wait_ge(outs, 6)
            sp.dma_start(mix.rearrange("(k p) t -> p k t", p=P)[:, :, tokens], out[:, :, :]).then_inc(stored, 16)
            sp.wait_ge(stored, 16 * (2 + 2 * SEQS))

        @block.tensor
        def _(pe):
            pe.wait_ge(loaded, 16 * LOADS)
            for q in range(2):
                last = nc.tensor.matmul(z_acc[:, q * TS:(q + 1) * TS], m.gate_w[:, q * P:(q + 1) * P], glr[:, :],
                                        start=True, stop=True)
            last.then_inc(logits, 1)
            pe.wait_ge(queries, 2)
            pe.wait_ge(keys, 2)
            for q in range(2):
                for f in range(2):
                    last = nc.tensor.matmul(s_acc[tok_rows(f), q * TS:(q + 1) * TS], k_in[head_rows(f), q, :],
                                            q_in[head_rows(f), q, :], start=True, stop=True)
            last.then_inc(scored, 1)
            for q in range(2):
                for f in range(2):
                    last = nc.tensor.matmul(t_acc[tok_rows(f), q * DK:(q + 1) * DK], k_end[head_rows(f), q, :],
                                            ident[head_rows(f), 64 * f:64 * f + 64], start=True, stop=True)
            last.then_inc(k_turned, 1)
            pe.wait_ge(v_gained, 2)
            for h in range(HS):
                last = nc.tensor.matmul(m_acc[:, h * TS:(h + 1) * TS], vn[:, h * P:(h + 1) * P],
                                        m.spatial_s[:, h, :], start=True, stop=True)
            last.then_inc(spatials, 1)
            pe.wait_ge(masked, 2)
            pe.wait_ge(state_in_sem, 16 * 2 * SEQS)
            for q in range(2):
                for f in range(2):
                    h = 2 * q + f
                    nc.tensor.matmul(o_acc[f][:, q * TS:(q + 1) * TS], v[head_rows(f), h * DV:(h + 1) * DV],
                                     scores[head_rows(f), q, :], start=True, stop=False)
                    for b in range(SEQS):
                        cols = slice(b * SL, (b + 1) * SL)
                        last = nc.tensor.matmul(o_acc[f][:, q * TS + b * SL:q * TS + (b + 1) * SL],
                                                state[head_rows(f), b, q, :], q_state[head_rows(f), q, cols],
                                                start=False, stop=(b == SEQS - 1))
            last.then_inc(outputs, 1)
            pe.wait_ge(k_split, 2)
            pe.wait_ge(outs, 1)
            for b in range(SEQS):
                for q in range(2):
                    for f in range(2):
                        h, at = 2 * q + f, (b % 2) * 2 + q
                        last = nc.tensor.matmul(kv_acc[b // 2][head_rows(f), at * DV:(at + 1) * DV],
                                                k_seq[tok_rows(f), q, b, :], v[tok_rows(f), h * DV:(h + 1) * DV],
                                                start=True, stop=True)
            last.then_inc(kv_made, 1)
            pe.wait_ge(squared, 2)
            nc.tensor.matmul(n_acc[:, 0:4 * TS], m.average[:, :], square[:, :, :, :].rearrange("p f q t -> p (f q t)"),
                             start=True, stop=True).then_inc(averaged, 1)

        @block.scalar
        def _(act):
            act.preload_act_table_set("natural_log_exp_and_others")
            act.wait_ge(decays, 1)
            nc.scalar.activation(soft[:, :], z[:, :], ACT.Abs).then_inc(softs, 1)
            act.wait_ge(softs, 1)
            nc.scalar.activation(soft[:, :], soft[:, :], ACT.Exp, scale=-1.0).then_inc(softs, 1)
            act.wait_ge(softs, 2)
            nc.scalar.activation(soft[:, :], soft[:, :], ACT.Ln, bias=1.0).then_inc(softs, 1)
            act.wait_ge(decays, 5)
            for out_, in_, sign in ((e_k, from_mid, -1.0), (e_end, to_end, 1.0), (e_q, from_mid, 1.0),
                                    (e_cum, cum, 1.0)):
                nc.scalar.activation(out_[:, :], in_[:, :], ACT.Exp, scale=sign / TAU).then_inc(factors, 1)
            act.wait_ge(k_turned, 1)
            for f in range(2):
                nc.scalar.activation(k_tok[tok_rows(f), :, :].rearrange("p q d -> p (q d)"),
                                     t_acc[tok_rows(f), 0:2 * DK], ACT.Copy).then_inc(k_copied, 1)
            act.wait_ge(outputs, 1)
            for f in range(2):
                nc.scalar.activation(square[:, f].rearrange("p q t -> p (q t)"), o_acc[f][:, 0:2 * TS],
                                     ACT.Square).then_inc(squared, 1)
            act.wait_ge(averaged, 1)
            flat = inv[:, :, :, :].rearrange("p f q t -> p (f q t)")
            nc.scalar.activation(flat, n_acc[:, 0:4 * TS], ACT.Ln, bias=consts[:, 0:1]).then_inc(inverse, 1)
            act.wait_ge(inverse, 1)
            nc.scalar.activation(flat, flat, ACT.Exp, scale=-0.5).then_inc(inverse, 1)

        @block.gpsimd
        def _(pool):
            pool.wait_ge(stat, 2 * HS)
            nc.gpsimd.tensor_tensor(v_var[:, :], mv[:, :, 1:2].rearrange("p h a -> p (h a)"),
                                    consts[0:TS, 0:1].to_broadcast([TS, HS]), ALU.add).then_inc(v_power, 1)
            pool.wait_ge(v_power, 1)
            nc.gpsimd.tensor_tensor(v_rstd[:, :], v_var[:, :], consts[0:TS, 1:2].to_broadcast([TS, HS]), ALU.pow)\
                .then_inc(v_power, 1)
            pool.wait_ge(v_normed, HS)
            nc.gpsimd.tensor_tensor(vn[:, :], vn[:, :], m.ln_gain[0:TS, :], ALU.mult).then_inc(v_gained, 1)
            pool.wait_ge(v_gained, 1)
            nc.gpsimd.tensor_tensor(vn[:, :], vn[:, :], m.ln_bias[0:TS, :], ALU.add).then_inc(v_gained, 1)
            for i, (out_, e) in enumerate(((k_in, e_k), (k_end, e_end))):
                pool.wait_ge(factors, i + 1)
                nc.gpsimd.tensor_tensor(out_[:, :, :], qk[:, 2:4, :], e[:, :].rearrange("p (q t) -> p q t", q=2),
                                        ALU.mult).then_inc(keys, 1)

        @block.vector
        def _(dve):
            nc.vector.memset(v[:, :], 0.0).then_inc(zeroed, 1)
            nc.vector.memset(scores[:, :, :], 0.0).then_inc(zeroed, 1)
            dve.wait_ge(logits, 1)
            nc.vector.tensor_tensor(z[:, :].rearrange("p (q t) -> p q t", q=2),
                                    z_acc[:, 0:W].rearrange("p (q t) -> p q t", q=2),
                                    bcast(m.gate_b[:, :], TS), ALU.add).then_inc(decays, 1)
            dve.wait_ge(loaded, 16 * LOADS)
            for h in range(HS):
                nc.vector.bn_stats(stats[:, h, :], vs[:, h * P:(h + 1) * P]).then_inc(stat, 1)
            dve.wait_ge(stat, HS)
            for h in range(HS):
                nc.vector.bn_aggr(mv[:, h, :], stats[:, h, :]).then_inc(stat, 1)
            dve.wait_ge(softs, 3)
            nc.vector.scalar_tensor_tensor(out=logd[:, :], in0=z[:, :], scalar=0.0, in1=soft[:, :],
                                           op0=ALU.min, op1=ALU.subtract).then_inc(decays, 1)
            dve.wait_ge(decays, 2)
            nc.vector.tensor_tensor_scan(out=cum[:, :], data0=m.reset_s[:, :], data1=logd[:, :], initial=0.0,
                                         op0=ALU.mult, op1=ALU.add).then_inc(decays, 1)
            dve.wait_ge(decays, 3)
            chunks = lambda x: x[:, :].rearrange("p (a c) -> p a c", c=SL)
            c = chunks(cum)
            nc.vector.tensor_tensor(chunks(from_mid), c, c[:, :, SL // 2 - 1:SL // 2].to_broadcast([P, 2 * SEQS, SL]),
                                    ALU.subtract).then_inc(decays, 1)
            nc.vector.tensor_tensor(chunks(to_end), c[:, :, SL - 1:SL].to_broadcast([P, 2 * SEQS, SL]), c,
                                    ALU.subtract).then_inc(decays, 1)
            dve.wait_ge(v_power, 2)
            for h in range(HS):
                nc.vector.tensor_scalar(vn[:, h * P:(h + 1) * P], vs[:, h * P:(h + 1) * P], mv[:, h, 0:1],
                                        v_rstd[:, h:h + 1], ALU.subtract, ALU.mult).then_inc(v_normed, 1)
            for i, (out_, e) in enumerate(((q_in, e_q), (q_state, e_cum))):
                dve.wait_ge(factors, i + 3)
                nc.vector.scalar_tensor_tensor(out=out_[:, :, :].rearrange("p q t -> p (q t)"),
                                               in0=qk[:, 0:2, :].rearrange("p q t -> p (q t)"),
                                               scalar=DK ** -0.5, in1=e[:, :], op0=ALU.mult, op1=ALU.mult)\
                    .then_inc(queries, 1)
            dve.wait_ge(scored, 1)
            dve.wait_ge(zeroed, 2)
            for f in range(2):
                rows = tok_rows(f)
                nc.vector.copy_predicated(scores[rows, :, :],
                                          m.causal_s[rows, :].bitcast(I32).unsqueeze(1).to_broadcast([TS, 2, TS]),
                                          s_acc[rows, 0:W].rearrange("p (q i) -> p q i", q=2)).then_inc(masked, 1)
            dve.wait_ge(spatials, 1)
            nc.vector.tensor_tensor(mixed_b[:, :, :], m_acc[:, 0:HS * TS].rearrange("p (h t) -> p h t", h=HS),
                                    m.spatial_b_s[:, :, :], ALU.add).then_inc(outs, 1)
            dve.wait_ge(outs, 1)
            nc.vector.tensor_tensor(out[:, H:2 * H, :], mixed_b[:, :, :], ru[:, H:2 * H, :], ALU.mult).then_inc(outs, 1)
            for f in range(2):
                rows = tok_rows(f)
                dve.wait_ge(k_copied, f + 1)
                for q in range(2):
                    last = nc.vector.tensor_tensor(k_seq[rows, q], k_tok[rows, q].unsqueeze(1).to_broadcast([TS, SEQS, DK]),
                                                   bcast(m.own_seq[rows, :], DK), ALU.mult)
                last.then_inc(k_split, 1)
            dve.wait_ge(state_in_sem, 16 * 2 * SEQS)
            decay = e_cum[:, :].rearrange("p (q b c) -> p b q c", q=2, c=SL)[:, :, :, SL - 1:SL]
            nc.vector.tensor_tensor(new_state[:, :, :, :], state[:, :, :, :], decay.to_broadcast([P, SEQS, 2, DV]),
                                    ALU.mult).then_inc(states, 1)
            dve.wait_ge(kv_made, 1)
            dve.wait_ge(states, 1)
            for i in range(SEQS // 2):
                part = new_state[:, 2 * i:2 * i + 2].rearrange("p b q e -> p (b q e)")
                nc.vector.tensor_tensor(part, part, kv_acc[i][:, :], ALU.add).then_inc(states, 1)
            dve.wait_ge(inverse, 2)
            for f in range(2):
                nc.vector.tensor_tensor(normed[:, f], o_acc[f][:, 0:W].rearrange("p (q t) -> p q t", q=2),
                                        inv[:, f], ALU.mult).then_inc(outs, 1)
            for f in range(2):
                dve.wait_ge(outs, 3 + f)
                heads = lambda x: x[:, 0:H, :].rearrange("p (q f) t -> p f q t", f=2)[:, f]
                nc.vector.scalar_tensor_tensor(out=heads(out), in0=normed[:, f], scalar=m.gain_out[:, 0:1],
                                               in1=heads(ru), op0=ALU.mult, op1=ALU.mult).then_inc(outs, 1)


def build(nc, a, outs):
    dram = lambda n, s: nc.dram_tensor(n, s, F32).ap()
    pt = dram("proj_features", [13 * P, T])
    v_s = dram("proj_v", [T, H * DV])
    vs_s = dram("proj_vs", [T, HS * P])
    mix = dram("mix", [D, T])
    x1, x2 = dram("x1", [T, D]), dram("x2", [T, D])
    hidden = dram("hidden", [FF, T])
    down0 = dram("down0", [T, 512])
    x_p = a["x_prompt"][0]
    x_s = a["x_sample"].rearrange("b t d -> (b t) d")

    def x_tiles(t):
        return x_s if isinstance(t, int) and t == NT else x_p[ds(t * P, P), :]

    ctx = ExitStack()
    with ctx:
        ident = ctx.enter_context(nc.sbuf_tensor("ident", [P, P], F32))
        consts = ctx.enter_context(nc.sbuf_tensor("consts", [P, 2], F32))
        gains = ctx.enter_context(nc.sbuf_tensor("gains", [P, 3, KC], F32))
        made = ctx.enter_context(nc.semaphore("made"))
        gains_in = ctx.enter_context(nc.semaphore("gains_in"))
        with nc.Block() as block:
            @block.gpsimd
            def _(pool):
                identity(nc, ident, made)
                nc.gpsimd.memset(consts[:, 0:1], EPS)
                nc.gpsimd.memset(consts[:, 1:2], -0.5)

            @block.sync
            def _(sp):
                with nc.allow_non_contiguous_dma(reason="a gain's 1024 values, features on partitions"):
                    for i, g in enumerate(("g_mix_pre", "g_ffn_pre", "g_ple_in")):
                        sp.dma_start(gains[:, i, :], a[g][0].rearrange("(k p) -> p k", p=P)).then_inc(gains_in, 16)
                sp.wait_ge(gains_in, 48)

        with nc.sbuf_tensor("xh", [P, KC, T], F32R) as xh, nc.sbuf_tensor("xl", [P, KC, T], F32R) as xl:
            with ExitStack() as held:
                raw = [held.enter_context(nc.sbuf_tensor(f"in_raw{i}", [P, KC, P], F32)) for i in range(2)]
                raw_in = [held.enter_context(nc.semaphore(f"in_raw_in{i}")) for i in range(2)]
                w_view = a["w_in"][0].rearrange("(k p) n -> p k n", p=P)
                first_chunks = [(raw[i][:, :, :], w_view[:, :, c:c + P], raw_in[i])
                                for i, c in enumerate(in_chunks()[:2])]
                phase_norm(nc, "n1", x_tiles, xh, xl, ident, consts, ahead=first_chunks)
                phase_in(nc, xh, xl, a["w_in"][0], gains[:, 0, :], pt, v_s, vs_s, raw, raw_in)

        with ExitStack() as held:
            m = MixerConsts(nc, held)
            phase_mixer_consts(nc, a, m, ident)
            phase_mixers(nc, m, pt, v_s, vs_s, mix, outs[2][0, 0], ident, consts)
            phase_mixers_sample(nc, m, pt, v_s, vs_s, mix, a["state_gla"][0], outs[3][0],
                                outs[6][0].rearrange("b t n -> (b t) n"), ident, consts)

        x1_of = lambda t: x1[token_rows(t), :]
        phase_rows(nc, "out", mix, KC, a["w_out"][0], D, gain=a["g_mix_post"][0], residual=x_tiles, store=x1_of,
                   consts=consts)
        with ExitStack() as held:
            tail = held.enter_context(nc.sbuf_tensor("tail", [P, 2 * FC, 2 + 2 * SEQS], F32))
            wraw = [held.enter_context(nc.sbuf_tensor(f"down_ahead{i}", [P, 512], F32)) for i in range(DOWN_AHEAD)]
            wraw_in = [held.enter_context(nc.semaphore(f"down_ahead_in{i}")) for i in range(DOWN_AHEAD)]
            w_down = a["w_down"][0]
            first_chunks = [(wraw[i][:, :], w_down[i * P:(i + 1) * P, 0:512], wraw_in[i]) for i in range(DOWN_AHEAD)]
            with nc.sbuf_tensor("ffn_features", [P, 2 * FC, 20], F32) as ffn:
                phase_ffn_rows(nc, [a["state_ffn_conv"][0].rearrange("b c n -> (b c) n"), a["w_conv"][0], a["b_conv"]],
                               ffn, ident)
                with nc.sbuf_tensor("xh2", [P, KC, T], F32R) as xh, nc.sbuf_tensor("xl2", [P, KC, T], F32R) as xl:
                    phase_norm(nc, "n2", x1_of, xh, xl, ident, consts)
                    phase_up(nc, xh, xl, a["w_up"][0], gains[:, 1, :], ffn[:, :, 16:19], ffn[:, :, 19],
                             ffn[:, :, 0:16], tail, hidden, first_chunks)
            phase_down(nc, hidden, w_down, tail, outs[4][0, 0], outs[5][0].rearrange("b c n -> (b c) n"), down0,
                       a["g_ffn_post"][0], x1_of, lambda t: x2[token_rows(t), :], wraw, wraw_in, ident, consts)

        def p_tiles(t):
            if known(t) and t == NT:
                return ((slice(0, P - TS), a["p_prompt"][0, 0][TP - P + TS:TP, :]),
                        (slice(P - TS, P), a["p_sample"][0].rearrange("b t d -> (b t) d")))
            return ((slice(0, P), a["p_prompt"][0, 0][token_rows(t), :]),)

        def y_tiles(t):
            if known(t) and t == NT:
                return outs[1].rearrange("b t d -> (b t) d")
            return outs[0][0][token_rows(t), :]
        phase_ple(nc, x2, p_tiles, a["w_ple_gate"][0], gains[:, 2, :], a["w_ple"][0], a["g_ple_post"][0], y_tiles,
                  ident, consts)


_OUTS = [(1, TP, D), (SEQS, SL, D), (1, 1, H, DK, DV), (1, SEQS, H, DK, DV), (1, 1, 2, 2 * FF),
         (1, SEQS, 2, 2 * FF), (1, SEQS, SL, HS * P)]


def kernel(**inputs):
    import numpy as np
    import concourse.bacc as bacc
    from concourse.bass_utils import run_bass_kernel_spmd

    nc = bacc.Bacc("TRN2", target_bir_lowering=False, num_devices=1)
    arrays, a = {}, {}
    for name, value in inputs.items():
        value = np.ascontiguousarray(value)
        arrays[f"in_{name}"] = value
        a[name] = nc.dram_tensor(f"in_{name}", value.shape, F32, kind="ExternalInput").ap()
    outs = [nc.dram_tensor(f"out_{i}", shape, F32, kind="ExternalOutput").ap() for i, shape in enumerate(_OUTS)]
    build(nc, a, outs)
    got = run_bass_kernel_spmd(nc, [arrays], core_ids=[0])
    return tuple(got.results[0][f"out_{i}"] for i in range(len(outs)))
```

```python
import concourse.bass as bass
from concourse import mybir
from contextlib import ExitStack

F32 = mybir.dt.float32
F32R = mybir.dt.float32r
I32 = mybir.dt.int32
ALU = mybir.AluOpType
ACT = mybir.ActivationFunctionType

P = 128
D = 1024
KC = D // P
TP = 2048
SEQS, SL = 8, 4
TS = SEQS * SL
T = TP + TS
NT = TP // P
TB = 416
NBLK = T // TB
H, DK, DV = 4, 64, 128
C = 64
NCH = P // C
RANK = 16
TAU = 16.0
HS = 4
FF = 2816
FC = FF // P
PLE = 256
PC = PLE // P
EPS = 1e-6
COL_QK, COL_V, COL_R, COL_GLR = 0, 512, 1024, 1536
COL_U, COL_VS = 1552, 2064


def ds(start, size):
    return bass.ds(start, size)


def bcast(ap, n):
    return ap.unsqueeze(2).to_broadcast([ap.shape[0], ap.shape[1], n])


def tile_rows(t):
    return P if t < NT else TS


def rows_in_bank(t):
    return slice(0, P) if t < NT else slice(P - TS, P)


def identity(nc, ident, made):
    nc.gpsimd.memset(ident[:, :], 0.0).then_inc(made, 1)
    nc.gpsimd.wait_ge(made, 1)
    nc.gpsimd.affine_select(out=ident[:, :], in_=ident[:, :], compare_op=ALU.not_equal, fill=1.0,
                            base=0, pattern=[[-1, P]], channel_multiplier=1).then_inc(made, 1)


def rstd_ops(nc, pool, out, parts, tmp, consts, step, base):
    terms = list(parts) + [consts[:, 0:1]]
    for i in range(1, len(terms)):
        left = terms[0] if i == 1 else tmp
        if i > 1:
            pool.wait_ge(step, base + (i - 1))
        nc.gpsimd.tensor_tensor(tmp, left, terms[i], ALU.add).then_inc(step, 1)
    pool.wait_ge(step, base + len(parts))
    nc.gpsimd.tensor_tensor(out, tmp, consts[:, 1:2], ALU.pow).then_inc(step, 1)


def in_chunks():
    cols = [COL_V + P * i for i in range(4)] + [COL_VS + P * i for i in (2, 3, 0, 1)]
    cols += [COL_QK + P * i for i in range(4)] + [COL_R + P * i for i in range(4)]
    return cols + [COL_U + P * i for i in range(4)] + [COL_GLR]


def phase_in(nc, rows, xh, xl, w_in, gain, pt_scratch, v_scratch, vs_scratch, ident, consts):
    ctx = ExitStack()
    with ctx:
        sb = lambda n, s, d=F32: ctx.enter_context(nc.sbuf_tensor(f"in_{n}", s, d))
        sem = phase_semaphores(nc, ctx, "in")
        BANKS = 5
        SLOTS = 6
        with ExitStack() as placed:
            x = []
            for part in range(2):
                placed.enter_context(nc.sbuf_tensor(f"in_below_x{part}", [P, 4, KC, P], F32))
                x += [placed.enter_context(nc.sbuf_tensor(f"in_x{2 * part + i}", [P, D], F32)) for i in range(2)]
        wh = sb("wh", [P, SLOTS, KC, P], F32R)
        wl = sb("wl", [P, SLOTS, KC, P], F32R)
        raws = [sb(f"raw{i}", [P, KC, P]) for i in range(2)]
        outs = sb("outs", [P, BANKS * 512])
        out = [outs[:, i * 512:(i + 1) * 512] for i in range(BANKS)]
        raws += [outs[:, i * D:(i + 1) * D].rearrange("p (k c) -> p k c", k=KC) for i in range(2)]
        bank = lambda n: ctx.enter_context(nc.psum_tensor(f"in_{n}", [P, 512], F32))
        wide_acc = [bank(f"acc{i}") for i in range(4)]
        turn_acc = [bank(f"turn{i}") for i in range(4)]
        acc = wide_acc + turn_acc[:1]
        xn = [sb(f"xn{i}", [P, D]) for i in range(2)]
        total, mean, rstd = sb("total", [P, 4]), sb("mean", [P, 4]), sb("rstd", [P, 4])
        x_in = [sem(f"x_in{i}") for i in range(4)]
        x_summed, powers, scaled = sem("x_summed"), sem("powers"), sem("scaled")
        turned, x_high, x_split = sem("turned"), sem("x_high"), sem("x_split")
        raws_in = [sem(f"raw_in{i}") for i in range(4)]
        gained, gained_early, high, ready = sem("gained"), sem("gained_early"), sem("high"), sem("ready")
        summed, evacuated = sem("summed"), sem("evacuated")
        stored = [sem(f"stored{i}") for i in range(BANKS)]
        block = ctx.enter_context(nc.Block())

        wide = 2 * 4
        cols = in_chunks()
        n_chunks = len(cols)
        slot = [0, 1, 2, 3, 4, 5, 2, 3] + [n % 2 for n in range(wide, n_chunks)]
        by_vector = (1, 3)
        first_bank = 2 * (NT + 1)
        w_view = w_in.rearrange("(k p) n -> p k n", p=P)

        def raw(n):
            return raws[n if n < 4 else n % 2]

        def raw_arrived(eng, n):
            if n < 4:
                eng.wait_ge(raws_in[n], 16)
            else:
                eng.wait_ge(raws_in[n % 2], 16 * (n // 2))

        def slot_free(eng, n):
            if 4 <= n < 6:
                eng.wait_ge(scaled, NT + 1)
            if 6 <= n < wide + 2:
                eng.wait_ge(summed, NT + 1)
            elif n >= wide + 2:
                eng.wait_ge(summed, first_bank + (n - 1 - wide) * NBLK)

        @block.sync
        def _(sp):
            def load(n):
                if n >= 4:
                    sp.wait_ge(ready, n - 3 if n < 6 else n - 1)
                sp.dma_start(raw(n)[:, :, :], w_view[:, :, cols[n]:cols[n] + P])\
                    .then_inc(raws_in[n if n < 4 else n % 2], 16)

            def store(m, dst, rows, width):
                sp.wait_ge(evacuated, m + 1)
                sp.dma_start(dst, out[m % BANKS][rows, 0:width]).then_inc(stored[m % BANKS], 16)

            def load_x(t):
                if t >= 4:
                    sp.wait_ge(scaled, t - 3)
                sp.dma_start(x[t % 4][0:tile_rows(t), :], rows(t)).then_inc(x_in[t % 4], 16)

            load_x(0)
            load(0)
            load(1)
            load_x(1)
            load(2)
            load(3)
            load_x(2)
            load_x(3)
            load(4)
            load(5)
            for g, scratch in enumerate((v_scratch, vs_scratch)):
                for t in range(NT + 1):
                    if g == 0 and t + 4 <= NT:
                        load_x(t + 4)
                    if t in ((NT - 2, NT - 1), (1, 2))[g]:
                        load(6 + 2 * g + (t + g) % 2)
                    store(g * (NT + 1) + t, scratch[t * P:t * P + tile_rows(t), :], rows_in_bank(t), 512)
            for n in range(wide, n_chunks):
                if n + 2 < n_chunks:
                    load(n + 2)
                for b in range(NBLK):
                    store(first_bank + (n - wide) * NBLK + b,
                          pt_scratch[(n - wide) * P:(n - wide + 1) * P, b * TB:(b + 1) * TB], slice(0, P), TB)
            total = first_bank + (n_chunks - wide) * NBLK
            for i in range(BANKS):
                sp.wait_ge(stored[i], 16 * len(range(i, total, BANKS)))

        @block.gpsimd
        def _(pool):
            def gains(n):
                raw_arrived(pool, n)
                nc.gpsimd.tensor_tensor(raw(n)[:, :, :], raw(n)[:, :, :], bcast(gain[:, :], P),
                                        ALU.mult).then_inc(gained, 1)

            for t in range(NT + 1):
                n, q = tile_rows(t), t % 4
                pool.wait_ge(x_summed, t + 1)
                if t >= 4:
                    pool.wait_ge(scaled, t - 3)
                rstd_ops(nc, pool, rstd[0:n, q:q + 1], [total[0:n, q:q + 1]], mean[0:n, q:q + 1],
                         consts[0:n, :], powers, t * 2)
                if t in (0, 1, 5, 6):
                    gains({0: 0, 1: 2, 5: 4, 6: 5}[t])
            for n in range(6, n_chunks):
                gains(n)

        @block.vector
        def _(dve):
            def early_gain(n):
                raw_arrived(dve, n)
                nc.vector.tensor_tensor(raw(n)[:, :, :], raw(n)[:, :, :], bcast(gain[:, :], P),
                                        ALU.mult).then_inc(gained_early, 1)

            def split_w(n):
                dve.wait_ge(high, n + 1)
                nc.vector.tensor_tensor(wl[:, slot[n]], raw(n)[:, :, :], wh[:, slot[n]].bitcast(F32),
                                        ALU.subtract).then_inc(ready, 1)

            def scales(t):
                n, q = tile_rows(t), t % 4
                dve.wait_ge(powers, t * 2 + 2)
                if t >= 2:
                    dve.wait_ge(turned, t * 2 - 2)
                nc.vector.tensor_scalar(xn[t % 2][0:n, :], x[q][0:n, :], rstd[0:n, q:q + 1], None, ALU.mult)\
                    .then_inc(scaled, 1)

            def splits(t):
                n = tile_rows(t)
                for h in range(2):
                    dve.wait_ge(x_high, t * 2 + (h + 1))
                    here = (slice(None), slice(4 * h, 4 * h + 4), slice(t * P, t * P + n))
                    nc.vector.tensor_tensor(xl[here], turn_acc[t % 2 * 2 + h][:, 0:4 * n]
                                            .rearrange("p (k t) -> p k t", k=4), xh[here].bitcast(F32),
                                            ALU.subtract).then_inc(x_split, 1)

            scales(0)
            early_gain(by_vector[0])
            split_w(0)
            split_w(1)
            scales(1)
            splits(0)
            early_gain(by_vector[1])
            split_w(2)
            split_w(3)
            scales(2)
            splits(1)
            scales(3)
            for t in range(2, NT + 1):
                splits(t)
                if t + 2 <= NT:
                    scales(t + 2)
            for n in range(4, n_chunks):
                split_w(n)

        @block.scalar
        def _(act):
            def round_up(n):
                if n in by_vector:
                    act.wait_ge(gained_early, by_vector.index(n) + 1)
                else:
                    act.wait_ge(gained, n + 1 - sum(i < n for i in by_vector))
                slot_free(act, n)
                nc.scalar.activation(wh[:, slot[n]], raw(n)[:, :, :], ACT.Copy).then_inc(high, 1)

            def evacuate(m, bank, rows, width, func, acc):
                act.wait_ge(summed, m + 1)
                if m >= BANKS:
                    act.wait_ge(stored[bank], m // BANKS * 16)
                nc.scalar.activation(out[bank][rows, 0:width], acc[rows, 0:width], func)\
                    .then_inc(evacuated, 1)

            def sums(t):
                n, q = tile_rows(t), t % 4
                act.wait_ge(x_in[q], t // 4 * 16 + 16)
                if t >= 2:
                    act.wait_ge(turned, t * 2 - 2)
                nc.scalar.activation(xn[t % 2][0:n, :], x[q][0:n, :], ACT.Square, scale=D ** -0.5,
                                     accum_out=total[0:n, q:q + 1]).then_inc(x_summed, 1)

            def rounds(t):
                n = tile_rows(t)
                act.wait_ge(turned, t * 2 + 2)
                for h in range(2):
                    nc.scalar.activation(xh[:, 4 * h:4 * h + 4, t * P:t * P + n],
                                         turn_acc[t % 2 * 2 + h][:, 0:4 * n].rearrange("p (k t) -> p k t", k=4),
                                         ACT.Copy).then_inc(x_high, 1)

            sums(0)
            round_up(0)
            round_up(1)
            sums(1)
            rounds(0)
            round_up(2)
            round_up(3)
            sums(2)
            rounds(1)
            sums(3)
            for g, func in enumerate((ACT.Copy, ACT.Gelu_apprx_tanh)):
                for t in range(NT + 1):
                    m = g * (NT + 1) + t
                    if g == 0 and t == NT:
                        round_up(6)
                        round_up(7)
                    evacuate(m, m % BANKS, rows_in_bank(t), 512, func, wide_acc[m % 4])
                    if g == 0 and t + 2 <= NT:
                        rounds(t + 2)
                    if g == 0 and t + 4 <= NT:
                        sums(t + 4)
                    if g == 0 and t in (NT - 3, NT - 2):
                        round_up(t - (NT - 7))
                    if g == 1 and t == 3:
                        round_up(wide)
            for n in range(wide, n_chunks):
                func = ACT.Copy if n < wide + 4 or n == n_chunks - 1 else \
                    (ACT.Silu if n < wide + 8 else ACT.Gelu_apprx_tanh)
                for b in range(NBLK):
                    m = first_bank + (n - wide) * NBLK + b
                    evacuate(m, m % BANKS, slice(0, P), TB, func, acc[(m - first_bank) % BANKS])
                    if b == 0 and n + 1 < n_chunks:
                        round_up(n + 1)

        @block.tensor
        def _(pe):
            def turns(t):
                n = tile_rows(t)
                pe.wait_ge(scaled, t + 1)
                if t >= 2:
                    pe.wait_ge(x_split, t * 2 - 2)
                for h in range(2):
                    for k in range(4):
                        f = (4 * h + k) * P
                        last = nc.tensor.transpose(turn_acc[t % 2 * 2 + h][:, k * n:(k + 1) * n],
                                                   xn[t % 2][0:n, f:f + P], ident[0:n, 0:n])
                    last.then_inc(turned, 1)

            turns(0)
            turns(1)
            for g in range(2):
                for t in range(NT + 1):
                    m = g * (NT + 1) + t
                    first = min(t * P, T - P)
                    if t == 0:
                        pe.wait_ge(ready, 4 * g + 4)
                    if g == 0:
                        pe.wait_ge(x_split, t * 2 + 2)
                    if m >= 4:
                        pe.wait_ge(evacuated, m - 3)
                    for k in range(KC):
                        for p, (x, w) in enumerate(((xh, wh), (xh, wl), (xl, wh))):
                            last = nc.tensor.matmul(wide_acc[m % 4][:, :], x[:, k, first:first + P],
                                                    w[:, 2 * g:2 * g + 4, k, :],
                                                    start=(k == 0 and p == 0), stop=(k == KC - 1 and p == 2))
                    last.then_inc(summed, 1)
                    if g == 0 and t + 2 <= NT:
                        turns(t + 2)

            def chunk(c, s, m0):
                pe.wait_ge(ready, c + (wide + 1))
                for b in range(NBLK):
                    bank = (s * NBLK + b) % BANKS
                    if known(c) and c == 0:
                        pe.wait_ge(evacuated, min(first_bank - 1 + b, first_bank))
                    else:
                        pe.wait_ge(evacuated, m0 + b - (BANKS - 1))
                    for k in range(KC):
                        for p, (w, x) in enumerate(((wh, xh), (wh, xl), (wl, xh))):
                            last = nc.tensor.matmul(acc[bank][:, 0:TB], w[:, s, k, :],
                                                    x[:, k, b * TB:(b + 1) * TB],
                                                    start=(k == 0 and p == 0), stop=(k == KC - 1 and p == 2))
                    last.then_inc(summed, 1)
            chunk(0, 0, first_bank)
            chunk(1, 1, first_bank + NBLK)
            chunk_pairs = (n_chunks - wide) // 2
            with pe.Fori(1, chunk_pairs) as i:
                for s in range(2):
                    chunk(i * 2 + s, s, i * (2 * NBLK) + (first_bank + s * NBLK))
            chunk(2 * chunk_pairs, 0, first_bank + 2 * chunk_pairs * NBLK)


def phase_semaphores(nc, ctx, tag):
    held = []

    def clear():
        nc.clear_and_free_semaphores(held)
        nc.all_engine_barrier()
    ctx.callback(clear)

    def sem(name):
        held.append(nc.alloc_semaphore(name=f"{tag}_{name}"))
        return held[-1]
    return sem


def walk(eng, step):
    step(0, 0, 0)
    step(1, 1, 0)
    with eng.Fori(1, NT // 2 - 1) as i:
        step(i * 2, 0, i)
        step(i * 2 + 1, 1, i)
    step(NT - 2, 0, NT // 2 - 1)
    step(NT - 1, 1, NT // 2 - 1)
    step(NT, 0, NT // 2)


def walk_by_four(eng, step):
    for t in range(4):
        step(t, t, 0)
    with eng.Fori(1, NT // 4 - 1) as j:
        for q in range(4):
            step(j * 4 + q, q, j)
    for t in range(NT - 4, NT + 1):
        step(t, t % 4, t // 4)


def known(t):
    return isinstance(t, int)


def tokens_of(t):
    return slice(min(t * P, T - P), min(t * P, T - P) + P) if known(t) else ds(t * P, P)


def bank_rows(t):
    return rows_in_bank(t) if known(t) else slice(0, P)


def token_rows(t):
    return slice(t * P, t * P + tile_rows(t)) if known(t) else ds(t * P, P)


class MixerConsts:

    def __init__(self, nc, ctx):
        sb = lambda n, s: ctx.enter_context(nc.sbuf_tensor(f"mc_{n}", s, F32))
        self.average = sb("average", [P, P])
        self.gate_w = sb("gate_w", [RANK, H * DK])
        self.gate_b = sb("gate_b", [P, 2])
        self.gain_out = sb("gain_out", [P, 1])
        self.ln_gain, self.ln_bias = sb("ln_gain", [P, HS * P]), sb("ln_bias", [P, HS * P])
        self.spatial_raw = sb("spatial_raw", [P, HS, P])
        self.spatial = sb("spatial", [P, HS, P])
        self.spatial_b = sb("spatial_b", [P, HS, P])
        self.reset = sb("reset", [P, 2 * P])
        self.causal = sb("causal", [P, P])
        self.spatial_s = sb("spatial_s", [TS, HS, TS])
        self.spatial_b_s = sb("spatial_b_s", [P, HS, TS])
        self.reset_s = sb("reset_s", [P, 2 * TS])
        self.causal_s = sb("causal_s", [P, TS])
        self.own_seq = sb("own_seq", [P, SEQS])


class SampleTiles:

    def __init__(self, nc, ctx):
        sb = lambda n, s: ctx.enter_context(nc.sbuf_tensor(f"sample_{n}", s, F32))
        self.qk, self.ru, self.glr = sb("qk", [P, 4, TS]), sb("ru", [P, 2 * H, TS]), sb("glr", [RANK, TS])
        self.vs = sb("vs", [TS, HS * P])
        self.v = sb("v", [P, H * DV])
        self.state, self.new_state = sb("state", [P, SEQS, 2, DV]), sb("new_state", [P, SEQS, 2, DV])
        self.vn, self.out = sb("vn", [TS, HS * P]), sb("out", [P, 2 * H, TS])
        self.z, self.soft, self.logd, self.cum, self.from_mid, self.to_end = (
            sb(n, [P, 2 * TS]) for n in ("z", "soft", "logd", "cum", "from_mid", "to_end"))
        self.e_cum, self.e_q, self.e_k, self.e_end = (sb(n, [P, 2 * TS]) for n in ("e_cum", "e_q", "e_k", "e_end"))
        self.q_state, self.q_in, self.k_in, self.k_end = (
            sb(n, [P, 2, TS]) for n in ("q_state", "q_in", "k_in", "k_end"))
        self.stats, self.mv = sb("stats", [TS, HS, 6]), sb("mv", [TS, HS, 2])
        self.v_var, self.v_rstd = sb("v_var", [TS, HS]), sb("v_rstd", [TS, HS])
        self.scores = sb("scores", [P, 2, TS])
        self.k_tok = sb("k_tok", [P, 2, DK])
        self.k_seq = sb("k_seq", [P, 2, SEQS, DK])
        self.square, self.inv, self.normed = (sb(n, [P, 2, 2, TS]) for n in ("square", "inv", "normed"))
        self.mixed_b = sb("mixed_b", [P, HS, TS])
        self.loaded, self.state_in, self.stored, self.mix_stored = (
            ctx.enter_context(nc.semaphore(f"sample_{n}")) for n in ("loaded", "state_in", "stored", "mix_stored"))


def by_half(x):
    return x.rearrange("b (q f) d e -> f d (b q) e", f=2)


def phase_mixer_consts(nc, a, m, ident, sample, state_in, pt_scratch, v_scratch, vs_scratch, ffn_rows, features):
    n_rows, n_cols = 20, 2 * FC
    per_bank = 512 // n_rows
    ctx = ExitStack()
    with ctx:
        sem = phase_semaphores(nc, ctx, "mc")
        acc = ctx.enter_context(nc.psum_tensor("mc_acc", [P, 512], F32))
        loaded, spatial_in, turned, copied, cut, zeroed = (sem(n) for n in (
            "loaded", "spatial_in", "turned", "copied", "cut", "zeroed"))
        base_in, diag_in, filled = sem("base_in"), sem("diag_in"), sem("filled")
        rows_in, rows_turned, v_zeroed = sem("rows_in"), sem("rows_turned"), sem("v_zeroed")
        flat = ctx.enter_context(nc.sbuf_tensor("mc_flat", [n_rows, 2 * FF], F32))
        rows_acc = [ctx.enter_context(nc.psum_tensor(f"mc_rows_acc{i}", [P, 512], F32)) for i in range(2)]
        block = ctx.enter_context(nc.Block())
        pt_view = pt_scratch.rearrange("(k p) t -> p k t", p=P)
        tokens = slice(TP, T)
        b_spatial = a["b_spatial"][0]

        @block.sync
        def _(sp):
            sp.dma_start(m.spatial_raw[:, :, :], a["w_spatial"][0].rearrange("h t s -> t h s")).then_inc(spatial_in, 16)
            n = 0
            with nc.allow_non_contiguous_dma(reason="a few hundred values, features on partitions"):
                for out, src in ((m.gate_w[:, :], a["w_gla_gate"][0]),
                                 (m.gate_b[:, :], a["b_gla_gate"][0].rearrange("(c p) -> p c", p=P)),
                                 (m.gain_out[:, :], a["g_gla_out"][0].rearrange("(p c) -> p c", c=1)),
                                 (m.ln_gain[:, :], a["g_sgu_ln"][0].partition_broadcast(P)),
                                 (m.ln_bias[:, :], a["b_sgu_ln"][0].partition_broadcast(P)),
                                 (m.spatial_b[:, :, :], b_spatial.partition_broadcast(P))):
                    sp.dma_start(out, src).then_inc(loaded, 16)
                    n += 1
            at = 0
            for rows in ffn_rows:
                sp.dma_start(flat[at:at + rows.shape[0], :], rows).then_inc(rows_in, 16)
                at += rows.shape[0]
            sp.dma_start(sample.qk[:, :, :], pt_view[:, 0:4, tokens]).then_inc(sample.loaded, 16)
            sp.dma_start(sample.glr[:, :], pt_scratch[12 * P:12 * P + RANK, tokens]).then_inc(sample.loaded, 16)
            sp.dma_start(sample.vs[:, :], vs_scratch[tokens, :]).then_inc(sample.loaded, 16)
            sp.dma_start(sample.ru[:, :, :], pt_view[:, 4:12, tokens]).then_inc(sample.loaded, 16)
            for f in range(2):
                sp.dma_start(sample.state[head_rows(f)].rearrange("p b q e -> p (b q) e"), by_half(state_in)[f])\
                    .then_inc(sample.state_in, 16)
            sp.wait_ge(v_zeroed, 1)
            for f in range(2):
                sp.dma_start(sample.v[64 * f:64 * f + TS, :], v_scratch[tokens, :]).then_inc(sample.loaded, 16)
            sp.wait_ge(loaded, 16 * n)
            sp.wait_ge(cut, 1)
            sp.wait_ge(zeroed, 1)
            for q in range(SEQS):
                sp.dma_start(m.spatial_s[SL * q:SL * q + SL, :, SL * q:SL * q + SL], m.spatial[0:SL, :, 0:SL])\
                    .then_inc(diag_in, 16)
            sp.wait_ge(diag_in, 16 * SEQS)

        @block.tensor
        def _(pe):
            pe.wait_ge(spatial_in, 16)
            for h in range(HS):
                last = nc.tensor.transpose(acc[:, h * P:(h + 1) * P], m.spatial_raw[:, h, :], ident[:, :])
            last.then_inc(turned, 1)
            pe.wait_ge(rows_in, 16 * len(ffn_rows))
            for f in range(n_cols):
                b, q = divmod(f, per_bank)
                nc.tensor.transpose(rows_acc[b][:, q * n_rows:(q + 1) * n_rows], flat[:, f * P:(f + 1) * P],
                                    ident[0:n_rows, 0:n_rows]).then_inc(rows_turned, 1)

        @block.vector
        def _(dve):
            nc.vector.memset(sample.v[:, :], 0.0).then_inc(v_zeroed, 1)
            dve.wait_ge(turned, 1)
            nc.vector.tensor_copy(m.spatial[:, :, :], acc[:, :].rearrange("p (h t) -> p h t", h=HS)).then_inc(copied, 1)
            nc.vector.memset(m.average[:, :], 1.0 / DV)
            nc.vector.memset(m.reset[:, :], 1.0)
            nc.vector.memset(m.reset_s[:, :], 1.0).then_inc(filled, 1)
            dve.wait_ge(filled, 1)
            nc.vector.memset(m.reset[:, :].rearrange("p (a c) -> p a c", c=C)[:, :, 0:1], 0.0)
            nc.vector.memset(m.reset_s[:, :].rearrange("p (a c) -> p a c", c=SL)[:, :, 0:1], 0.0)
            dve.wait_ge(loaded, 16 * 6)
            nc.vector.tensor_copy(m.spatial_b_s[:, :, :].rearrange("p h (q c) -> p h q c", c=SL),
                                  m.spatial_b[:, :, 0:SL].unsqueeze(2).to_broadcast([P, HS, SEQS, SL]))
            for b in range(2):
                n = min(per_bank, n_cols - b * per_bank)
                dve.wait_ge(rows_turned, b * per_bank + n)
                nc.vector.tensor_copy(features[:, b * per_bank:b * per_bank + n, :],
                                      rows_acc[b][:, 0:n * n_rows].rearrange("p (f r) -> p f r", r=n_rows))

        @block.gpsimd
        def _(pool):
            nc.gpsimd.memset(m.spatial_s[:, :, :], 0.0).then_inc(zeroed, 1)
            for x in (m.causal, m.causal_s, m.own_seq):
                nc.gpsimd.memset(x[:, :], 1.0).then_inc(base_in, 1)
            pool.wait_ge(base_in, 3)
            n = 3

            def keep(x, pattern, base, channel):
                nonlocal n
                nc.gpsimd.affine_select(out=x, in_=x, compare_op=ALU.is_ge, fill=0.0, base=base, pattern=pattern,
                                        channel_multiplier=channel).then_inc(base_in, 1)
                n += 1
                pool.wait_ge(base_in, n)

            keep(m.causal[:, :], [[1, P]], 0, -1)
            keep(m.causal[0:C, :], [[-1, P]], C - 1, 0)
            for f in range(2):
                rows = slice(64 * f, 64 * f + 64)
                keep(m.causal_s[rows, :], [[1, TS]], 0, -1)
                keep(m.causal_s[rows, :], [[-SL, SEQS], [0, SL]], 0, 1)
                keep(m.own_seq[rows, :], [[-SL, SEQS]], 0, 1)
                keep(m.own_seq[rows, :], [[SL, SEQS]], SL - 1, -1)
            pool.wait_ge(copied, 1)
            nc.gpsimd.affine_select(out=m.spatial[:, :, :], in_=m.spatial[:, :, :], compare_op=ALU.is_ge, fill=0.0,
                                    base=0, pattern=[[0, HS], [1, P]], channel_multiplier=-1).then_inc(cut, 1)


def head_rows(f):
    return slice(64 * f, 64 * f + 64)


def walk_long_head(eng, step):
    for t in range(6):
        step(t, t % 2, t // 2)
    with eng.Fori(3, NT // 2 - 1) as i:
        step(i * 2, 0, i)
        step(i * 2 + 1, 1, i)
    for t in range(NT - 2, NT + 1):
        step(t, t % 2, t // 2)


def phase_out(nc, mix, gain, residual, store, wraw, wraw_in, m, sample, state_out, vn_out, ident, consts):
    ctx = ExitStack()
    with ctx:
        sb = lambda n, s, d=F32: ctx.enter_context(nc.sbuf_tensor(f"out_{n}", s, d))
        sem = phase_semaphores(nc, ctx, "out")
        wh, wl = sb("wh", [P, KC, D], F32R), sb("wl", [P, KC, D], F32R)
        raw = [sb(f"raw{i}", [P, KC, P]) for i in range(2)]
        sh = [sb(f"sh{i}", [P, KC, P], F32R) for i in range(2)]
        sl = [sb(f"sl{i}", [P, KC, P], F32R) for i in range(2)]
        acc = [[ctx.enter_context(nc.psum_tensor(f"out_acc{i}{h}", [P, 512], F32)) for h in range(2)]
               for i in range(2)]
        y, res = [sb(f"y{i}", [P, D]) for i in range(2)], [sb(f"res{i}", [P, D]) for i in range(2)]
        junk = [[sb(f"junk{i}{h}", [P, 512]) for h in range(2)] for i in range(2)]
        gain_rows = sb("gain_rows", [P, D])
        part = sb("part", [P, 2, 2])
        mean, rstd = sb("mean", [P, 2]), sb("rstd", [P, 2])
        whigh, wready, gain_in = sem("whigh"), sem("wready"), sem("gain_in")
        src_in, res_in = [sem("src_in0"), sem("src_in1")], [sem("res_in0"), sem("res_in1")]
        high, split, summed = sem("high"), sem("split"), sem("summed")
        stored = [sem("stored0"), sem("stored1")]
        squared, powers, finished, added = sem("squared"), sem("powers"), sem("finished"), sem("added")
        first_acc, kv_acc = (ctx.enter_context(nc.psum_tensor(f"out_{n}_acc", [P, 512], F32)) for n in ("first", "kv"))
        o_acc = [ctx.enter_context(nc.psum_tensor(f"out_o{f}_acc", [P, 512], F32)) for f in range(2)]
        W = 2 * TS
        z_acc, s_acc = first_acc[:, 0:W], first_acc[:, W:2 * W]
        t_acc, m_acc = first_acc[:, 2 * W:2 * W + 2 * DK], first_acc[:, 2 * W + 2 * DK:2 * W + 2 * DK + HS * TS]
        n_acc = first_acc[:, 0:2 * W]
        (zeroed, logits, decays, softs, factors, queries, keys, stat, v_power, v_normed, v_gained, scored,
         masked, k_turned, k_copied, k_split, kv_made, states, outputs, s_squared, averaged, inverse, spatials,
         outs) = (sem(f"s_{n}") for n in (
             "zeroed", "logits", "decays", "softs", "factors", "queries", "keys", "stat", "v_power", "v_normed",
             "v_gained", "scored", "masked", "k_turned", "k_copied", "k_split", "kv_made", "states", "outputs",
             "squared", "averaged", "inverse", "spatials", "outs"))
        LOADS = 6
        KV_PARTS = SEQS // 2
        block = ctx.enter_context(nc.Block())

        def tok_rows(f):
            return slice(64 * f, 64 * f + TS)

        src_view = mix.rearrange("(k p) t -> p k t", p=P)

        @block.sync
        def _(sp):
            def load_src(t, s):
                if not known(t) or t >= 2:
                    sp.wait_ge(split, t - 1)
                if known(t) and t == NT:
                    sp.wait_ge(sample.mix_stored, 16)
                sp.dma_start(raw[s][:, :, :], src_view[:, :, tokens_of(t)]).then_inc(src_in[s], 16)

            def load_rest(t, s):
                if not known(t) or t >= 2:
                    sp.wait_ge(added, t - 1)
                sp.dma_start(res[s][bank_rows(t), :], residual(t)).then_inc(res_in[s], 16)

            def step(t, s, i):
                if not known(t) or t + 2 <= NT:
                    load_src(t + 2, s)
                if not known(t) or t < NT:
                    load_rest(t + 1, 1 - s)
                sp.wait_ge(added, t + 1)
                sp.dma_start(store(t), y[s][bank_rows(t), :]).then_inc(stored[s], 16)
                if known(t) and t == 2:
                    sp.wait_ge(v_gained, 2)
                    sp.dma_start(vn_out, sample.vn[:, :]).then_inc(sample.stored, 16)
                if known(t) and t == 5:
                    sp.wait_ge(states, 1 + KV_PARTS)
                    for f in range(2):
                        sp.dma_start(by_half(state_out)[f],
                                     sample.new_state[head_rows(f)].rearrange("p b q e -> p (b q) e"))\
                            .then_inc(sample.stored, 16)
                    sp.wait_ge(outs, 6)
                    sp.dma_start(src_view[:, :, TP:T], sample.out[:, :, :]).then_inc(sample.mix_stored, 16)

            load_src(0, 0)
            load_src(1, 1)
            sp.dma_start(gain_rows[:, :], gain.partition_broadcast(P)).then_inc(gain_in, 16)
            load_rest(0, 0)
            walk_long_head(sp, step)
            sp.wait_ge(stored[0], 16 * (NT // 2 + 1))
            sp.wait_ge(stored[1], 16 * (NT // 2))
            sp.wait_ge(sample.stored, 16 * 3)

        @block.scalar
        def _(act):
            def rounds(t, s, i):
                act.wait_ge(src_in[s], i * 16 + 16)
                if not known(t) or t >= 2:
                    act.wait_ge(summed, (t - 1) * 2)
                nc.scalar.activation(sh[s][:, :, :], raw[s][:, :, :], ACT.Copy).then_inc(high, 1)

            def step(t, s, i):
                if not known(t) or t < NT:
                    rounds(t + 1, 1 - s, i + s)
                rows = bank_rows(t)
                if not known(t) or t >= 2:
                    act.wait_ge(powers, (t - 1) * 3)
                for h in range(2):
                    act.wait_ge(summed, t * 2 + (h + 1))
                    nc.scalar.activation(junk[s][h][rows, :], acc[s][h][rows, :], ACT.Square, scale=D ** -0.5,
                                         accum_out=part[rows, s, h:h + 1]).then_inc(squared, 1)
                if known(t):
                    sample_part(t)

            def sample_part(t):
                x = sample
                if t == 0:
                    act.wait_ge(decays, 1)
                    nc.scalar.activation(x.soft[:, :], x.z[:, :], ACT.Abs).then_inc(softs, 1)
                    act.wait_ge(softs, 1)
                    nc.scalar.activation(x.soft[:, :], x.soft[:, :], ACT.Exp, scale=-1.0).then_inc(softs, 1)
                    act.wait_ge(softs, 2)
                    nc.scalar.activation(x.soft[:, :], x.soft[:, :], ACT.Ln, bias=1.0).then_inc(softs, 1)
                    act.wait_ge(decays, 5)
                    for out_, in_, sign in ((x.e_k, x.from_mid, -1.0), (x.e_end, x.to_end, 1.0),
                                            (x.e_q, x.from_mid, 1.0), (x.e_cum, x.cum, 1.0)):
                        nc.scalar.activation(out_[:, :], in_[:, :], ACT.Exp, scale=sign / TAU).then_inc(factors, 1)
                elif t == 1:
                    act.wait_ge(masked, 2)
                    act.wait_ge(outs, 1)
                    for f in range(2):
                        nc.scalar.activation(x.k_tok[tok_rows(f), :, :].rearrange("p q d -> p (q d)"),
                                             t_acc[tok_rows(f), :], ACT.Copy).then_inc(k_copied, 1)
                elif t == 2:
                    act.wait_ge(outputs, 1)
                    for f in range(2):
                        nc.scalar.activation(x.square[:, f].rearrange("p q t -> p (q t)"), o_acc[f][:, 0:2 * TS],
                                             ACT.Square).then_inc(s_squared, 1)
                elif t == 3:
                    act.wait_ge(averaged, 1)
                    flat = x.inv[:, :, :, :].rearrange("p f q t -> p (f q t)")
                    nc.scalar.activation(flat, n_acc, ACT.Ln, bias=consts[:, 0:1]).then_inc(inverse, 1)
                    act.wait_ge(inverse, 1)
                    nc.scalar.activation(flat, flat, ACT.Exp, scale=-0.5).then_inc(inverse, 1)

            act.preload_act_table_set("natural_log_exp_and_others")
            act.wait_ge(wraw_in, 16 * KC)
            for k in range(KC):
                nc.scalar.activation(wh[:, k, :], wraw[:, k, :], ACT.Copy).then_inc(whigh, 1)
                if k == 1:
                    rounds(0, 0, 0)
            walk_long_head(act, step)

        @block.vector
        def _(dve):
            def splits(t, s):
                dve.wait_ge(high, t + 1)
                nc.vector.tensor_tensor(sl[s][:, :, :], raw[s][:, :, :], sh[s][:, :, :].bitcast(F32),
                                        ALU.subtract).then_inc(split, 1)

            def step(t, s, i):
                if not known(t) or t < NT:
                    splits(t + 1, 1 - s)
                rows = bank_rows(t)
                dve.wait_ge(powers, t * 3 + 3)
                if not known(t) or t >= 2:
                    dve.wait_ge(stored[s], i * 16)
                for h in range(2):
                    nc.vector.scalar_tensor_tensor(out=y[s][rows, 512 * h:512 * h + 512], in0=acc[s][h][rows, :],
                                                   scalar=rstd[rows, s:s + 1],
                                                   in1=gain_rows[rows, 512 * h:512 * h + 512],
                                                   op0=ALU.mult, op1=ALU.mult).then_inc(finished, 1)
                if known(t):
                    sample_part(t)

            def add_kv(i):
                dve.wait_ge(kv_made, i + 1)
                rows = sample.new_state[:, 2 * i:2 * i + 2].rearrange("p b q e -> p (b q e)")
                nc.vector.tensor_tensor(rows, rows, kv_acc[:, :], ALU.add).then_inc(states, 1)

            def sample_part(t):
                x = sample
                if t == 0:
                    nc.vector.memset(x.scores[:, :, :], 0.0).then_inc(zeroed, 1)
                    dve.wait_ge(logits, 1)
                    nc.vector.tensor_tensor(x.z[:, :].rearrange("p (q t) -> p q t", q=2),
                                            z_acc.rearrange("p (q t) -> p q t", q=2),
                                            bcast(m.gate_b[:, :], TS), ALU.add).then_inc(decays, 1)
                    dve.wait_ge(sample.loaded, 16 * LOADS)
                    for h in range(HS):
                        nc.vector.bn_stats(x.stats[:, h, :], x.vs[:, h * P:(h + 1) * P]).then_inc(stat, 1)
                    dve.wait_ge(stat, HS)
                    for h in range(HS):
                        nc.vector.bn_aggr(x.mv[:, h, :], x.stats[:, h, :]).then_inc(stat, 1)
                    dve.wait_ge(softs, 3)
                    nc.vector.scalar_tensor_tensor(out=x.logd[:, :], in0=x.z[:, :], scalar=0.0, in1=x.soft[:, :],
                                                   op0=ALU.min, op1=ALU.subtract).then_inc(decays, 1)
                    dve.wait_ge(decays, 2)
                    nc.vector.tensor_tensor_scan(out=x.cum[:, :], data0=m.reset_s[:, :], data1=x.logd[:, :],
                                                 initial=0.0, op0=ALU.mult, op1=ALU.add).then_inc(decays, 1)
                    dve.wait_ge(decays, 3)
                    chunks = lambda y: y[:, :].rearrange("p (a c) -> p a c", c=SL)
                    c = chunks(x.cum)
                    nc.vector.tensor_tensor(chunks(x.from_mid), c,
                                            c[:, :, SL // 2 - 1:SL // 2].to_broadcast([P, 2 * SEQS, SL]),
                                            ALU.subtract).then_inc(decays, 1)
                    nc.vector.tensor_tensor(chunks(x.to_end), c[:, :, SL - 1:SL].to_broadcast([P, 2 * SEQS, SL]), c,
                                            ALU.subtract).then_inc(decays, 1)
                    dve.wait_ge(v_power, 2)
                    for h in range(HS):
                        nc.vector.tensor_scalar(x.vn[:, h * P:(h + 1) * P], x.vs[:, h * P:(h + 1) * P],
                                                x.mv[:, h, 0:1], x.v_rstd[:, h:h + 1], ALU.subtract, ALU.mult)\
                            .then_inc(v_normed, 1)
                    for i, (out_, e) in enumerate(((x.q_in, x.e_q), (x.q_state, x.e_cum))):
                        dve.wait_ge(factors, i + 3)
                        nc.vector.scalar_tensor_tensor(out=out_[:, :, :].rearrange("p q t -> p (q t)"),
                                                       in0=x.qk[:, 0:2, :].rearrange("p q t -> p (q t)"),
                                                       scalar=DK ** -0.5, in1=e[:, :], op0=ALU.mult, op1=ALU.mult)\
                            .then_inc(queries, 1)
                elif t == 1:
                    dve.wait_ge(spatials, 1)
                    for f in range(2):
                        rows = tok_rows(f)
                        nc.vector.copy_predicated(x.scores[rows, :, :], m.causal_s[rows, :].bitcast(I32)
                                                  .unsqueeze(1).to_broadcast([TS, 2, TS]),
                                                  s_acc[rows, :].rearrange("p (q i) -> p q i", q=2))\
                            .then_inc(masked, 1)
                    nc.vector.tensor_tensor(x.mixed_b[:, :, :], m_acc.rearrange("p (h t) -> p h t", h=HS),
                                            m.spatial_b_s[:, :, :], ALU.add).then_inc(outs, 1)
                    dve.wait_ge(outs, 1)
                    nc.vector.tensor_tensor(x.out[:, H:2 * H, :], x.mixed_b[:, :, :], x.ru[:, H:2 * H, :], ALU.mult)\
                        .then_inc(outs, 1)
                    for f in range(2):
                        rows = tok_rows(f)
                        dve.wait_ge(k_copied, f + 1)
                        for q in range(2):
                            last = nc.vector.tensor_tensor(x.k_seq[rows, q], x.k_tok[rows, q].unsqueeze(1)
                                                           .to_broadcast([TS, SEQS, DK]),
                                                           bcast(m.own_seq[rows, :], DK), ALU.mult)
                        last.then_inc(k_split, 1)
                    dve.wait_ge(sample.state_in, 16 * 2)
                    decay = x.e_cum[:, :].rearrange("p (q b c) -> p b q c", q=2, c=SL)[:, :, :, SL - 1:SL]
                    nc.vector.tensor_tensor(x.new_state[:, :, :, :], x.state[:, :, :, :],
                                            decay.to_broadcast([P, SEQS, 2, DV]), ALU.mult).then_inc(states, 1)
                    dve.wait_ge(states, 1)
                elif t == 2:
                    add_kv(0)
                elif t == 3:
                    add_kv(1)
                    dve.wait_ge(inverse, 2)
                    for f in range(2):
                        nc.vector.tensor_tensor(x.normed[:, f], o_acc[f][:, 0:W].rearrange("p (q t) -> p q t", q=2),
                                                x.inv[:, f], ALU.mult).then_inc(outs, 1)
                    for f in range(2):
                        dve.wait_ge(outs, 3 + f)
                        heads = lambda y: y[:, 0:H, :].rearrange("p (q f) t -> p f q t", f=2)[:, f]
                        nc.vector.scalar_tensor_tensor(out=heads(x.out), in0=x.normed[:, f],
                                                       scalar=m.gain_out[:, 0:1], in1=heads(x.ru),
                                                       op0=ALU.mult, op1=ALU.mult).then_inc(outs, 1)
                elif t < 2 + KV_PARTS:
                    add_kv(t - 2)

            for k in range(KC):
                dve.wait_ge(whigh, k + 1)
                nc.vector.tensor_tensor(wl[:, k, :], wraw[:, k, :], wh[:, k, :].bitcast(F32),
                                        ALU.subtract).then_inc(wready, 1)
                if k == 1:
                    splits(0, 0)
            dve.wait_ge(gain_in, 16)
            walk_long_head(dve, step)

        @block.gpsimd
        def _(pool):
            def step(t, s, i):
                rows = bank_rows(t)
                if not known(t) or t >= 1:
                    pool.wait_ge(added, t)
                pool.wait_ge(squared, t * 2 + 2)
                if not known(t) or t >= 2:
                    pool.wait_ge(finished, (t - 1) * 2)
                rstd_ops(nc, pool, rstd[rows, s:s + 1], [part[rows, s, 0:1], part[rows, s, 1:2]],
                         mean[rows, s:s + 1], consts[rows, :], powers, t * 3)
                pool.wait_ge(res_in[s], i * 16 + 16)
                pool.wait_ge(finished, t * 2 + 2)
                nc.gpsimd.tensor_tensor(y[s][rows, :], y[s][rows, :], res[s][rows, :], ALU.add)\
                    .then_inc(added, 1)
                if known(t) and t == 0:
                    sample_part()

            def sample_part():
                x = sample
                pool.wait_ge(stat, 2 * HS)
                nc.gpsimd.tensor_tensor(x.v_var[:, :], x.mv[:, :, 1:2].rearrange("p h a -> p (h a)"),
                                        consts[0:TS, 0:1].to_broadcast([TS, HS]), ALU.add).then_inc(v_power, 1)
                pool.wait_ge(v_power, 1)
                nc.gpsimd.tensor_tensor(x.v_rstd[:, :], x.v_var[:, :], consts[0:TS, 1:2].to_broadcast([TS, HS]),
                                        ALU.pow).then_inc(v_power, 1)
                pool.wait_ge(v_normed, HS)
                nc.gpsimd.tensor_tensor(x.vn[:, :], x.vn[:, :], m.ln_gain[0:TS, :], ALU.mult).then_inc(v_gained, 1)
                pool.wait_ge(v_gained, 1)
                nc.gpsimd.tensor_tensor(x.vn[:, :], x.vn[:, :], m.ln_bias[0:TS, :], ALU.add).then_inc(v_gained, 1)
                for i, (out_, e) in enumerate(((x.k_in, x.e_k), (x.k_end, x.e_end))):
                    pool.wait_ge(factors, i + 1)
                    nc.gpsimd.tensor_tensor(out_[:, :, :], x.qk[:, 2:4, :],
                                            e[:, :].rearrange("p (q t) -> p q t", q=2), ALU.mult).then_inc(keys, 1)
            walk_long_head(pool, step)

        @block.tensor
        def _(pe):
            def step(t, s, i):
                pe.wait_ge(split, t + 1)
                if not known(t) or t >= 2:
                    pe.wait_ge(finished, (t - 1) * 2)
                for h in range(2):
                    for k in range(KC):
                        if known(t) and t == 0 and h == 0:
                            pe.wait_ge(wready, k + 1)
                        for p, (x, ww) in enumerate(((sh, wh), (sh, wl), (sl, wh))):
                            last = nc.tensor.matmul(acc[s][h][:, :], x[s][:, k, :],
                                                    ww[:, k, 512 * h:512 * h + 512],
                                                    start=(k == 0 and p == 0), stop=(k == KC - 1 and p == 2))
                    last.then_inc(summed, 1)
                if known(t):
                    sample_part(t)

            def multiply_kv(i):
                pe.wait_ge(k_split, 2)
                if i > 0:
                    pe.wait_ge(states, 1 + i)
                for b in range(2):
                    for q in range(2):
                        for f in range(2):
                            h, at = 2 * q + f, b * 2 + q
                            last = nc.tensor.matmul(kv_acc[head_rows(f), at * DV:(at + 1) * DV],
                                                    sample.k_seq[tok_rows(f), q, 2 * i + b, :],
                                                    sample.v[tok_rows(f), h * DV:(h + 1) * DV],
                                                    start=True, stop=True)
                last.then_inc(kv_made, 1)

            def sample_part(t):
                x = sample
                if t == 0:
                    pe.wait_ge(sample.loaded, 16 * LOADS)
                    for q in range(2):
                        last = nc.tensor.matmul(z_acc[:, q * TS:(q + 1) * TS], m.gate_w[:, q * P:(q + 1) * P],
                                                x.glr[:, :], start=True, stop=True)
                    last.then_inc(logits, 1)
                elif t == 1:
                    pe.wait_ge(queries, 2)
                    pe.wait_ge(keys, 2)
                    for q in range(2):
                        for f in range(2):
                            last = nc.tensor.matmul(s_acc[tok_rows(f), q * TS:(q + 1) * TS],
                                                    x.k_in[head_rows(f), q, :], x.q_in[head_rows(f), q, :],
                                                    start=True, stop=True)
                    for q in range(2):
                        for f in range(2):
                            last = nc.tensor.matmul(t_acc[tok_rows(f), q * DK:(q + 1) * DK],
                                                    x.k_end[head_rows(f), q, :],
                                                    ident[head_rows(f), 64 * f:64 * f + 64], start=True, stop=True)
                    pe.wait_ge(v_gained, 2)
                    for h in range(HS):
                        last = nc.tensor.matmul(m_acc[:, h * TS:(h + 1) * TS], x.vn[:, h * P:(h + 1) * P],
                                                m.spatial_s[:, h, :], start=True, stop=True)
                    last.then_inc(spatials, 1)
                elif t == 2:
                    pe.wait_ge(masked, 2)
                    pe.wait_ge(sample.state_in, 16 * 2)
                    for q in range(2):
                        for f in range(2):
                            h = 2 * q + f
                            nc.tensor.matmul(o_acc[f][:, q * TS:(q + 1) * TS], x.v[head_rows(f), h * DV:(h + 1) * DV],
                                             x.scores[head_rows(f), q, :], start=True, stop=False)
                            for b in range(SEQS):
                                cols = slice(b * SL, (b + 1) * SL)
                                last = nc.tensor.matmul(o_acc[f][:, q * TS + b * SL:q * TS + (b + 1) * SL],
                                                        x.state[head_rows(f), b, q, :],
                                                        x.q_state[head_rows(f), q, cols],
                                                        start=False, stop=(b == SEQS - 1))
                    last.then_inc(outputs, 1)
                    multiply_kv(0)
                elif t == 3:
                    pe.wait_ge(s_squared, 2)
                    pe.wait_ge(k_copied, 2)
                    nc.tensor.matmul(n_acc, m.average[:, :], x.square[:, :, :, :].rearrange("p f q t -> p (f q t)"),
                                     start=True, stop=True).then_inc(averaged, 1)
                    multiply_kv(1)
                elif t < 2 + KV_PARTS:
                    multiply_kv(t - 2)
            walk_long_head(pe, step)


def phase_up(nc, rows, xh, xl, w_up, gain, taps, bias, prefix, tail, h_scratch, ahead, x_area, ident, consts):
    ctx = ExitStack()
    with ctx:
        sb = lambda n, s, d=F32: ctx.enter_context(nc.sbuf_tensor(f"up_{n}", s, d))
        sem = phase_semaphores(nc, ctx, "up")
        LAST = TB - TS
        raw = [sb(f"raw{i}", [P, KC, P]) for i in range(2)]
        wh = [sb(f"wh{i}", [P, KC, P], F32R) for i in range(2)]
        wl = [sb(f"wl{i}", [P, KC, P], F32R) for i in range(2)]
        up = [sb(f"up{b}", [P, 2 + TB]) for b in range(NBLK)]
        up_s = sb("up_s", [P, SEQS, 2 + SL])
        conv = [sb(f"conv{b}", [P, TB]) for b in range(NBLK)]
        gates = sb("gates", [P, NBLK * TB])
        gate = [gates[:, b * TB:(b + 1) * TB] for b in range(NBLK)]
        x = [x_area[:, q * D:(q + 1) * D] for q in range(4)]
        xn = [gates[:, i * D:(i + 1) * D] for i in range(2)]
        square = sb("square", [P, D])
        total, mean, rstd = sb("total", [P, 4]), sb("mean", [P, 4]), sb("rstd", [P, 4])
        acc = [ctx.enter_context(nc.psum_tensor(f"up_acc{b}", [P, 512], F32)) for b in range(NBLK)]
        turn_acc = [ctx.enter_context(nc.psum_tensor(f"up_turn{b}", [P, 512], F32)) for b in range(3)] + [acc[-1]]
        x_in = [sem(f"x_in{i}") for i in range(4)]
        x_summed, powers, scaled = sem("x_summed"), sem("powers"), sem("scaled")
        turned, x_high, x_split = sem("turned"), sem("x_high"), sem("x_split")
        last_tile = [-(-(b + 1) * TB // P) - 1 for b in range(NBLK)]
        turned_to = [min(t + 5, NT) for t in last_tile]
        raw_in = [sem("raw_in0"), sem("raw_in1")]
        gained, high, ready = sem("gained"), sem("high"), sem("ready")
        summed = sem("summed")
        evacuated = sem("evacuated")
        prefixed = sem("prefixed")
        tapped = sem("tapped")
        convolved = sem("convolved")
        gated = sem("gated")
        kept = sem("kept")
        made = sem("made")
        zeroed = sem("zeroed")
        stored = [sem(f"stored{b}") for b in range(NBLK)]
        block = ctx.enter_context(nc.Block())
        w_view = w_up.rearrange("(k p) n -> p k n", p=P)

        @block.sync
        def _(sp):
            def load(j, kind, n, turn):
                if not known(n) or n >= 2:
                    sp.wait_ge(ready, n - 1)
                sp.dma_start(raw[kind][:, :, :], w_view[:, :, ds(j * P + kind * FF, P)]).then_inc(raw_in[kind], 16)

            def store(j):
                for b in range(NBLK):
                    sp.wait_ge(made, j * NBLK + (b + 1))
                    sp.dma_start(h_scratch[ds(j * P, P), b * TB:(b + 1) * TB], conv[b][:, :])\
                        .then_inc(stored[b], 16)
            load(0, 0, 0, 0)
            for t in range(NT + 1):
                if t >= 4:
                    sp.wait_ge(scaled, t - 3)
                sp.dma_start(x[t % 4][0:tile_rows(t), :], rows(t)).then_inc(x_in[t % 4], 16)
                if t == 3:
                    load(0, 1, 1, 0)
            with sp.Fori(0, FC - 1) as j:
                for kind in range(2):
                    load(j + 1, kind, j * 2 + (2 + kind), j + 1)
                store(j)
            for dst, src, arrived in ahead:
                sp.dma_start(dst, src).then_inc(arrived, 16)
            store(FC - 1)
            for b in range(NBLK):
                sp.wait_ge(stored[b], 16 * FC)

        @block.gpsimd
        def _(pool):
            def gains(n, kind, j):
                pool.wait_ge(raw_in[kind], j * 16 + 16)
                nc.gpsimd.tensor_tensor(raw[kind][:, :, :], raw[kind][:, :, :], bcast(gain, P), ALU.mult)\
                    .then_inc(gained, 1)

            def keep(j, kind):
                pool.wait_ge(evacuated, j * (2 * NBLK) + (NBLK * (kind + 1)))
                at = ds(j + kind * FC, 1)
                nc.gpsimd.tensor_copy(tail[:, at, 0:2].rearrange("p a c -> p (a c)"), up[NBLK - 1][:, LAST:LAST + 2])
                nc.gpsimd.tensor_copy(tail[:, at, 2:18].rearrange("p a (q c) -> p (a q) c", c=2),
                                      up_s[:, :, SL:SL + 2]).then_inc(kept, 1)

            def history(j, kind, n):
                if not (known(n) and n == 0):
                    pool.wait_ge(convolved, n * NBLK)
                nc.gpsimd.tensor_copy(up_s[:, :, 0:2], prefix[:, ds(j + kind * FC, 1), :]
                                      .rearrange("p a (q c) -> p (a q) c", c=2)).then_inc(prefixed, 1)

            nc.gpsimd.memset(up[0][:, 0:2], 0.0).then_inc(zeroed, 1)
            gains(0, 0, 0)
            history(0, 0, 0)
            for t in range(NT + 1):
                n, q = tile_rows(t), t % 4
                pool.wait_ge(x_summed, t + 1)
                if t >= 4:
                    pool.wait_ge(scaled, t - 3)
                rstd_ops(nc, pool, rstd[0:n, q:q + 1], [total[0:n, q:q + 1]], mean[0:n, q:q + 1],
                         consts[0:n, :], powers, t * 2)
                if t == last_tile[2]:
                    gains(None, 1, 0)
            with pool.Fori(0, FC - 1) as j:
                keep(j, 0)
                history(j, 1, j * 2 + 1)
                gains(None, 0, j + 1)
                keep(j, 1)
                history(j + 1, 0, j * 2 + 2)
                gains(None, 1, j + 1)
            keep(FC - 1, 0)
            history(FC - 1, 1, 2 * FC - 1)
            keep(FC - 1, 1)

        @block.scalar
        def _(act):
            def rounds(n, kind):
                act.wait_ge(gained, n + 1)
                if not known(n) or n >= 2:
                    act.wait_ge(summed, (n - 1) * NBLK)
                nc.scalar.activation(wh[kind][:, :, :], raw[kind][:, :, :], ACT.Copy).then_inc(high, 1)

            def block_out(j, kind, n, b, first):
                act.wait_ge(summed, n * NBLK + (b + 1))
                at = ds(j + kind * FC, 1)
                a = acc[b]
                prompt = TB if b < NBLK - 1 else LAST
                if not first:
                    act.wait_ge(convolved, (n - 1) * NBLK + (min(b + 2, NBLK)))
                    if b == NBLK - 1:
                        act.wait_ge(kept, n)
                if kind == 0:
                    if not first:
                        act.wait_ge(stored[b], j * 16)
                else:
                    act.wait_ge(gated, j * NBLK + (b + 1))
                if b == NBLK - 1:
                    act.wait_ge(prefixed, n + 1)
                nc.scalar.activation(up[b][:, 2:2 + prompt], a[:, 0:prompt], ACT.Copy)
                if b < NBLK - 1:
                    nc.scalar.activation(up[b + 1][:, 0:2], a[:, TB - 2:TB], ACT.Copy)
                else:
                    nc.scalar.activation(up_s[:, :, 2:2 + SL], a[:, LAST:TB].rearrange("p (q c) -> p q c", c=SL),
                                         ACT.Copy)
                nc.scalar.activation(conv[b][:, :], a[:, 0:TB], ACT.Identity,
                                     scale=taps[:, at, 2:3].rearrange("p a c -> p (a c)"),
                                     bias=bias[:, at]).then_inc(evacuated, 1)

            def gelu(j, b, first):
                act.wait_ge(convolved, j * (2 * NBLK) + (b + 1))
                if not first:
                    act.wait_ge(made, (j - 1) * NBLK + (b + 1))
                nc.scalar.activation(gate[b], conv[b][:, :], ACT.Gelu_apprx_tanh).then_inc(gated, 1)

            def pair(j, first, last):
                for b in range(NBLK):
                    block_out(j, 0, j * 2, b, first)
                    if b == 0:
                        rounds(j * 2 + 1, 1)
                    else:
                        gelu(j, b - 1, first)
                gelu(j, NBLK - 1, first)
                for b in range(NBLK):
                    block_out(j, 1, j * 2 + 1, b, False)
                    if b == 0 and not last:
                        rounds(j * 2 + 2, 0)

            def sums(t):
                n, q = tile_rows(t), t % 4
                act.wait_ge(x_in[q], t // 4 * 16 + 16)
                if t >= 1:
                    act.wait_ge(powers, t * 2)
                nc.scalar.activation(square[0:n, :], x[q][0:n, :], ACT.Square, scale=D ** -0.5,
                                     accum_out=total[0:n, q:q + 1]).then_inc(x_summed, 1)

            act.wait_ge(zeroed, 1)
            sums(0)
            rounds(0, 0)
            sums(1)
            sums(2)
            for t in range(NT + 1):
                if t + 3 <= NT:
                    sums(t + 3)
                n = tile_rows(t)
                for h in range(2):
                    act.wait_ge(turned, t * 2 + (h + 1))
                    nc.scalar.activation(xh[:, 4 * h:4 * h + 4, t * P:t * P + n],
                                         turn_acc[t % 2 * 2 + h][:, 0:4 * n].rearrange("p (k t) -> p k t", k=4),
                                         ACT.Copy).then_inc(x_high, 1)
                for b in range(NBLK - 1):
                    if t == turned_to[b]:
                        block_out(0, 0, 0, b, True)
            rounds(1, 1)
            block_out(0, 0, 0, NBLK - 1, True)
            for b in range(NBLK):
                gelu(0, b, True)
            for b in range(NBLK):
                block_out(0, 1, 1, b, False)
                if b == 0:
                    rounds(2, 0)
            with act.Fori(1, FC - 1) as j:
                pair(j, False, False)
            pair(FC - 1, False, True)

        @block.vector
        def _(dve):
            def splits(n, kind):
                dve.wait_ge(high, n + 1)
                nc.vector.tensor_tensor(wl[kind][:, :, :], raw[kind][:, :, :], wh[kind][:, :, :].bitcast(F32),
                                        ALU.subtract).then_inc(ready, 1)

            def convolve(j, kind, n, b, base):
                dve.wait_ge(evacuated, n * NBLK + (b + 1))
                at = ds(j + kind * FC, 1)
                prompt = TB if b < NBLK - 1 else LAST
                parts = [(conv[b][:, 0:prompt], lambda c: up[b][:, c:c + prompt])]
                if b == NBLK - 1:
                    parts.append((conv[b][:, LAST:TB].rearrange("p (q c) -> p q c", c=SL),
                                  lambda c: up_s[:, :, c:c + SL]))
                for c in (1, 0):
                    if c == 0:
                        dve.wait_ge(tapped, base + 1)
                    for i, (out, x) in enumerate(parts):
                        last = nc.vector.scalar_tensor_tensor(out=out, in0=x(c), in1=out,
                                                              scalar=taps[:, at, c:c + 1].rearrange("p a c -> p (a c)"),
                                                              op0=ALU.mult, op1=ALU.add)
                    last.then_inc(tapped if c == 1 else convolved, 1)

            def product(j, b):
                dve.wait_ge(convolved, j * (2 * NBLK) + (NBLK + b + 1))
                nc.vector.tensor_tensor(conv[b][:, :], conv[b][:, :], gate[b], ALU.mult).then_inc(made, 1)

            def pair(j, last):
                for b in range(NBLK):
                    convolve(j, 0, j * 2, b, j * (2 * NBLK) + b)
                    if b == 0:
                        splits(j * 2 + 1, 1)
                values(j, last)

            def values(j, last):
                for b in range(NBLK):
                    convolve(j, 1, j * 2 + 1, b, j * (2 * NBLK) + (NBLK + b))
                    product(j, b)
                    if b == 0 and not last:
                        splits(j * 2 + 2, 0)

            def scales(t):
                n, q = tile_rows(t), t % 4
                dve.wait_ge(powers, t * 2 + 2)
                if t >= 2:
                    dve.wait_ge(turned, t * 2 - 2)
                nc.vector.tensor_scalar(xn[t % 2][0:n, :], x[q][0:n, :], rstd[0:n, q:q + 1], None, ALU.mult)\
                    .then_inc(scaled, 1)

            scales(0)
            splits(0, 0)
            scales(1)
            for t in range(NT + 1):
                if t + 2 <= NT:
                    scales(t + 2)
                n = tile_rows(t)
                for h in range(2):
                    dve.wait_ge(x_high, t * 2 + (h + 1))
                    here = (slice(None), slice(4 * h, 4 * h + 4), slice(t * P, t * P + n))
                    nc.vector.tensor_tensor(xl[here], turn_acc[t % 2 * 2 + h][:, 0:4 * n]
                                            .rearrange("p (k t) -> p k t", k=4), xh[here].bitcast(F32),
                                            ALU.subtract).then_inc(x_split, 1)
                for b in range(NBLK - 1):
                    if t == turned_to[b]:
                        convolve(0, 0, 0, b, b)
            splits(1, 1)
            convolve(0, 0, 0, NBLK - 1, NBLK - 1)
            values(0, False)
            with dve.Fori(1, FC - 1) as j:
                pair(j, False)
            pair(FC - 1, True)

        @block.tensor
        def _(pe):
            def turns(t):
                n = tile_rows(t)
                pe.wait_ge(scaled, t + 1)
                if t >= 2:
                    pe.wait_ge(x_split, t * 2 - 2)
                for h in range(2):
                    for k in range(4):
                        f = (4 * h + k) * P
                        last = nc.tensor.transpose(turn_acc[t % 2 * 2 + h][:, k * n:(k + 1) * n],
                                                   xn[t % 2][0:n, f:f + P], ident[0:n, 0:n])
                    last.then_inc(turned, 1)

            def product(kind, b, parts=range(KC)):
                for k in parts:
                    for p, (w, x) in enumerate(((wh, xh), (wh, xl), (wl, xh))):
                        last = nc.tensor.matmul(acc[b][:, 0:TB], w[kind][:, k, :], x[:, k, b * TB:(b + 1) * TB],
                                                start=(k == 0 and p == 0), stop=(k == KC - 1 and p == 2))
                if k == KC - 1:
                    last.then_inc(summed, 1)

            def chunk(n, kind):
                pe.wait_ge(ready, n + 1)
                for b in range(NBLK):
                    pe.wait_ge(evacuated, (n - 1) * NBLK + (b + 1))
                    product(kind, b)

            for t in range(turned_to[0] - 2):
                turns(t)
            pe.wait_ge(ready, 1)
            pieces = (range(0, 3), range(3, 6), range(6, KC))
            for b in range(NBLK):
                tiles = list(range((turned_to[b - 1] if b else turned_to[0] - 3) + 1, turned_to[b] + 1))
                pe.wait_ge(x_split, last_tile[b] * 2 + 2)
                for i, parts in enumerate(pieces):
                    product(0, b, parts)
                    if i < len(tiles):
                        turns(tiles[i])
            chunk(1, 1)
            with pe.Fori(1, FC) as j:
                for kind in range(2):
                    chunk(j * 2 + kind, kind)


def walk_twice(eng, step, between):
    walk(eng, lambda t, s, i: step(0, t, t, s, i))
    between()
    walk(eng, lambda t, s, i: step(1, t, t + (NT + 1), 1 - s, i + (NT // 2 + s)))


DOWN_AHEAD = 8


def phase_down(nc, hidden, w, tail, prompt_out, sample_out, scratch, gain, residual, store, wraw, wraw_in,
               spare, ahead, ident, consts):
    ctx = ExitStack()
    with ctx:
        sb = lambda n, s, d=F32: ctx.enter_context(nc.sbuf_tensor(f"down_{n}", s, d))
        bank = lambda n: ctx.enter_context(nc.psum_tensor(f"down_{n}", [P, 512], F32))
        sem = phase_semaphores(nc, ctx, "down")
        W = 512
        wraw, wraw_in = wraw + [spare[:, 0:W]], wraw_in + [sem("wraw_in")]
        R = len(wraw)
        wh, wl = sb("wh", [P, FC, W], F32R), sb("wl", [P, FC, W], F32R)
        raw = [sb(f"raw{i}", [P, FC, P]) for i in range(2)]
        sh = [sb(f"sh{i}", [P, FC, P], F32R) for i in range(2)]
        sl = [sb(f"sl{i}", [P, FC, P], F32R) for i in range(2)]
        y = [sb(f"y{i}", [P, D]) for i in range(2)]
        area = sb("area", [P, 2 * FF])
        n_rows, groups = 2 + 2 * SEQS, 2 * FC // 4
        tail_rows = area[0:n_rows, :]
        res = [area[:, i * D:(i + 1) * D] for i in range(2)]
        half = [area[:, 2 * D + i * W:2 * D + (i + 1) * W] for i in range(2)]
        junk = [area[:, 3 * D + i * W:3 * D + (i + 1) * W] for i in range(2)]
        gain_rows = area[:, 4 * D:5 * D]
        part = sb("part", [P, 2, 2])
        mean, rstd = sb("mean", [P, 2]), sb("rstd", [P, 2])
        acc, tail_acc = [bank("acc0"), bank("acc1")], [bank(f"tail_acc{i}") for i in range(4)]
        whigh, wready, used = sem("whigh"), sem("wready"), sem("used")
        src_in = [sem("src_in0"), sem("src_in1")]
        high, split, summed = sem("high"), sem("split"), sem("summed")
        copied = sem("copied")
        stored = [sem("stored0"), sem("stored1")]
        tail_turned, tail_copied, tail_stored = sem("tail_turned"), sem("tail_copied"), sem("tail_stored")
        gain_in = sem("gain_in")
        res_in, half_in = [sem("res_in0"), sem("res_in1")], [sem("half_in0"), sem("half_in1")]
        squared, powers = sem("squared"), sem("powers")
        finished = sem("finished")
        added = sem("added")
        block = ctx.enter_context(nc.Block())
        w_view = w.rearrange("(k p) n -> p k n", p=P)
        src_view = hidden.rearrange("(k p) t -> p k t", p=P)

        def two_back(half_no, t):
            return half_no == 1 or not known(t) or t >= 2

        def tail_groups(t):
            return {0: range(0, 4), 1: range(4, 8), NT - 2: range(8, groups)}.get(t, ()) if known(t) else ()

        def products_done(eng, half_no, t, g):
            if half_no == 0 and known(t) and t == NT:
                eng.wait_ge(used, FC)
            else:
                eng.wait_ge(summed, g + 1 if half_no == 0 else g)

        @block.sync
        def _(sp):
            def load_w(n):
                if n >= R:
                    sp.wait_ge(wready, n - (R - 1))
                c = n // FC * W
                sp.dma_start(wraw[n % R], w_view[:, n % FC, c:c + W]).then_inc(wraw_in[n % R], 16)

            def load_src(t, g, s):
                if not known(g) or g >= 2:
                    sp.wait_ge(split, g - 1)
                sp.dma_start(raw[s][:, :, :], src_view[:, :, tokens_of(t)]).then_inc(src_in[s], 16)

            def load_rest(t, s):
                if not known(t) or t >= 2:
                    sp.wait_ge(added, t - 1)
                sp.dma_start(res[s][bank_rows(t), :], residual(t)).then_inc(res_in[s], 16)
                sp.dma_start(half[s][bank_rows(t), :], scratch[token_rows(t), :]).then_inc(half_in[s], 16)

            def step(half_no, t, g, s, u):
                if not known(t) or t + 2 <= NT:
                    load_src(t + 2, g + 2, s)
                elif half_no == 0:
                    load_src(t + 1 - NT, g + 2, s)
                if half_no == 0:
                    if known(t) and t == NT - 1:
                        sp.wait_ge(tail_copied, groups)
                        sp.dma_start(prompt_out, tail_rows[0:2, :]).then_inc(tail_stored, 16)
                        sp.dma_start(sample_out, tail_rows[2:n_rows, :]).then_inc(tail_stored, 16)
                    if known(t) and t == 1:
                        for n in range(FC, FC + R):
                            load_w(n)
                    if known(t) and t == NT:
                        for n in range(FC + R, 2 * FC):
                            load_w(n)
                    sp.wait_ge(copied, t + 1)
                    sp.dma_start(scratch[token_rows(t), :], y[s][bank_rows(t), 0:W]).then_inc(stored[s], 16)
                else:
                    if not known(t) or t < NT:
                        load_rest(t + 1, s)
                    if known(t) and t == 1:
                        sp.wait_ge(wready, 2 * FC)
                        for dst, src, arrived in ahead:
                            sp.dma_start(dst, src).then_inc(arrived, 16)
                    sp.wait_ge(added, t + 1)
                    sp.dma_start(store(t), y[s][bank_rows(t), :]).then_inc(stored[s], 16)

            def between():
                sp.wait_ge(tail_stored, 32)
                sp.dma_start(gain_rows, gain.partition_broadcast(P)).then_inc(gain_in, 16)
                sp.wait_ge(stored[0], 16 * (NT // 2 + 1))
                sp.wait_ge(stored[1], 16 * (NT // 2))
                load_rest(0, 0)

            load_src(0, 0, 0)
            for n in range(DOWN_AHEAD, FC):
                load_w(n)
            load_src(1, 1, 1)
            walk_twice(sp, step, between)
            sp.wait_ge(stored[0], 16 * (NT + 1))
            sp.wait_ge(stored[1], 16 * (NT + 1))

        @block.scalar
        def _(act):
            def round_w(n):
                act.wait_ge(wraw_in[n % R], 16 * (n // R + 1))
                if n >= FC:
                    act.wait_ge(used, n - (FC - 1))
                nc.scalar.activation(wh[:, n % FC, :], wraw[n % R], ACT.Copy).then_inc(whigh, 1)

            def rounds(half_no, t, g, s, u):
                act.wait_ge(src_in[s], u * 16 + 16)
                if two_back(half_no, t):
                    if half_no == 1 and known(t) and t < 2:
                        products_done(act, 0, NT - 1 + t, g - 2)
                    else:
                        products_done(act, half_no, t - 2, g - 2)
                nc.scalar.activation(sh[s][:, :, :], raw[s][:, :, :], ACT.Copy).then_inc(high, 1)

            def step(half_no, t, g, s, u):
                if not known(t) or t < NT:
                    rounds(half_no, t + 1, g + 1, 1 - s, u + s)
                elif half_no == 0:
                    rounds(1, 0, g + 1, 1 - s, u + s)
                    for n in range(FC, 2 * FC):
                        round_w(n)
                rows = bank_rows(t)
                if half_no == 0:
                    products_done(act, 0, t, g)
                    if two_back(half_no, t):
                        act.wait_ge(stored[s], u * 16)
                    nc.scalar.activation(y[s][rows, 0:W], acc[s][rows, :], ACT.Copy).then_inc(copied, 1)
                    return
                q = 1 - s
                if not known(t) or t >= 1:
                    act.wait_ge(powers, t * 3)
                act.wait_ge(half_in[q], (u - NT // 2 - q) * 16 + 16)
                nc.scalar.activation(junk[0][rows, :], half[q][rows, :], ACT.Square, scale=D ** -0.5,
                                     accum_out=part[rows, q, 0:1]).then_inc(squared, 1)
                products_done(act, 1, t, g)
                nc.scalar.activation(junk[1][rows, :], acc[s][rows, :], ACT.Square, scale=D ** -0.5,
                                     accum_out=part[rows, q, 1:2]).then_inc(squared, 1)

            for n in range(FC):
                round_w(n)
                if n == 1:
                    rounds(0, 0, 0, 0, 0)
            walk_twice(act, step, lambda: act.wait_ge(tail_stored, 32))

        @block.vector
        def _(dve):
            def split_w(n):
                dve.wait_ge(whigh, n + 1)
                nc.vector.tensor_tensor(wl[:, n % FC, :], wraw[n % R], wh[:, n % FC, :].bitcast(F32),
                                        ALU.subtract).then_inc(wready, 1)

            def splits(g, s):
                dve.wait_ge(high, g + 1)
                nc.vector.tensor_tensor(sl[s][:, :, :], raw[s][:, :, :], sh[s][:, :, :].bitcast(F32),
                                        ALU.subtract).then_inc(split, 1)

            def step(half_no, t, g, s, u):
                if not known(t) or t < NT or half_no == 0:
                    splits(g + 1, 1 - s)
                if half_no == 0:
                    for gr in tail_groups(t):
                        dve.wait_ge(tail_turned, gr + 1)
                        nc.vector.tensor_copy(tail_rows[:, gr * 512:(gr + 1) * 512],
                                              tail_acc[gr % 4][0:n_rows, :]).then_inc(tail_copied, 1)
                    if known(t) and t == NT:
                        for n in range(FC, 2 * FC):
                            split_w(n)
                    return
                rows, q = bank_rows(t), 1 - s
                dve.wait_ge(powers, t * 3 + 3)
                dve.wait_ge(stored[s], u * 16)
                for h, half_row in enumerate((half[q], acc[s])):
                    nc.vector.scalar_tensor_tensor(out=y[s][rows, W * h:W * h + W], in0=half_row[rows, :],
                                                   scalar=rstd[rows, q:q + 1],
                                                   in1=gain_rows[rows, W * h:W * h + W],
                                                   op0=ALU.mult, op1=ALU.mult).then_inc(finished, 1)

            split_w(0)
            split_w(1)
            splits(0, 0)
            for n in range(2, FC):
                split_w(n)
            walk_twice(dve, step, lambda: dve.wait_ge(gain_in, 16))

        @block.gpsimd
        def _(pool):
            def step(t, q, i):
                rows = bank_rows(t)
                s = 1 - q
                if not known(t) or t >= 1:
                    pool.wait_ge(added, t)
                pool.wait_ge(squared, t * 2 + 2)
                if not known(t) or t >= 2:
                    pool.wait_ge(finished, (t - 1) * 2)
                rstd_ops(nc, pool, rstd[rows, q:q + 1], [part[rows, q, 0:1], part[rows, q, 1:2]],
                         mean[rows, q:q + 1], consts[rows, :], powers, t * 3)
                pool.wait_ge(res_in[q], i * 16 + 16)
                pool.wait_ge(finished, t * 2 + 2)
                nc.gpsimd.tensor_tensor(y[s][rows, :], y[s][rows, :], res[q][rows, :], ALU.add)\
                    .then_inc(added, 1)
            walk(pool, step)

        @block.tensor
        def _(pe):
            def step(half_no, t, g, s, u):
                pe.wait_ge(split, g + 1)
                if half_no == 0 and two_back(0, t):
                    pe.wait_ge(copied, g - 1)
                elif half_no == 1 and known(t) and t < 2:
                    pe.wait_ge(copied, g - 1)
                elif half_no == 1:
                    pe.wait_ge(finished, (t - 1) * 2)
                first, last_left = known(t) and t == 0, half_no == 0 and known(t) and t == NT
                for k in range(FC):
                    if first:
                        pe.wait_ge(wready, half_no * FC + k + 1)
                    for p, (x, ww) in enumerate(((sh, wh), (sh, wl), (sl, wh))):
                        last = nc.tensor.matmul(acc[s][:, :], x[s][:, k, :], ww[:, k, :],
                                                start=(k == 0 and p == 0), stop=(k == FC - 1 and p == 2))
                    if last_left:
                        last.then_inc(used, 1)
                if not last_left:
                    last.then_inc(summed, 1)
                for gr in tail_groups(t) if half_no == 0 else ():
                    if gr >= 4:
                        pe.wait_ge(tail_copied, gr - 3)
                    for q in range(4):
                        last = nc.tensor.transpose(tail_acc[gr % 4][0:n_rows, q * P:(q + 1) * P],
                                                   tail[:, 4 * gr + q, :], ident[:, :])
                    last.then_inc(tail_turned, 1)
            walk_twice(pe, step, lambda: None)


PLE_AHEAD = 4


def phase_ple(nc, x, p_tiles, w_gate, gate_gain, w_ple, gain, y_tiles, wraw, wraw_in, ident, consts):
    ctx = ExitStack()
    with ctx:
        sb = lambda n, s, d=F32: ctx.enter_context(nc.sbuf_tensor(f"ple_{n}", s, d))
        sem = phase_semaphores(nc, ctx, "ple")
        bank = lambda n: ctx.enter_context(nc.psum_tensor(f"ple_{n}_acc", [P, 512], F32))
        two = lambda n, s, d=F32: [sb(f"{n}{i}", s, d) for i in range(2)]
        K2 = KC + PC
        wh, wl = sb("wh", [P, K2, D], F32R), sb("wl", [P, K2, D], F32R)
        xt = [sb(f"x{i}", [P, D]) for i in range(4)]
        pt, xn = two("p", [P, PLE]), two("xn", [P, D])
        junk = two("junk", [P, D])
        sh, sl = two("sh", [P, K2, P], F32R), two("sl", [P, K2, P], F32R)
        gate, e, y = two("gate", [P, D]), two("e", [P, D]), two("y", [P, D])
        gain_rows = sb("gain_rows", [P, D])
        total, mean, rstd = sb("total", [P, 2]), sb("mean", [P, 2]), sb("rstd", [P, 2])
        total2, mean2, rstd2 = sb("total2", [P, 2]), sb("mean2", [P, 2]), sb("rstd2", [P, 2])
        turn_acc = [bank("turn0"), bank("turn1"), bank("turn2")]
        gate_acc, ple_acc = [bank("gate0"), bank("gate1")], [bank("ple0"), bank("ple1")]
        x_in, p_in = [sem(f"x_in{i}") for i in range(4)], [sem("p_in0"), sem("p_in1")]
        gain_in = sem("gain_in")
        whigh, wready = sem("whigh"), sem("wready")
        summed, powers, scaled = sem("summed"), sem("powers"), sem("scaled")
        turned, high, split = sem("turned"), sem("high"), sem("split")
        gates, ples = sem("gates"), sem("ples")
        opened, gated = sem("opened"), sem("gated")
        squared, powers2, finished, added = sem("squared"), sem("powers2"), sem("finished"), sem("added")
        stored = [sem("stored0"), sem("stored1")]
        block = ctx.enter_context(nc.Block())
        sizes = (4, 4, PC)
        starts = (0, 4, 8)

        @block.sync
        def _(sp):
            def load_w(k):
                if k >= PLE_AHEAD:
                    sp.wait_ge(wready, k - (PLE_AHEAD - 1))
                src = w_gate[k * P:(k + 1) * P, :] if k < KC else w_ple[(k - KC) * P:(k - KC + 1) * P, :]
                sp.dma_start(wraw[k % PLE_AHEAD], src).then_inc(wraw_in[k % PLE_AHEAD], 16)

            def load(t, q):
                if not known(t) or t >= 4:
                    sp.wait_ge(added, t - 3)
                sp.dma_start(xt[q][:, :], x[tokens_of(t), :]).then_inc(x_in[q], 16)
                if not known(t) or t >= 2:
                    sp.wait_ge(turned, t * 3 - 3)
                for rows, src in p_tiles(t):
                    sp.dma_start(pt[q % 2][rows, :], src).then_inc(p_in[q % 2], 16)

            def step(t, q, j):
                s = q % 2
                if not known(t) or t + 3 <= NT:
                    load(t + 3, (q + 3) % 4)
                sp.wait_ge(added, t + 1)
                sp.dma_start(y_tiles(t), y[s][bank_rows(t), :]).then_inc(stored[s], 16)

            sp.dma_start(gain_rows[:, :], gain.partition_broadcast(P)).then_inc(gain_in, 16)
            load(0, 0)
            load(1, 1)
            for k in range(PLE_AHEAD, K2):
                load_w(k)
            load(2, 2)
            walk_by_four(sp, step)
            sp.wait_ge(stored[0], 16 * (NT // 2 + 1))
            sp.wait_ge(stored[1], 16 * (NT // 2))

        @block.scalar
        def _(act):
            def squares(t, q, j):
                s = q % 2
                act.wait_ge(x_in[q], j * 16 + 16)
                if not known(t) or t >= 2:
                    act.wait_ge(powers, t * 2 - 2)
                nc.scalar.activation(junk[s][:, :], xt[q][:, :], ACT.Square, scale=D ** -0.5,
                                     accum_out=total[:, s:s + 1]).then_inc(summed, 1)

            def rounds(t, s):
                for g in range(3):
                    act.wait_ge(turned, t * 3 + (g + 1))
                    if g == 0 and (not known(t) or t >= 2):
                        act.wait_ge(ples, t * 2 - 2)
                    n = sizes[g]
                    nc.scalar.activation(sh[s][:, starts[g]:starts[g] + n, :],
                                         turn_acc[g][:, 0:n * P].rearrange("p (k t) -> p k t", k=n),
                                         ACT.Copy).then_inc(high, 1)

            def open_gate(t, s, h):
                act.wait_ge(gates, t * 2 + (h + 1))
                if not known(t) or t >= 2:
                    act.wait_ge(gated, (t - 1) * 2)
                nc.scalar.activation(gate[s][:, 512 * h:512 * h + 512], gate_acc[h][:, :], ACT.Sigmoid)\
                    .then_inc(opened, 1)

            def step(t, q, j):
                s = q % 2
                if not known(t) or t + 2 <= NT:
                    squares(t + 2, (q + 2) % 4, j + q // 2)
                open_gate(t, s, 0)
                if not known(t) or t < NT:
                    rounds(t + 1, 1 - s)
                open_gate(t, s, 1)
                act.wait_ge(gated, t * 2 + 2)
                if not known(t) or t >= 2:
                    act.wait_ge(powers2, t * 2 - 2)
                nc.scalar.activation(junk[s][:, :], e[s][:, :], ACT.Square, scale=D ** -0.5,
                                     accum_out=total2[:, s:s + 1]).then_inc(squared, 1)

            squares(0, 0, 0)
            for k in range(K2):
                act.wait_ge(wraw_in[k % PLE_AHEAD], 16 * (k // PLE_AHEAD + 1))
                scale = gate_gain[:, k:k + 1] if k < KC else 1.0
                nc.scalar.activation(wh[:, k, :], wraw[k % PLE_AHEAD], ACT.Copy, scale=scale).then_inc(whigh, 1)
                if k == 1:
                    rounds(0, 0)
                    squares(1, 1, 0)
            walk_by_four(act, step)

        @block.gpsimd
        def _(pool):
            def inner(t, s):
                pool.wait_ge(summed, t + 1)
                if not known(t) or t >= 2:
                    pool.wait_ge(scaled, t - 1)
                rstd_ops(nc, pool, rstd[:, s:s + 1], [total[:, s:s + 1]], mean[:, s:s + 1], consts, powers, t * 2)

            def step(t, q, j):
                s = q % 2
                if not known(t) or t + 2 <= NT:
                    inner(t + 2, s)
                pool.wait_ge(squared, t + 1)
                if not known(t) or t >= 2:
                    pool.wait_ge(finished, t - 1)
                rstd_ops(nc, pool, rstd2[:, s:s + 1], [total2[:, s:s + 1]], mean2[:, s:s + 1], consts, powers2,
                         t * 2)
                pool.wait_ge(finished, t + 1)
                nc.gpsimd.tensor_tensor(y[s][:, :], y[s][:, :], xt[q][:, :], ALU.add).then_inc(added, 1)
            inner(0, 0)
            inner(1, 1)
            walk_by_four(pool, step)

        @block.vector
        def _(dve):
            def scale(t, q):
                s = q % 2
                dve.wait_ge(powers, t * 2 + 2)
                if not known(t) or t >= 2:
                    dve.wait_ge(turned, t * 3 - 3)
                nc.vector.tensor_scalar(xn[s][:, :], xt[q][:, :], rstd[:, s:s + 1], None, ALU.mult)\
                    .then_inc(scaled, 1)

            def splits(t, s):
                for g in range(3):
                    dve.wait_ge(high, t * 3 + (g + 1))
                    n = sizes[g]
                    here = (slice(None), slice(starts[g], starts[g] + n), slice(None))
                    nc.vector.tensor_tensor(sl[s][here], turn_acc[g][:, 0:n * P].rearrange("p (k t) -> p k t", k=n),
                                            sh[s][here].bitcast(F32), ALU.subtract).then_inc(split, 1)

            def step(t, q, j):
                s = q % 2
                if not known(t) or t + 2 <= NT:
                    scale(t + 2, (q + 2) % 4)
                if not known(t) or t < NT:
                    splits(t + 1, 1 - s)
                for h in range(2):
                    dve.wait_ge(ples, t * 2 + (h + 1))
                    dve.wait_ge(opened, t * 2 + (h + 1))
                    if not known(t) or t >= 2:
                        dve.wait_ge(finished, t - 1)
                    nc.vector.tensor_tensor(e[s][:, 512 * h:512 * h + 512], ple_acc[h][:, :],
                                            gate[s][:, 512 * h:512 * h + 512], ALU.mult).then_inc(gated, 1)
                dve.wait_ge(powers2, t * 2 + 2)
                if not known(t) or t >= 2:
                    dve.wait_ge(stored[s], j * 32 + (q // 2) * 16)
                nc.vector.scalar_tensor_tensor(out=y[s][:, :], in0=e[s][:, :], scalar=rstd2[:, s:s + 1],
                                               in1=gain_rows[:, :], op0=ALU.mult, op1=ALU.mult).then_inc(finished, 1)

            scale(0, 0)
            for k in range(K2):
                dve.wait_ge(whigh, k + 1)
                if k < KC:
                    nc.vector.scalar_tensor_tensor(out=wl[:, k, :], in0=wraw[k % PLE_AHEAD], scalar=gate_gain[:, k:k + 1],
                                                   in1=wh[:, k, :].bitcast(F32), op0=ALU.mult, op1=ALU.subtract)\
                        .then_inc(wready, 1)
                    if k == 1:
                        splits(0, 0)
                        scale(1, 1)
                else:
                    nc.vector.tensor_tensor(wl[:, k, :], wraw[k % PLE_AHEAD], wh[:, k, :].bitcast(F32), ALU.subtract)\
                        .then_inc(wready, 1)
            dve.wait_ge(gain_in, 16)
            walk_by_four(dve, step)

        @block.tensor
        def _(pe):
            def turns(t, s, i):
                pe.wait_ge(scaled, t + 1)
                pe.wait_ge(p_in[s], i * 16 + 16)
                if known(t) and t == NT:
                    pe.wait_ge(p_in[s], i * 16 + 32)
                if not known(t) or t >= 1:
                    pe.wait_ge(split, t * 3)
                for g in range(3):
                    for k in range(sizes[g]):
                        src = xn[s][:, (starts[g] + k) * P:(starts[g] + k + 1) * P] if g < 2 else \
                            pt[s][:, k * P:(k + 1) * P]
                        last = nc.tensor.transpose(turn_acc[g][:, k * P:(k + 1) * P], src, ident[:, :])
                    last.then_inc(turned, 1)

            def products(t, s, acc, chunks, h, done):
                for k in chunks:
                    if known(t) and t == 0 and h == 0:
                        pe.wait_ge(wready, k + 1)
                    for p, (a, w) in enumerate(((sh, wh), (sh, wl), (sl, wh))):
                        last = nc.tensor.matmul(acc[h][:, :], a[s][:, k, :], w[:, k, 512 * h:512 * h + 512],
                                                start=(k == chunks[0] and p == 0), stop=(k == chunks[-1] and p == 2))
                last.then_inc(done, 1)

            def step(t, s, i):
                pe.wait_ge(split, t * 3 + 3)
                for h in range(2):
                    if not known(t) or t >= 1:
                        pe.wait_ge(opened, t * 2)
                    products(t, s, gate_acc, range(KC), h, gates)
                    if h == 0 and (not known(t) or t < NT):
                        turns(t + 1, 1 - s, i + s)
                for h in range(2):
                    if not known(t) or t >= 1:
                        pe.wait_ge(gated, t * 2)
                    products(t, s, ple_acc, range(KC, K2), h, ples)
            turns(0, 0, 0)
            walk(pe, step)


def phase_mixers(nc, m, pt_scratch, v_scratch, vs_scratch, mix, state_out, ident, consts, ahead):
    ctx = ExitStack()
    with ctx:
        sb = lambda n, s, d=F32: ctx.enter_context(nc.sbuf_tensor(f"gla_{n}", s, d))
        sem = phase_semaphores(nc, ctx, "gla")
        bank = lambda n: ctx.enter_context(nc.psum_tensor(f"gla_{n}_acc", [P, 512], F32))
        two = lambda n, s: [sb(f"{n}{i}", s) for i in range(2)]
        qk = two("qk", [P, 4, P])
        glr = two("glr", [RANK, P])
        vs = two("vs", [P, HS * P])
        v = two("v", [P, H * DV])
        ru = two("ru", [P, 2 * H, P])
        z, soft, logd = sb("z", [P, 2 * P]), sb("soft", [P, 2 * P]), sb("logd", [P, 2 * P])
        cum, from_mid, to_end = sb("cum", [P, 2 * P]), sb("from_mid", [P, 2 * P]), sb("to_end", [P, 2 * P])
        e_cum = two("e_cum", [P, 2 * P])
        e_q, e_k, e_end = sb("e_q", [P, 2 * P]), sb("e_k", [P, 2 * P]), sb("e_end", [P, 2 * P])
        q_state, q_in = (two(n, [P, 2, 2, P]) for n in ("q_state", "q_in"))
        k_in, k_end = (two(n, [P, 2, P]) for n in ("k_in", "k_end"))
        stats = sb("stats", [P, HS, 6])
        mv = sb("mv", [P, HS, 2])
        v_var, v_rstd = sb("v_var", [P, HS]), sb("v_rstd", [P, HS])
        vn = two("vn", [P, HS * P])
        scores = sb("scores", [P, 2, 2, P])
        k_tok = sb("k_tok", [P, 2, P])
        state = two("state", [P, 2, DV])
        square = sb("square", [P, H * P])
        inv = sb("inv", [P, H * P])
        normed = sb("normed", [P, H * P])
        mixed_b = sb("mixed_b", [P, HS, P])
        out = two("out", [P, 2 * H, P])
        zt_acc, s_acc = bank("zt"), bank("s")
        kv_acc, o_acc = [bank("kv0"), bank("kv1")], [bank("o0"), bank("o1")]
        n_acc, m_acc = bank("n"), bank("m")

        a_in, b_in = [sem("a_in0"), sem("a_in1")], [sem("b_in0"), sem("b_in1")]
        logits = sem("logits")
        z_made = sem("z_made")
        decays = sem("decays")
        softs = sem("softs")
        factors = sem("factors")
        queries, keys = sem("queries"), sem("keys")
        stat, v_power = sem("stat"), sem("v_power")
        v_normed, v_gained = sem("v_normed"), sem("v_gained")
        scored, masked = sem("scored"), sem("masked")
        k_turned, k_copied = sem("k_turned"), sem("k_copied")
        kv_made = sem("kv_made")
        states = sem("states")
        outputs = sem("outputs")
        squared, averaged, inverse = sem("squared"), sem("averaged"), sem("inverse")
        spatials = sem("spatials")
        gla_outs = sem("gla_outs")
        sgu_outs = sem("sgu_outs")
        zeroed = sem("zeroed")
        stored = [sem("stored0"), sem("stored1")]
        state_stored = sem("state_stored")
        block = ctx.enter_context(nc.Block())
        pt_view = pt_scratch.rearrange("(k p) t -> p k t", p=P)
        mix_view = mix.rearrange("(k p) t -> p k t", p=P)

        def walk_prompt(eng, step):
            step(0, 0, 0)
            step(1, 1, 0)
            with eng.Fori(1, NT // 2 - 1) as i:
                step(i * 2, 0, i)
                step(i * 2 + 1, 1, i)
            step(NT - 2, 0, NT // 2 - 1)
            step(NT - 1, 1, NT // 2 - 1)

        def more(t):
            return not known(t) or t + 1 < NT

        def old(t):
            return not known(t) or t >= 2

        def later(t):
            return not known(t) or t >= 1

        @block.sync
        def _(sp):
            def load_first(t, s):
                here = ds(t * P, P)
                if old(t):
                    sp.wait_ge(queries, t * 4 - 4)
                    sp.wait_ge(keys, t * 2 - 2)
                    sp.wait_ge(v_normed, t * 4 - 4)
                sp.dma_start(qk[s][:, :, :], pt_view[:, 0:4, here]).then_inc(a_in[s], 16)
                sp.dma_start(glr[s][:, :], pt_scratch[12 * P:12 * P + RANK, here]).then_inc(a_in[s], 16)
                sp.dma_start(vs[s][:, :], vs_scratch[here, :]).then_inc(a_in[s], 16)

            def load_second(t, s):
                here = ds(t * P, P)
                if old(t):
                    sp.wait_ge(outputs, t * 2 - 2)
                    sp.wait_ge(sgu_outs, t * 2 - 2)
                    sp.wait_ge(gla_outs, t * 2 - 2)
                sp.dma_start(v[s][:, :], v_scratch[here, :]).then_inc(b_in[s], 16)
                sp.dma_start(ru[s][:, :, :], pt_view[:, 4:12, here]).then_inc(b_in[s], 16)

            def store(t, s):
                sp.wait_ge(sgu_outs, t * 2 + 2)
                sp.wait_ge(gla_outs, t * 2 + 2)
                sp.dma_start(mix_view[:, :, ds(t * P, P)], out[s][:, :, :]).then_inc(stored[s], 16)

            def step(t, s, i):
                if not known(t) or t + 2 < NT:
                    load_first(t + 2, s)
                if more(t):
                    load_second(t + 1, 1 - s)
                if later(t):
                    store(t - 1, 1 - s)
            load_first(0, 0)
            load_second(0, 0)
            load_first(1, 1)
            for dst, src, arrived in ahead:
                sp.dma_start(dst, src).then_inc(arrived, 16)
            walk_prompt(sp, step)
            store(NT - 1, 1)
            sp.wait_ge(states, 4 * NT)
            for f in range(2):
                sp.dma_start(state_out.rearrange("(q f) d e -> f d q e", f=2)[f], state[0][head_rows(f), :, :])\
                    .then_inc(state_stored, 16)
            sp.wait_ge(state_stored, 32)
            for s in range(2):
                sp.wait_ge(stored[s], 16 * (NT // 2))

        @block.tensor
        def _(pe):
            def gate_logits(t, s, i):
                pe.wait_ge(a_in[s], i * 48 + 48)
                for q in range(2):
                    last = nc.tensor.matmul(zt_acc[:, q * P:(q + 1) * P], m.gate_w[:, q * P:(q + 1) * P], glr[s][:, :],
                                            start=True, stop=True)
                return last

            def mean(t):
                pe.wait_ge(squared, t + 1)
                if later(t):
                    pe.wait_ge(inverse, t * 2 - 1)
                nc.tensor.matmul(n_acc[:, :], m.average[:, :], square[:, :], start=True, stop=True)\
                    .then_inc(averaged, 1)

            def step(t, s, i):
                pe.wait_ge(keys, t * 2 + 2)
                pe.wait_ge(z_made, t * 2 + 2)
                if later(t):
                    pe.wait_ge(k_copied, t)
                if more(t):
                    gate_logits(t + 1, 1 - s, i + s)
                for q in range(2):
                    last = nc.tensor.transpose(zt_acc[:, (2 + q) * P:(3 + q) * P], k_end[s][:, q, :], ident[:, :])
                last.then_inc(k_turned, 1)
                pe.wait_ge(queries, t * 4 + 4)
                if later(t):
                    pe.wait_ge(masked, t)
                for q in range(2):
                    last = nc.tensor.matmul(s_acc[:, q * 2 * P:(q + 1) * 2 * P], k_in[s][:, q, :],
                                            q_in[s][:, q].rearrange("p f t -> p (f t)"), start=True, stop=True)
                last.then_inc(scored, 1)
                if later(t):
                    mean(t - 1)
                pe.wait_ge(v_gained, t * 2 + 2)
                if later(t):
                    pe.wait_ge(sgu_outs, t * 2 - 1)
                for h in range(HS):
                    if h == HS // 2:
                        pe.wait_ge(b_in[s], i * 32 + 32)
                        pe.wait_ge(k_copied, t + 1)
                        if later(t):
                            pe.wait_ge(states, t * 4)
                    last = nc.tensor.matmul(m_acc[:, h * P:(h + 1) * P], vn[s][:, h * P:(h + 1) * P],
                                            m.spatial[:, h, :], start=True, stop=True)
                last.then_inc(spatials, 1)
                for c in range(NCH):
                    chunk = slice(c * C, c * C + C)
                    for q in range(2):
                        for f in range(2):
                            h = 2 * q + f
                            last = nc.tensor.matmul(kv_acc[c][head_rows(f), q * DV:(q + 1) * DV],
                                                    k_tok[chunk, q, f * DK:(f + 1) * DK],
                                                    v[s][chunk, h * DV:(h + 1) * DV], start=True, stop=True)
                    last.then_inc(kv_made, 1)
                pe.wait_ge(masked, t + 1)
                if old(t):
                    pe.wait_ge(gla_outs, t * 2 - 3)
                o = o_acc[s][:, :].rearrange("p (q f t) -> p q f t", q=2, f=2)
                for c in range(NCH):
                    if c > 0:
                        pe.wait_ge(states, t * 4 + 2)
                    cols = slice(c * C, c * C + C)
                    for q in range(2):
                        nc.tensor.matmul(o[:, q, :, cols], state[c][:, q, :], q_state[s][:, q, :, cols],
                                         start=True, stop=False)
                        for f in range(2):
                            h = 2 * q + f
                            last = nc.tensor.matmul(o[:, q, f, cols], v[s][:, h * DV:(h + 1) * DV],
                                                    scores[:, q, f, cols], start=False, stop=(f == 1))
                    last.then_inc(outputs, 1)
            pe.wait_ge(zeroed, 6)
            gate_logits(0, 0, 0).then_inc(logits, 1)
            walk_prompt(pe, step)
            mean(NT - 1)

        @block.scalar
        def _(act):
            def soft_logs(t, s):
                if known(t) and t == 0:
                    act.wait_ge(logits, 1)
                else:
                    act.wait_ge(k_turned, t)
                    act.wait_ge(decays, t * 4 - 3)
                for q in range(2):
                    nc.scalar.activation(z[:, q * P:(q + 1) * P], zt_acc[:, q * P:(q + 1) * P], ACT.Identity,
                                         bias=m.gate_b[:, q:q + 1]).then_inc(z_made, 1)
                act.wait_ge(z_made, t * 2 + 2)
                nc.scalar.activation(soft[:, :], z[:, :], ACT.Abs).then_inc(softs, 1)
                act.wait_ge(softs, t * 3 + 1)
                nc.scalar.activation(soft[:, :], soft[:, :], ACT.Exp, scale=-1.0).then_inc(softs, 1)
                act.wait_ge(softs, t * 3 + 2)
                nc.scalar.activation(soft[:, :], soft[:, :], ACT.Ln, bias=1.0).then_inc(softs, 1)

            def exps(t, s):
                act.wait_ge(decays, t * 4 + 4)
                if old(t):
                    act.wait_ge(states, t * 4 - 4)
                if later(t):
                    act.wait_ge(queries, t * 4)
                    act.wait_ge(keys, t * 2)
                for out_, in_, sign in ((e_k, from_mid, -1.0), (e_end, to_end, 1.0), (e_q, from_mid, 1.0),
                                        (e_cum[s], cum, 1.0)):
                    nc.scalar.activation(out_[:, :], in_[:, :], ACT.Exp, scale=sign / TAU).then_inc(factors, 1)

            def inverse_norm(t):
                act.wait_ge(averaged, t + 1)
                if later(t):
                    act.wait_ge(gla_outs, t * 2 - 1)
                nc.scalar.activation(inv[:, :], n_acc[:, :], ACT.Ln, bias=consts[:, 0:1]).then_inc(inverse, 1)
                act.wait_ge(inverse, t * 2 + 1)
                nc.scalar.activation(inv[:, :], inv[:, :], ACT.Exp, scale=-0.5).then_inc(inverse, 1)

            def step(t, s, i):
                if more(t):
                    soft_logs(t + 1, 1 - s)
                act.wait_ge(k_turned, t + 1)
                if later(t):
                    act.wait_ge(kv_made, t * 2)
                nc.scalar.activation(k_tok[:, :, :].rearrange("p q d -> p (q d)"), zt_acc[:, 2 * P:4 * P],
                                     ACT.Copy).then_inc(k_copied, 1)
                if later(t):
                    inverse_norm(t - 1)
                if more(t):
                    exps(t + 1, 1 - s)
                act.wait_ge(outputs, t * 2 + 2)
                if later(t):
                    act.wait_ge(averaged, t)
                nc.scalar.activation(square[:, :], o_acc[s][:, :], ACT.Square).then_inc(squared, 1)
            act.preload_act_table_set("natural_log_exp_and_others")
            soft_logs(0, 0)
            exps(0, 0)
            walk_prompt(act, step)
            inverse_norm(NT - 1)

        @block.gpsimd
        def _(pool):
            def make_keys(t, s):
                if old(t):
                    pool.wait_ge(outputs, t * 2 - 2)
                for i, (out_, e) in enumerate(((k_in[s], e_k), (k_end[s], e_end))):
                    pool.wait_ge(factors, t * 4 + (i + 1))
                    nc.gpsimd.tensor_tensor(out_[:, :, :], qk[s][:, 2:4, :],
                                            e[:, :].rearrange("p (q t) -> p q t", q=2), ALU.mult).then_inc(keys, 1)

            def v_tail(t, s):
                pool.wait_ge(v_normed, t * 4 + 4)
                nc.gpsimd.tensor_tensor(vn[s][:, :], vn[s][:, :], m.ln_gain[:, :], ALU.mult).then_inc(v_gained, 1)
                pool.wait_ge(v_gained, t * 2 + 1)
                nc.gpsimd.tensor_tensor(vn[s][:, :], vn[s][:, :], m.ln_bias[:, :], ALU.add).then_inc(v_gained, 1)

            def v_scale(t):
                pool.wait_ge(stat, t * 8 + 8)
                nc.gpsimd.tensor_tensor(v_var[:, :], mv[:, :, 1:2].rearrange("p h a -> p (h a)"),
                                        consts[:, 0:1].to_broadcast([P, HS]), ALU.add).then_inc(v_power, 1)
                pool.wait_ge(v_power, t * 2 + 1)
                nc.gpsimd.tensor_tensor(v_rstd[:, :], v_var[:, :], consts[:, 1:2].to_broadcast([P, HS]), ALU.pow)\
                    .then_inc(v_power, 1)

            def first(t, s):
                v_scale(t)
                make_keys(t, s)
                v_tail(t, s)

            def step(t, s, i):
                if more(t):
                    first(t + 1, 1 - s)
                if old(t):
                    pool.wait_ge(stored[s], i * 16)
                pool.wait_ge(b_in[s], i * 32 + 32)
                pool.wait_ge(sgu_outs, t * 2 + 1)
                nc.gpsimd.tensor_tensor(out[s][:, H:2 * H, :], mixed_b[:, :, :], ru[s][:, H:2 * H, :], ALU.mult)\
                    .then_inc(sgu_outs, 1)
            first(0, 0)
            walk_prompt(pool, step)

        @block.vector
        def _(dve):
            def chunks(x):
                return x[:, :].rearrange("p (a c) -> p a c", c=C)

            def log_decays(t, s):
                dve.wait_ge(stat, t * 8 + 4)
                dve.wait_ge(softs, t * 3 + 3)
                nc.vector.scalar_tensor_tensor(out=logd[:, :], in0=z[:, :], scalar=0.0, in1=soft[:, :],
                                               op0=ALU.min, op1=ALU.subtract).then_inc(decays, 1)
                for h in range(HS):
                    nc.vector.bn_aggr(mv[:, h, :], stats[:, h, :]).then_inc(stat, 1)
                dve.wait_ge(decays, t * 4 + 1)
                nc.vector.tensor_tensor_scan(out=cum[:, :], data0=m.reset[:, :], data1=logd[:, :], initial=0.0,
                                             op0=ALU.mult, op1=ALU.add).then_inc(decays, 1)
                dve.wait_ge(decays, t * 4 + 2)
                c = chunks(cum)
                nc.vector.tensor_tensor(chunks(from_mid), c, c[:, :, C // 2 - 1:C // 2].to_broadcast([P, 2 * NCH, C]),
                                        ALU.subtract).then_inc(decays, 1)
                nc.vector.tensor_tensor(chunks(to_end), c[:, :, C - 1:C].to_broadcast([P, 2 * NCH, C]), c,
                                        ALU.subtract).then_inc(decays, 1)

            def make_queries(t, s):
                if old(t):
                    dve.wait_ge(outputs, t * 2 - 2)
                for i, (out_, e) in enumerate(((q_in[s], e_q), (q_state[s], e_cum[s]))):
                    dve.wait_ge(factors, t * 4 + (i + 3))
                    for f in range(2):
                        rows = head_rows(f)
                        nc.vector.scalar_tensor_tensor(out=out_[rows, :, f, :], in0=qk[s][rows, 0:2, :],
                                                       scalar=DK ** -0.5,
                                                       in1=e[rows, :].rearrange("p (q t) -> p q t", q=2),
                                                       op0=ALU.mult, op1=ALU.mult).then_inc(queries, 1)

            def v_stats(t, s, i):
                dve.wait_ge(a_in[s], i * 48 + 48)
                if later(t):
                    dve.wait_ge(v_normed, t * 4)
                for h in range(HS):
                    nc.vector.bn_stats(stats[:, h, :], vs[s][:, h * P:(h + 1) * P]).then_inc(stat, 1)

            def v_norm(t, s):
                dve.wait_ge(v_power, t * 2 + 2)
                if old(t):
                    dve.wait_ge(spatials, t - 1)
                for h in range(HS):
                    nc.vector.tensor_scalar(vn[s][:, h * P:(h + 1) * P], vs[s][:, h * P:(h + 1) * P],
                                            mv[:, h, 0:1], v_rstd[:, h:h + 1], ALU.subtract, ALU.mult)\
                        .then_inc(v_normed, 1)

            def mask(t):
                nc.vector.copy_predicated(scores[:, :, :, :].rearrange("p q f i -> p (q f) i"),
                                          m.causal[:, :].bitcast(I32).unsqueeze(1).to_broadcast([P, H, P]),
                                          s_acc[:, :].rearrange("p (a i) -> p a i", i=P))\
                    .then_inc(masked, 1)

            def advance(t, s, c):
                dve.wait_ge(kv_made, t * 2 + 2)
                if c == 1:
                    dve.wait_ge(outputs, t * 2 + 1)
                elif later(t):
                    dve.wait_ge(outputs, t * 2)
                    dve.wait_ge(states, t * 4)
                if c == 1:
                    dve.wait_ge(states, t * 4 + 2)
                decay = e_cum[s][:, :].rearrange("p (q t) -> p q t", q=2)[:, :, (c + 1) * C - 1:(c + 1) * C]
                nc.vector.tensor_tensor(state[1 - c][:, :, :], state[c][:, :, :], decay.to_broadcast([P, 2, DV]),
                                        ALU.mult).then_inc(states, 1)
                dve.wait_ge(states, t * 4 + (2 * c + 1))
                nc.vector.tensor_tensor(state[1 - c][:, :, :], state[1 - c][:, :, :],
                                        kv_acc[c][:, 0:2 * DV].rearrange("p (q e) -> p q e", q=2),
                                        ALU.add).then_inc(states, 1)

            def finish_gla(t, s):
                dve.wait_ge(inverse, t * 2 + 2)
                nc.vector.tensor_tensor(normed[:, :], o_acc[s][:, :], inv[:, :], ALU.mult).then_inc(gla_outs, 1)
                dve.wait_ge(gla_outs, t * 2 + 1)
                flat = lambda x: x[s][:, 0:H, :].rearrange("p h t -> p (h t)")
                nc.vector.scalar_tensor_tensor(out=flat(out), in0=normed[:, :], scalar=m.gain_out[:, 0:1],
                                               in1=flat(ru), op0=ALU.mult, op1=ALU.mult).then_inc(gla_outs, 1)

            def finish_sgu(t, s, i):
                if old(t):
                    dve.wait_ge(stored[s], i * 16)
                dve.wait_ge(spatials, t + 1)
                if later(t):
                    dve.wait_ge(sgu_outs, t * 2)
                nc.vector.tensor_tensor(mixed_b[:, :, :], m_acc[:, :].rearrange("p (h t) -> p h t", h=HS),
                                        m.spatial_b[:, :, :], ALU.add).then_inc(sgu_outs, 1)

            def step(t, s, i):
                dve.wait_ge(scored, t + 1)
                if later(t):
                    dve.wait_ge(outputs, t * 2)
                if more(t):
                    v_stats(t + 1, 1 - s, i + s)
                mask(t)
                if more(t):
                    log_decays(t + 1, 1 - s)
                if later(t):
                    finish_gla(t - 1, 1 - s)
                if more(t):
                    make_queries(t + 1, 1 - s)
                advance(t, s, 0)
                finish_sgu(t, s, i)
                advance(t, s, 1)
                if more(t):
                    v_norm(t + 1, 1 - s)

            nc.vector.memset(scores[:, :, :, :], 0.0).then_inc(zeroed, 1)
            nc.vector.memset(state[0][:, :, :], 0.0).then_inc(zeroed, 1)
            for x in q_in + q_state:
                nc.vector.memset(x[:, :, :, :], 0.0).then_inc(zeroed, 1)
            dve.wait_ge(zeroed, 6)
            v_stats(0, 0, 0)
            log_decays(0, 0)
            v_norm(0, 0)
            make_queries(0, 0)
            walk_prompt(dve, step)
            finish_gla(NT - 1, 1)


def build(nc, a, outs):
    dram = lambda n, s: nc.dram_tensor(n, s, F32).ap()
    pt = dram("proj_features", [13 * P, T])
    v_s = dram("proj_v", [T, H * DV])
    vs_s = dram("proj_vs", [T, HS * P])
    mix = dram("mix", [D, T])
    x1, x2 = dram("x1", [T, D]), dram("x2", [T, D])
    hidden = dram("hidden", [FF, T])
    down0 = dram("down0", [T, 512])
    x_p = a["x_prompt"][0]
    x_s = a["x_sample"].rearrange("b t d -> (b t) d")

    def x_tiles(t):
        return x_s if isinstance(t, int) and t == NT else x_p[ds(t * P, P), :]

    ctx = ExitStack()
    with ctx:
        ident = ctx.enter_context(nc.sbuf_tensor("ident", [P, P], F32))
        consts = ctx.enter_context(nc.sbuf_tensor("consts", [P, 2], F32))
        gains = ctx.enter_context(nc.sbuf_tensor("gains", [P, 3, KC], F32))
        made = ctx.enter_context(nc.semaphore("made"))
        gains_in = ctx.enter_context(nc.semaphore("gains_in"))
        with nc.Block() as block:
            @block.gpsimd
            def _(pool):
                identity(nc, ident, made)
                nc.gpsimd.memset(consts[:, 0:1], EPS)
                nc.gpsimd.memset(consts[:, 1:2], -0.5)

            @block.sync
            def _(sp):
                with nc.allow_non_contiguous_dma(reason="a gain's 1024 values, features on partitions"):
                    for i, g in enumerate(("g_mix_pre", "g_ffn_pre", "g_ple_in")):
                        sp.dma_start(gains[:, i, :], a[g][0].rearrange("(k p) -> p k", p=P)).then_inc(gains_in, 16)
                sp.wait_ge(gains_in, 48)

        with nc.sbuf_tensor("xh", [P, KC, T], F32R) as xh, nc.sbuf_tensor("xl", [P, KC, T], F32R) as xl:
            phase_in(nc, x_tiles, xh, xl, a["w_in"][0], gains[:, 0, :], pt, v_s, vs_s, ident, consts)

        x1_of = lambda t: x1[token_rows(t), :]
        ffn = ctx.enter_context(nc.sbuf_tensor("ffn_features", [P, 2 * FC, 20], F32))
        with ExitStack() as held:
            w_out = held.enter_context(nc.sbuf_tensor("out_wraw", [P, KC, D], F32))
            w_out_in = held.enter_context(nc.semaphore("out_wraw_in"))
            w_out_loads = [(w_out[:, k, :], a["w_out"][0][k * P:(k + 1) * P, :], w_out_in) for k in range(KC)]
            sample = SampleTiles(nc, held)
            m = MixerConsts(nc, held)
            phase_mixer_consts(nc, a, m, ident, sample, a["state_gla"][0], pt, v_s, vs_s,
                               [a["state_ffn_conv"][0].rearrange("b c n -> (b c) n"), a["w_conv"][0], a["b_conv"]],
                               ffn)
            phase_mixers(nc, m, pt, v_s, vs_s, mix, outs[2][0, 0], ident, consts, w_out_loads)
            phase_out(nc, mix, a["g_mix_post"][0], x_tiles, x1_of, w_out, w_out_in, m, sample, outs[3][0],
                      outs[6][0].rearrange("b t n -> (b t) n"), ident, consts)

        def p_tiles(t):
            if known(t) and t == NT:
                return ((slice(0, P - TS), a["p_prompt"][0, 0][TP - P + TS:TP, :]),
                        (slice(P - TS, P), a["p_sample"][0].rearrange("b t d -> (b t) d")))
            return ((slice(0, P), a["p_prompt"][0, 0][token_rows(t), :]),)

        def y_tiles(t):
            if known(t) and t == NT:
                return outs[1].rearrange("b t d -> (b t) d")
            return outs[0][0][token_rows(t), :]

        with ExitStack() as held:
            tail = held.enter_context(nc.sbuf_tensor("tail", [P, 2 * FC, 2 + 2 * SEQS], F32))
            ahead = held.enter_context(nc.sbuf_tensor("down_ahead", [P, DOWN_AHEAD * 512], F32))
            wraw = [ahead[:, i * 512:(i + 1) * 512] for i in range(DOWN_AHEAD)]
            wraw_in = [held.enter_context(nc.semaphore(f"down_ahead_in{i}")) for i in range(DOWN_AHEAD)]
            ple_wraw = [ahead[:, i * D:(i + 1) * D] for i in range(PLE_AHEAD)]
            ple_wraw_in = [held.enter_context(nc.semaphore(f"ple_ahead_in{i}")) for i in range(PLE_AHEAD)]
            first_ple_chunks = [(ple_wraw[i], a["w_ple_gate"][0][i * P:(i + 1) * P, :], ple_wraw_in[i])
                                for i in range(PLE_AHEAD)]
            w_down = a["w_down"][0]
            first_chunks = [(wraw[i], w_down[i * P:(i + 1) * P, 0:512], wraw_in[i]) for i in range(DOWN_AHEAD)]
            with nc.sbuf_tensor("xh2", [P, KC, T], F32R) as xh, nc.sbuf_tensor("xl2", [P, KC, T], F32R) as xl:
                phase_up(nc, x1_of, xh, xl, a["w_up"][0], gains[:, 1, :], ffn[:, :, 16:19], ffn[:, :, 19],
                         ffn[:, :, 0:16], tail, hidden, first_chunks, ahead[:, :], ident, consts)
            phase_down(nc, hidden, w_down, tail, outs[4][0, 0], outs[5][0].rearrange("b c n -> (b c) n"), down0,
                       a["g_ffn_post"][0], x1_of, lambda t: x2[token_rows(t), :], wraw, wraw_in,
                       ffn[:, :, :].rearrange("p f r -> p (f r)"), first_ple_chunks, ident, consts)
            phase_ple(nc, x2, p_tiles, a["w_ple_gate"][0], gains[:, 2, :], a["w_ple"][0], a["g_ple_post"][0], y_tiles,
                      ple_wraw, ple_wraw_in, ident, consts)


_OUTS = [(1, TP, D), (SEQS, SL, D), (1, 1, H, DK, DV), (1, SEQS, H, DK, DV), (1, 1, 2, 2 * FF),
         (1, SEQS, 2, 2 * FF), (1, SEQS, SL, HS * P)]


def kernel(**inputs):
    import numpy as np
    import concourse.bacc as bacc
    from concourse.bass_utils import run_bass_kernel_spmd

    nc = bacc.Bacc("TRN2", target_bir_lowering=False, num_devices=1)
    arrays, a = {}, {}
    for name, value in inputs.items():
        value = np.ascontiguousarray(value)
        arrays[f"in_{name}"] = value
        a[name] = nc.dram_tensor(f"in_{name}", value.shape, F32, kind="ExternalInput").ap()
    outs = [nc.dram_tensor(f"out_{i}", shape, F32, kind="ExternalOutput").ap() for i, shape in enumerate(_OUTS)]
    build(nc, a, outs)
    got = run_bass_kernel_spmd(nc, [arrays], core_ids=[0])
    return tuple(got.results[0][f"out_{i}"] for i in range(len(outs)))
```
